# Optimizing a Trainium2 kernel written in Bass

```python
import math
import jax
import jax.numpy as jnp
from jax import lax
import numpy as np
import jax, jax.numpy as jnp

D_MODEL = 1024
BATCH = 1
SEQ = 256
DEPTH = 2

HEAD_DIM = 64
ROPE_DIM = HEAD_DIM // 4
ROPE_THETA = 500000.0
NORM_EPS = 1e-6
NEG_INF = -1e30
FORCE_SCORE = 1e6

MOBA_HEADS = D_MODEL // (2 * HEAD_DIM)
MOBA_BLOCK = 256
MOBA_TOPK = 3
MOBA_QCHUNK = 32
DIFF_HEADS = D_MODEL // (4 * HEAD_DIM)
DIFF_VDIM = 2 * HEAD_DIM
DIFF_QCHUNK = 128
MOBA_W = MOBA_HEADS * HEAD_DIM
DIFF_QK_W = DIFF_HEADS * 2 * HEAD_DIM
DIFF_V_W = DIFF_HEADS * DIFF_VDIM
EVEN_IN = 3 * MOBA_W + 2 * DIFF_QK_W + DIFF_V_W
EVEN_MIX = MOBA_W + DIFF_V_W

NSA_HEADS = D_MODEL // HEAD_DIM
NSA_GROUP = 4
NSA_KV_HEADS = NSA_HEADS // NSA_GROUP
CMP_BLOCK = 32
CMP_STRIDE = 16
CMP_HIDDEN = 256
SLC_BLOCK = 64
SLC_TOPN = 16
WINDOW = 512
NSA_QCHUNK = 16
NSA_Q_W = NSA_HEADS * HEAD_DIM
NSA_KV_W = NSA_KV_HEADS * HEAD_DIM
ODD_IN = NSA_Q_W + 6 * NSA_KV_W + 3 * NSA_HEADS
ODD_MIX = NSA_Q_W

MOE_GROUPS = 4
MOE_PER_GROUP = 4
MOE_EXPERTS = MOE_GROUPS * MOE_PER_GROUP
MOE_TOPK = 2
MOE_FF = 256

N_EVEN = (DEPTH + 1) // 2
N_ODD = DEPTH // 2


def rms_norm(x, g):
    xf = x.astype(jnp.float32)
    y = xf * lax.rsqrt(jnp.mean(xf * xf, axis=-1, keepdims=True) + NORM_EPS)
    return (y * g.astype(jnp.float32)).astype(x.dtype)

def rope_tables(seq):
    pos = jnp.arange(seq, dtype=jnp.float32)
    inv = ROPE_THETA ** (-jnp.arange(0, ROPE_DIM, 2, dtype=jnp.float32) / ROPE_DIM)
    ang = pos[:, None] * inv[None, :]
    return jnp.cos(ang), jnp.sin(ang)

def apply_rope(t, cos, sin):
    half = ROPE_DIM // 2
    c = cos.astype(t.dtype)
    s = sin.astype(t.dtype)
    t1 = t[..., :half]
    t2 = t[..., half:ROPE_DIM]
    return jnp.concatenate([t1 * c - t2 * s, t2 * c + t1 * s, t[..., ROPE_DIM:]], axis=-1)

def split_heads(t, n):
    b, s, _ = t.shape
    return t.reshape(b, s, n, -1).transpose(0, 2, 1, 3)

def merge_heads(t):
    b, h, s, d = t.shape
    return t.transpose(0, 2, 1, 3).reshape(b, s, h * d)

def gather_blocks(blocks, idx):
    return jax.vmap(jax.vmap(lambda bl, ix: bl[ix]))(blocks, idx)

def moba_attention(q, k, v):
    b, h, s, d = q.shape
    nb = -(-s // MOBA_BLOCK)
    pad = nb * MOBA_BLOCK - s
    kp = jnp.pad(k, ((0, 0), (0, 0), (0, pad), (0, 0)))
    vp = jnp.pad(v, ((0, 0), (0, 0), (0, pad), (0, 0)))
    kb = kp.reshape(b, h, nb, MOBA_BLOCK, d)
    vb = vp.reshape(b, h, nb, MOBA_BLOCK, d)
    kmean = jnp.mean(kb.astype(jnp.float32), axis=3)
    ksel = max(1, min(MOBA_TOPK, nb - 1))
    scale = d ** -0.5
    nq = s // MOBA_QCHUNK
    qc = jnp.moveaxis(q.reshape(b, h, nq, MOBA_QCHUNK, d), 2, 0)

    def chunk(args):
        qi, ci = args
        q0 = ci * MOBA_QCHUNK
        qpos = q0 + jnp.arange(MOBA_QCHUNK)
        own = q0 // MOBA_BLOCK
        gs = jnp.einsum('bhqd,bhnd->bhqn', qi.astype(jnp.float32), kmean)
        gs = jnp.where(jnp.arange(nb) < own, gs, NEG_INF)
        _, idx = lax.top_k(gs, ksel)
        valid = idx < own
        k_sel = gather_blocks(kb, idx)
        v_sel = gather_blocks(vb, idx)
        s_sel = jnp.einsum('bhqd,bhqnld->bhqnl', qi, k_sel).astype(jnp.float32) * scale
        s_sel = jnp.where(valid[..., None], s_sel, NEG_INF).reshape(b, h, MOBA_QCHUNK, ksel * MOBA_BLOCK)
        k_own = lax.dynamic_slice_in_dim(kp, own * MOBA_BLOCK, MOBA_BLOCK, axis=2)
        v_own = lax.dynamic_slice_in_dim(vp, own * MOBA_BLOCK, MOBA_BLOCK, axis=2)
        kpos = own * MOBA_BLOCK + jnp.arange(MOBA_BLOCK)
        s_own = jnp.einsum('bhqd,bhld->bhql', qi, k_own).astype(jnp.float32) * scale
        s_own = jnp.where(kpos[None, :] <= qpos[:, None], s_own, NEG_INF)
        p = jax.nn.softmax(jnp.concatenate([s_sel, s_own], axis=-1), axis=-1).astype(v.dtype)
        p_sel = p[..., :ksel * MOBA_BLOCK].reshape(b, h, MOBA_QCHUNK, ksel, MOBA_BLOCK)
        p_own = p[..., ksel * MOBA_BLOCK:]
        return (jnp.einsum('bhqnl,bhqnld->bhqd', p_sel, v_sel)
                + jnp.einsum('bhql,bhld->bhqd', p_own, v_own))

    o = lax.map(chunk, (qc, jnp.arange(nq)))
    return jnp.moveaxis(o, 0, 2).reshape(b, h, s, d)

def diff_attention(q, k, v, lam):
    b, h, _, s, d = q.shape
    nq = s // DIFF_QCHUNK
    scale = d ** -0.5
    kpos = jnp.arange(s)
    qc = jnp.moveaxis(q.reshape(b, h, 2, nq, DIFF_QCHUNK, d), 3, 0)

    def chunk(args):
        qi, ci = args
        qpos = ci * DIFF_QCHUNK + jnp.arange(DIFF_QCHUNK)
        sc = jnp.einsum('bhmqd,bhmkd->bhmqk', qi, k).astype(jnp.float32) * scale
        sc = jnp.where(kpos[None, :] <= qpos[:, None], sc, NEG_INF)
        p = jax.nn.softmax(sc, axis=-1)
        w = p[:, :, 0] - lam * p[:, :, 1]
        return jnp.einsum('bhqk,bhke->bhqe', w.astype(v.dtype), v)

    o = lax.map(chunk, (qc, jnp.arange(nq)))
    return jnp.moveaxis(o, 0, 2).reshape(b, h, s, -1)

def compress_blocks(t, pos_emb, w1, b1, w2, b2):
    b, g, s, d = t.shape
    nc = (s - CMP_BLOCK) // CMP_STRIDE + 1
    idx = jnp.arange(nc)[:, None] * CMP_STRIDE + jnp.arange(CMP_BLOCK)[None, :]
    blocks = t[:, :, idx, :] + pos_emb.astype(t.dtype)
    hid = jax.nn.gelu(jnp.einsum('bgnld,ldf->bgnf', blocks, w1.reshape(CMP_BLOCK, d, -1)) + b1)
    return jnp.einsum('bgnf,fe->bgne', hid, w2) + b2

def nsa_attention(q, kc, vc, ks, vs, kw, vw, gates):
    b, hq, s, d = q.shape
    g = NSA_KV_HEADS
    r = NSA_GROUP
    nc = kc.shape[2]
    ns = s // SLC_BLOCK
    nsel = min(SLC_TOPN, ns)
    scale = d ** -0.5
    cmp_start = jnp.arange(nc) * CMP_STRIDE
    cmp_end = cmp_start + CMP_BLOCK - 1
    slc_start = jnp.arange(ns) * SLC_BLOCK
    overlap = ((cmp_start[:, None] <= slc_start[None, :] + SLC_BLOCK - 1)
               & (cmp_end[:, None] >= slc_start[None, :])).astype(jnp.float32)
    ksb = ks.reshape(b, g, ns, SLC_BLOCK, d)
    vsb = vs.reshape(b, g, ns, SLC_BLOCK, d)
    kwp = jnp.pad(kw, ((0, 0), (0, 0), (WINDOW, 0), (0, 0)))
    vwp = jnp.pad(vw, ((0, 0), (0, 0), (WINDOW, 0), (0, 0)))
    nq = s // NSA_QCHUNK
    qc = jnp.moveaxis(q.reshape(b, hq, nq, NSA_QCHUNK, d), 2, 0)
    gc = jnp.moveaxis(gates.reshape(b, hq, nq, NSA_QCHUNK, 3), 2, 0)
    blk = jnp.arange(ns)

    def chunk(args):
        qi, gi, ci = args
        q0 = ci * NSA_QCHUNK
        qpos = q0 + jnp.arange(NSA_QCHUNK)
        qg = qi.reshape(b, g, r, NSA_QCHUNK, d)
        s_c = jnp.einsum('bgrqd,bgnd->bgrqn', qg, kc).astype(jnp.float32) * scale
        s_c = jnp.where(cmp_end[None, :] <= qpos[:, None], s_c, NEG_INF)
        p_c = jax.nn.softmax(s_c, axis=-1)
        p_c = jnp.where((qpos >= CMP_BLOCK - 1)[:, None], p_c, 0.0)
        o_c = jnp.einsum('bgrqn,bgnd->bgrqd', p_c.astype(vc.dtype), vc)
        imp = jnp.einsum('bgrqn,nj->bgqj', p_c, overlap)
        own = qpos // SLC_BLOCK
        started = slc_start[None, :] <= qpos[:, None]
        forced = (blk[None, :] == 0) | (blk[None, :] == own[:, None]) | (blk[None, :] == own[:, None] - 1)
        imp = jnp.where(started, jnp.where(forced, FORCE_SCORE, imp), NEG_INF)
        _, sidx = lax.top_k(imp, nsel)
        k_sel = gather_blocks(ksb, sidx)
        v_sel = gather_blocks(vsb, sidx)
        s_s = jnp.einsum('bgrqd,bgqnld->bgrqnl', qg, k_sel).astype(jnp.float32) * scale
        tok = sidx[..., None] * SLC_BLOCK + jnp.arange(SLC_BLOCK)
        s_s = jnp.where((tok <= qpos[:, None, None])[:, :, None], s_s, NEG_INF)
        p_s = jax.nn.softmax(s_s.reshape(b, g, r, NSA_QCHUNK, -1), axis=-1).reshape(s_s.shape)
        o_s = jnp.einsum('bgrqnl,bgqnld->bgrqd', p_s.astype(v_sel.dtype), v_sel)
        k_w = lax.dynamic_slice_in_dim(kwp, q0, WINDOW + NSA_QCHUNK, axis=2)
        v_w = lax.dynamic_slice_in_dim(vwp, q0, WINDOW + NSA_QCHUNK, axis=2)
        kpos = q0 - WINDOW + jnp.arange(WINDOW + NSA_QCHUNK)
        band = ((kpos[None, :] <= qpos[:, None]) & (kpos[None, :] > qpos[:, None] - WINDOW)
                & (kpos[None, :] >= 0))
        s_w = jnp.einsum('bgrqd,bgkd->bgrqk', qg, k_w).astype(jnp.float32) * scale
        p_w = jax.nn.softmax(jnp.where(band, s_w, NEG_INF), axis=-1)
        o_w = jnp.einsum('bgrqk,bgkd->bgrqd', p_w.astype(v_w.dtype), v_w)
        gt = gi.reshape(b, g, r, NSA_QCHUNK, 3).astype(o_c.dtype)
        o = gt[..., 0:1] * o_c + gt[..., 1:2] * o_s + gt[..., 2:3] * o_w
        return o.reshape(b, hq, NSA_QCHUNK, d)

    o = lax.map(chunk, (qc, gc, jnp.arange(nq)))
    return jnp.moveaxis(o, 0, 2).reshape(b, hq, s, d)

def even_mixer(h, w_in, w_out, lam_p, subln_g, lambda_init, cos, sin):
    b, s, _ = h.shape
    p = h @ w_in
    c1 = MOBA_W
    c2 = 2 * MOBA_W
    c3 = 3 * MOBA_W
    c4 = c3 + DIFF_QK_W
    c5 = c4 + DIFF_QK_W
    qa, ka, va, qb, kb, vb = jnp.split(p, [c1, c2, c3, c4, c5], axis=-1)
    qa = apply_rope(split_heads(qa, MOBA_HEADS), cos, sin)
    ka = apply_rope(split_heads(ka, MOBA_HEADS), cos, sin)
    oa = moba_attention(qa, ka, split_heads(va, MOBA_HEADS))
    qb = apply_rope(qb.reshape(b, s, DIFF_HEADS, 2, HEAD_DIM).transpose(0, 2, 3, 1, 4), cos, sin)
    kb = apply_rope(kb.reshape(b, s, DIFF_HEADS, 2, HEAD_DIM).transpose(0, 2, 3, 1, 4), cos, sin)
    lp = lam_p.astype(jnp.float32)
    lam = jnp.exp(jnp.sum(lp[0] * lp[1])) - jnp.exp(jnp.sum(lp[2] * lp[3])) + lambda_init
    ob = diff_attention(qb, kb, split_heads(vb, DIFF_HEADS), lam)
    ob = rms_norm(ob, subln_g) * (1.0 - lambda_init)
    o = jnp.concatenate([merge_heads(oa), merge_heads(ob)], axis=-1)
    return o @ w_out

def odd_mixer(h, w_in, w_out, cmp_pos, cmp_w1, cmp_b1, cmp_w2, cmp_b2, cos, sin):
    b, s, _ = h.shape
    p = h @ w_in
    cuts = [NSA_Q_W + i * NSA_KV_W for i in range(7)]
    q, kc, vc, ks, vs, kw, vw, gl = jnp.split(p, cuts, axis=-1)
    q = apply_rope(split_heads(q, NSA_HEADS), cos, sin)
    kc = apply_rope(split_heads(kc, NSA_KV_HEADS), cos, sin)
    ks = apply_rope(split_heads(ks, NSA_KV_HEADS), cos, sin)
    kw = apply_rope(split_heads(kw, NSA_KV_HEADS), cos, sin)
    vc = split_heads(vc, NSA_KV_HEADS)
    vs = split_heads(vs, NSA_KV_HEADS)
    vw = split_heads(vw, NSA_KV_HEADS)
    gates = jax.nn.sigmoid(gl.astype(jnp.float32)).reshape(b, s, NSA_HEADS, 3).transpose(0, 2, 1, 3)
    k_cmp = compress_blocks(kc, cmp_pos[0], cmp_w1[0], cmp_b1[0], cmp_w2[0], cmp_b2[0])
    v_cmp = compress_blocks(vc, cmp_pos[1], cmp_w1[1], cmp_b1[1], cmp_w2[1], cmp_b2[1])
    o = nsa_attention(q, k_cmp, v_cmp, ks, vs, kw, vw, gates)
    return merge_heads(o) @ w_out

def hier_moe(h, wg, bg, we, be, w_gate, w_up, w_down):
    b, s, d = h.shape
    t = h.reshape(-1, d)
    n = t.shape[0]
    gl = (t @ wg + bg).astype(jnp.float32)
    gp = jax.nn.softmax(gl, axis=-1)
    _, gsel = lax.top_k(gl, 1)
    g_oh = jax.nn.one_hot(gsel[:, 0], MOE_GROUPS, dtype=jnp.float32)
    gw = jnp.sum(gp * g_oh, axis=-1, keepdims=True)
    el = (t @ we + be).astype(jnp.float32).reshape(n, MOE_GROUPS, MOE_PER_GROUP)
    el_g = jnp.sum(el * g_oh[:, :, None], axis=1)
    tv, ti = lax.top_k(el_g, MOE_TOPK)
    tw = jax.nn.softmax(tv, axis=-1)
    w_grp = jnp.sum(jax.nn.one_hot(ti, MOE_PER_GROUP, dtype=jnp.float32) * tw[..., None], axis=1)
    comb = ((g_oh * gw)[:, :, None] * w_grp[:, None, :]).reshape(n, MOE_EXPERTS)
    a = jax.nn.silu(jnp.einsum('td,edf->tef', t, w_gate)) * jnp.einsum('td,edf->tef', t, w_up)
    y = jnp.einsum('tef,efd->td', a * comb[:, :, None].astype(a.dtype), w_down)
    return y.reshape(b, s, d)

def first_inputs(seed: int = 0) -> dict:
    key = jax.random.key(seed)
    ks = jax.random.split(key, 28)
    D = D_MODEL

    def nrm(k, shape, std):
        return jax.random.normal(k, shape, jnp.float32) * std

    return {
        'x': nrm(ks[0], (BATCH, SEQ, D), 1.0),
        'c': nrm(ks[1], (BATCH, D), 1.0),
        'norm1_g': 1.0 + nrm(ks[2], (DEPTH, D), 0.02),
        'norm2_g': 1.0 + nrm(ks[3], (DEPTH, D), 0.02),
        'final_g': 1.0 + nrm(ks[4], (D,), 0.02),
        'ada_w': nrm(ks[5], (DEPTH, D, 6 * D), 0.5 * D ** -0.5),
        'ada_b': nrm(ks[6], (DEPTH, 6 * D), 0.02),
        'ev_w_in': nrm(ks[7], (N_EVEN, D, EVEN_IN), D ** -0.5),
        'ev_w_out': nrm(ks[8], (N_EVEN, EVEN_MIX, D), EVEN_MIX ** -0.5),
        'ev_lambda': nrm(ks[9], (N_EVEN, 4, HEAD_DIM), 0.1),
        'ev_subln_g': 1.0 + nrm(ks[10], (N_EVEN, DIFF_VDIM), 0.02),
        'od_w_in': nrm(ks[11], (N_ODD, D, ODD_IN), D ** -0.5),
        'od_w_out': nrm(ks[12], (N_ODD, ODD_MIX, D), ODD_MIX ** -0.5),
        'od_cmp_pos': nrm(ks[13], (N_ODD, 2, CMP_BLOCK, HEAD_DIM), 0.1),
        'od_cmp_w1': nrm(ks[14], (N_ODD, 2, CMP_BLOCK * HEAD_DIM, CMP_HIDDEN), (CMP_BLOCK * HEAD_DIM) ** -0.5),
        'od_cmp_b1': nrm(ks[15], (N_ODD, 2, CMP_HIDDEN), 0.01),
        'od_cmp_w2': nrm(ks[16], (N_ODD, 2, CMP_HIDDEN, HEAD_DIM), CMP_HIDDEN ** -0.5),
        'od_cmp_b2': nrm(ks[17], (N_ODD, 2, HEAD_DIM), 0.01),
        'moe_wg': nrm(ks[18], (DEPTH, D, MOE_GROUPS), D ** -0.5),
        'moe_bg': nrm(ks[19], (DEPTH, MOE_GROUPS), 0.01),
        'moe_we': nrm(ks[20], (DEPTH, D, MOE_EXPERTS), D ** -0.5),
        'moe_be': nrm(ks[21], (DEPTH, MOE_EXPERTS), 0.01),
        'moe_w_gate': nrm(ks[22], (DEPTH, MOE_EXPERTS, D, MOE_FF), D ** -0.5),
        'moe_w_up': nrm(ks[23], (DEPTH, MOE_EXPERTS, D, MOE_FF), D ** -0.5),
        'moe_w_down': nrm(ks[24], (DEPTH, MOE_EXPERTS, MOE_FF, D), MOE_FF ** -0.5),
    }

def first_block(x, c, norm1_g, norm2_g, final_g, ada_w, ada_b, ev_w_in, ev_w_out, ev_lambda,
              ev_subln_g, od_w_in, od_w_out, od_cmp_pos, od_cmp_w1, od_cmp_b1, od_cmp_w2,
              od_cmp_b2, moe_wg, moe_bg, moe_we, moe_be, moe_w_gate, moe_w_up, moe_w_down):
    s = x.shape[1]
    cos, sin = rope_tables(s)
    cs = jax.nn.silu(c)
    for l in range(DEPTH):
        mod = (cs @ ada_w[l] + ada_b[l])[:, None, :]
        sh1, sc1, g1, sh2, sc2, g2 = jnp.split(mod, 6, axis=-1)
        h = rms_norm(x, norm1_g[l]) * (1.0 + sc1) + sh1
        if l % 2 == 0:
            i = l // 2
            lambda_init = 0.8 - 0.6 * math.exp(-0.3 * l)
            y = even_mixer(h, ev_w_in[i], ev_w_out[i], ev_lambda[i], ev_subln_g[i], lambda_init, cos, sin)
        else:
            i = l // 2
            y = odd_mixer(h, od_w_in[i], od_w_out[i], od_cmp_pos[i], od_cmp_w1[i], od_cmp_b1[i],
                          od_cmp_w2[i], od_cmp_b2[i], cos, sin)
        x = x + g1 * y
        h = rms_norm(x, norm2_g[l]) * (1.0 + sc2) + sh2
        x = x + g2 * hier_moe(h, moe_wg[l], moe_bg[l], moe_we[l], moe_be[l],
                              moe_w_gate[l], moe_w_up[l], moe_w_down[l])
    return rms_norm(x, final_g)


DEPTH_2 = 1

SSD_INNER = D_MODEL
SSD_HEAD_DIM = 64
SSD_HEADS = SSD_INNER // SSD_HEAD_DIM
SSD_GROUPS = 4
SSD_STATE = 128
SSD_CHUNK = 128
SSD_CONV = 4
SSD_BC = SSD_GROUPS * SSD_STATE
SSD_CONV_CH = SSD_INNER + 2 * SSD_BC
DT_MIN = 0.001
DT_MAX = 0.1
ATT_HEAD_DIM = 64
ATT_HEADS = D_MODEL // 128
ATT_INNER = ATT_HEADS * ATT_HEAD_DIM
Q_BLOCK = 128
N_GROUPS = 4
EXPERTS_PER_GROUP = 4
N_EXPERTS = N_GROUPS * EXPERTS_PER_GROUP
TOP_K = 2
EXPERT_FF = D_MODEL // 2
IN_SIZES = (SSD_INNER, SSD_CONV_CH, SSD_HEADS, ATT_INNER, ATT_INNER, ATT_INNER, ATT_HEADS, D_MODEL, D_MODEL)
N_IN = sum(IN_SIZES)
N_MOD = 6
DEEPNORM_ALPHA = (2 * DEPTH_2) ** 0.25
DEEPNORM_BETA = (8 * DEPTH_2) ** -0.25
LN_EPS = 1e-5


def layer_norm(x, gain=None, bias=None):
    xf = x.astype(jnp.float32)
    mu = jnp.mean(xf, axis=-1, keepdims=True)
    var = jnp.mean(jnp.square(xf - mu), axis=-1, keepdims=True)
    y = ((xf - mu) * lax.rsqrt(var + LN_EPS)).astype(x.dtype)
    if gain is None:
        return y
    return y * gain + bias

def gated_rms_norm(y, z, w):
    g = (y * jax.nn.silu(z)).astype(jnp.float32)
    g = g * lax.rsqrt(jnp.mean(jnp.square(g), axis=-1, keepdims=True) + LN_EPS)
    return g.astype(y.dtype) * w

def causal_depthwise_conv(u, w, bias):
    k_width, ch = w.shape
    out = lax.conv_general_dilated(
        u, w[:, None, :].astype(u.dtype), window_strides=(1,),
        padding=((k_width - 1, 0),), dimension_numbers=('NWC', 'WIO', 'NWC'),
        feature_group_count=ch)
    return out + bias

def ssd_chunked(xh, dt, a_log, bmat, cmat):
    b, s, h, p = xh.shape
    g, n = bmat.shape[-2:]
    r = h // g
    L = SSD_CHUNK
    nc = s // L
    f32 = jnp.float32
    A = -jnp.exp(a_log.astype(f32))
    a = (dt * A).reshape(b, nc, L, g, r)
    xdt = (xh.astype(f32) * dt[..., None]).reshape(b, nc, L, g, r, p)
    bc = bmat.astype(f32).reshape(b, nc, L, g, n)
    cc = cmat.astype(f32).reshape(b, nc, L, g, n)
    a_cs = jnp.cumsum(a, axis=2)
    causal = jnp.tril(jnp.ones((L, L), dtype=bool))[None, None, :, :, None, None]
    seg = a_cs[:, :, :, None] - a_cs[:, :, None, :]
    decay = jnp.exp(jnp.where(causal, seg, -jnp.inf))
    cb = jnp.einsum('bclgn,bcsgn->bclsg', cc, bc)
    y_diag = jnp.einsum('bclsgr,bcsgrp->bclgrp', cb[..., None] * decay, xdt)
    to_end = jnp.exp(a_cs[:, :, -1:] - a_cs)
    states = jnp.einsum('bclgn,bclgrp->bcgrpn', bc, xdt * to_end[..., None])
    chunk_decay = jnp.exp(a_cs[:, :, -1])

    def carry_state(state, inp):
        st, dec = inp
        return state * dec[..., None, None] + st, state

    _, prev = lax.scan(carry_state, jnp.zeros_like(states[:, 0]),
                       (jnp.moveaxis(states, 1, 0), jnp.moveaxis(chunk_decay, 1, 0)))
    prev = jnp.moveaxis(prev, 0, 1)
    y_off = jnp.einsum('bclgn,bcgrpn->bclgrp', cc, prev) * jnp.exp(a_cs)[..., None]
    return (y_diag + y_off).reshape(b, s, h, p)

def forgetting_attention(q, k, v, log_f):
    b, s, h, d = q.shape
    fcum = jnp.cumsum(log_f.astype(jnp.float32), axis=1).transpose(0, 2, 1)
    scale = d ** -0.5
    q_pos = jnp.arange(Q_BLOCK)
    outs = []
    for i in range(s // Q_BLOCK):
        lo, hi = i * Q_BLOCK, (i + 1) * Q_BLOCK
        logits = jnp.einsum('bqhd,bkhd->bhqk', q[:, lo:hi], k[:, :hi]).astype(jnp.float32) * scale
        logits = logits + fcum[:, :, lo:hi, None] - fcum[:, :, None, :hi]
        causal = jnp.arange(hi)[None, :] <= (lo + q_pos)[:, None]
        logits = jnp.where(causal, logits, -jnp.inf)
        probs = jax.nn.softmax(logits, axis=-1).astype(v.dtype)
        outs.append(jnp.einsum('bhqk,bkhd->bqhd', probs, v[:, :hi]))
    return jnp.concatenate(outs, axis=1)

def hybrid_mixer(h, w_in, conv_w, conv_b, dt_bias, a_log, d_skip, ssd_norm_w, forget_b,
                 w_ssd_o, w_att_o, w_o):
    b, s, _ = h.shape
    split_points = np.cumsum(IN_SIZES)[:-1].tolist()
    proj = h @ w_in
    z, xbc, dt_raw, q, k, v, f_raw, g_ssd, g_att = jnp.split(proj, split_points, axis=-1)
    xbc = jax.nn.silu(causal_depthwise_conv(xbc, conv_w, conv_b))
    xs, bm, cm = jnp.split(xbc, [SSD_INNER, SSD_INNER + SSD_BC], axis=-1)
    dt = jax.nn.softplus((dt_raw + dt_bias).astype(jnp.float32))
    xh = xs.reshape(b, s, SSD_HEADS, SSD_HEAD_DIM)
    y = ssd_chunked(xh, dt, a_log,
                    bm.reshape(b, s, SSD_GROUPS, SSD_STATE),
                    cm.reshape(b, s, SSD_GROUPS, SSD_STATE))
    y = (y + d_skip[:, None] * xh).astype(h.dtype).reshape(b, s, SSD_INNER)
    y_ssd = gated_rms_norm(y, z, ssd_norm_w) @ w_ssd_o
    log_f = jax.nn.log_sigmoid((f_raw + forget_b).astype(jnp.float32))
    o = forgetting_attention(q.reshape(b, s, ATT_HEADS, ATT_HEAD_DIM),
                             k.reshape(b, s, ATT_HEADS, ATT_HEAD_DIM),
                             v.reshape(b, s, ATT_HEADS, ATT_HEAD_DIM), log_f)
    y_att = o.reshape(b, s, ATT_INNER) @ w_att_o
    merged = jax.nn.sigmoid(g_ssd) * y_ssd + jax.nn.sigmoid(g_att) * y_att
    return merged @ w_o

def hierarchical_moe(h, w_rg, b_rg, w_re, b_re, w_gate, w_up, w_down):
    b, s, d = h.shape
    t = h.reshape(-1, d)
    f32 = jnp.float32
    g_prob = jax.nn.softmax((t @ w_rg + b_rg).astype(f32), axis=-1)
    g_p, g_idx = lax.top_k(g_prob, 1)
    onehot_g = jax.nn.one_hot(g_idx[:, 0], N_GROUPS, dtype=f32)
    e_logits = (t @ w_re + b_re).astype(f32).reshape(-1, N_GROUPS, EXPERTS_PER_GROUP)
    e_in = jnp.einsum('tg,tge->te', onehot_g, e_logits)
    top_l, top_i = lax.top_k(e_in, TOP_K)
    w_k = jax.nn.softmax(top_l, axis=-1) * g_p
    w_group = jnp.einsum('tk,tke->te', w_k, jax.nn.one_hot(top_i, EXPERTS_PER_GROUP, dtype=f32))
    gates = (onehot_g[:, :, None] * w_group[:, None, :]).reshape(-1, N_EXPERTS).astype(t.dtype)
    out = jnp.zeros_like(t)
    for e in range(N_EXPERTS):
        hid = jax.nn.silu(t @ w_gate[e]) * (t @ w_up[e])
        out = out + gates[:, e:e + 1] * (hid @ w_down[e])
    return out.reshape(b, s, d)

def second_inputs(seed: int = 0) -> dict:
    key = jax.random.key(seed)
    ks = iter(jax.random.split(key, 32))
    f32 = jnp.float32

    def nrm(shape, scale):
        return jax.random.normal(next(ks), shape, f32) * scale

    offs = np.concatenate([[0], np.cumsum(IN_SIZES)])
    col_scale = np.ones((N_IN,), np.float32)
    col_scale[offs[1]:offs[1] + SSD_INNER] = DEEPNORM_BETA
    col_scale[offs[5]:offs[6]] = DEEPNORM_BETA
    dt0 = jnp.exp(jax.random.uniform(next(ks), (DEPTH_2, SSD_HEADS), f32)
                  * (math.log(DT_MAX) - math.log(DT_MIN)) + math.log(DT_MIN))
    return {
        'x': nrm((BATCH, SEQ, D_MODEL), 1.0),
        'c': nrm((BATCH, D_MODEL), 1.0),
        'w_mod': nrm((DEPTH_2, D_MODEL, N_MOD * D_MODEL), 0.5 * D_MODEL ** -0.5),
        'b_mod': nrm((DEPTH_2, N_MOD * D_MODEL), 0.02),
        'w_in': nrm((DEPTH_2, D_MODEL, N_IN), D_MODEL ** -0.5) * jnp.asarray(col_scale),
        'conv_w': nrm((DEPTH_2, SSD_CONV, SSD_CONV_CH), SSD_CONV ** -0.5),
        'conv_b': nrm((DEPTH_2, SSD_CONV_CH), 0.02),
        'dt_bias': dt0 + jnp.log(-jnp.expm1(-dt0)),
        'a_log': jnp.log(jax.random.uniform(next(ks), (DEPTH_2, SSD_HEADS), f32, minval=1.0, maxval=16.0)),
        'd_skip': 1.0 + nrm((DEPTH_2, SSD_HEADS), 0.1),
        'ssd_norm_w': 1.0 + nrm((DEPTH_2, SSD_INNER), 0.05),
        'forget_b': jax.random.uniform(next(ks), (DEPTH_2, ATT_HEADS), f32, minval=1.0, maxval=4.0),
        'w_ssd_o': nrm((DEPTH_2, SSD_INNER, D_MODEL), DEEPNORM_BETA * SSD_INNER ** -0.5),
        'w_att_o': nrm((DEPTH_2, ATT_INNER, D_MODEL), DEEPNORM_BETA * ATT_INNER ** -0.5),
        'w_o': nrm((DEPTH_2, D_MODEL, D_MODEL), DEEPNORM_BETA * D_MODEL ** -0.5),
        'ln1_g': 1.0 + nrm((DEPTH_2, D_MODEL), 0.05),
        'ln1_b': nrm((DEPTH_2, D_MODEL), 0.02),
        'w_router_group': nrm((DEPTH_2, D_MODEL, N_GROUPS), D_MODEL ** -0.5),
        'b_router_group': nrm((DEPTH_2, N_GROUPS), 0.01),
        'w_router_expert': nrm((DEPTH_2, D_MODEL, N_EXPERTS), D_MODEL ** -0.5),
        'b_router_expert': nrm((DEPTH_2, N_EXPERTS), 0.01),
        'w_gate': nrm((DEPTH_2, N_EXPERTS, D_MODEL, EXPERT_FF), D_MODEL ** -0.5),
        'w_up': nrm((DEPTH_2, N_EXPERTS, D_MODEL, EXPERT_FF), DEEPNORM_BETA * D_MODEL ** -0.5),
        'w_down': nrm((DEPTH_2, N_EXPERTS, EXPERT_FF, D_MODEL), DEEPNORM_BETA * EXPERT_FF ** -0.5),
        'ln2_g': 1.0 + nrm((DEPTH_2, D_MODEL), 0.05),
        'ln2_b': nrm((DEPTH_2, D_MODEL), 0.02),
    }

def second_block(x, c, w_mod, b_mod, w_in, conv_w, conv_b, dt_bias, a_log, d_skip, ssd_norm_w,
              forget_b, w_ssd_o, w_att_o, w_o, ln1_g, ln1_b, w_router_group, b_router_group,
              w_router_expert, b_router_expert, w_gate, w_up, w_down, ln2_g, ln2_b):
    c_act = jax.nn.silu(c)
    for l in range(DEPTH_2):
        mod = (c_act @ w_mod[l] + b_mod[l])[:, None, :]
        sh1, sc1, gt1, sh2, sc2, gt2 = jnp.split(mod, N_MOD, axis=-1)
        h = layer_norm(x) * (1.0 + sc1) + sh1
        y = hybrid_mixer(h, w_in[l], conv_w[l], conv_b[l], dt_bias[l], a_log[l], d_skip[l],
                         ssd_norm_w[l], forget_b[l], w_ssd_o[l], w_att_o[l], w_o[l])
        x = layer_norm(DEEPNORM_ALPHA * x + (1.0 + gt1) * y, ln1_g[l], ln1_b[l])
        h = layer_norm(x) * (1.0 + sc2) + sh2
        y = hierarchical_moe(h, w_router_group[l], b_router_group[l], w_router_expert[l],
                             b_router_expert[l], w_gate[l], w_up[l], w_down[l])
        x = layer_norm(DEEPNORM_ALPHA * x + (1.0 + gt2) * y, ln2_g[l], ln2_b[l])
    return x


def setup_inputs(seed=0):
    out = dict(first_inputs(seed))
    for name, value in second_inputs(seed + 1).items():
        if name != "x":
            out[name + "_2"] = value
    return out


def reference(
    x, c, norm1_g, norm2_g, final_g, ada_w, ada_b, ev_w_in, ev_w_out, ev_lambda, ev_subln_g,
    od_w_in, od_w_out, od_cmp_pos, od_cmp_w1, od_cmp_b1, od_cmp_w2, od_cmp_b2, moe_wg, moe_bg,
    moe_we, moe_be, moe_w_gate, moe_w_up, moe_w_down, c_2, w_mod_2, b_mod_2, w_in_2, conv_w_2,
    conv_b_2, dt_bias_2, a_log_2, d_skip_2, ssd_norm_w_2, forget_b_2, w_ssd_o_2, w_att_o_2,
    w_o_2, ln1_g_2, ln1_b_2, w_router_group_2, b_router_group_2, w_router_expert_2,
    b_router_expert_2, w_gate_2, w_up_2, w_down_2, ln2_g_2, ln2_b_2,
):
    x = first_block(
        x, c, norm1_g, norm2_g, final_g, ada_w, ada_b, ev_w_in, ev_w_out, ev_lambda, ev_subln_g,
        od_w_in, od_w_out, od_cmp_pos, od_cmp_w1, od_cmp_b1, od_cmp_w2, od_cmp_b2, moe_wg,
        moe_bg, moe_we, moe_be, moe_w_gate, moe_w_up, moe_w_down,
    )
    return second_block(
        x, c_2, w_mod_2, b_mod_2, w_in_2, conv_w_2, conv_b_2, dt_bias_2, a_log_2, d_skip_2,
        ssd_norm_w_2, forget_b_2, w_ssd_o_2, w_att_o_2, w_o_2, ln1_g_2, ln1_b_2,
        w_router_group_2, b_router_group_2, w_router_expert_2, b_router_expert_2, w_gate_2,
        w_up_2, w_down_2, ln2_g_2, ln2_b_2,
    )


_drawn_inputs = setup_inputs


def setup_inputs(seed=0):
    import zlib

    import numpy as np

    out = dict(_drawn_inputs(seed))
    spreads = {}
    factors = {'norm1_g': 8.0,
     'norm2_g': 3.541,
     'ev_lambda': 8.0,
     'ev_subln_g': 6.379,
     'od_cmp_pos': 5.244,
     'od_cmp_b1': 8.0,
     'od_cmp_b2': 27.39,
     'moe_bg': 6.619,
     'moe_be': 8.0,
     'b_mod_2': 3.979,
     'conv_b_2': 5.006,
     'd_skip_2': 5.72,
     'ssd_norm_w_2': 6.205,
     'forget_b_2': 25.776,
     'b_router_group_2': 18.442,
     'b_router_expert_2': 56.318,
     'ln2_b_2': 2.822}
    for name, (base, spread) in spreads.items():
        noise = np.random.default_rng([zlib.crc32(name.encode()), seed]).standard_normal(out[name].shape)
        drawn = base * np.exp(spread * noise) if base else spread * noise
        out[name] = jnp.asarray(drawn.astype(out[name].dtype))
    for name, factor in factors.items():
        out[name] = (out[name] * factor).astype(out[name].dtype)
    return out
```

```python
import math
from contextlib import ExitStack

import numpy as np

import concourse.bass as bass
from concourse import mybir

F32 = mybir.dt.float32
ALU = mybir.AluOpType
ACT = mybir.ActivationFunctionType
AX = mybir.AxisListType

P = 128
T = 256
TT = T // P
D = 1024
C = D // P
HD = 64
HALF_ROPE = 8
SCALE = HD ** -0.5
NEG = -1e30
RMS_EPS = 1e-6
LN_EPS = 1e-5
ALPHA = 2 ** 0.25
LAMBDA_INIT = 0.8 - 0.6 * math.exp(0.0)
NSLOT = 6
SLOT = 4096
NSMALL = 28
NCMP = (T - 32) // 16 + 1
GELU = ACT.Gelu_apprx_tanh

PHASES = [("ada0", 12), ("evin", 6), ("evout", 2), ("moe0", 24),
          ("ada1", 12), ("odin", 5), ("cmp", 2), ("odout", 2), ("moe1", 24),
          ("ada2", 12), ("xbc", 4), ("z", 2), ("ssdo", 2), ("qkv", 3), ("atto", 1),
          ("gates", 4), ("wo", 2), ("moe2", 48)]
TILE = {}
_n = 0
for _name, _k in PHASES:
    TILE[_name] = _n
    _n += _k
NTILES = _n
LOADS_PER_TILE = {}
for _n in range(NTILES):
    LOADS_PER_TILE[_n] = 1
for _moe in ("moe0", "moe1"):
    _u = 8
    for _n in range(TILE[_moe], TILE[_moe] + 3 * _u):
        _r = _n - TILE[_moe]
        _down = _r == 3 * _u - 1 or (_r >= 2 and (_r - 2) % 3 == 2)
        LOADS_PER_TILE[_n] = 1 if _down else 2
for _n in range(TILE["cmp"], TILE["cmp"] + 2):
    LOADS_PER_TILE[_n] = 1
LANDED = {}
_count = [0] * NSLOT
for _n in range(NTILES):
    _count[_n % NSLOT] += 16 * LOADS_PER_TILE[_n]
    LANDED[_n] = _count[_n % NSLOT]

TRANS = {}


def unit_tile(base, u):
    return base + (3 * u - 1 if u else 0)

TRANS_STAGES = [("h0", 4), ("qk0", 8), ("att0", 12), ("ob", 2), ("h1", 4),
                ("h2", 4), ("qkv1", 12), ("cmph", 1), ("att1", 48), ("h3", 4),
                ("h4", 4), ("xs", 4), ("btok", 1), ("gated", 4), ("qk2", 4), ("att2", 8),
                ("merged", 4), ("h5", 4)]
_n = 0
for _name, _k in TRANS_STAGES:
    TRANS[_name] = _n
    _n += _k
TRANS_END = {_name: TRANS[_name] + _k for _name, _k in TRANS_STAGES}

PROJ_STAGES = [("evin", 6, 1, 1), ("evout", 2, 0, 1), ("odin", 6, 1, 1), ("odout", 2, 0, 1),
               ("xbc", 4, 1, 1), ("z", 2, 1, 0), ("ssdo", 2, 1, 1), ("qkv", 3, 1, 1),
               ("atto", 2, 1, 1), ("gates", 4, 1, 0), ("wo", 2, 0, 1)]
PROJ = {}
PROJ_ACT, PROJ_DVE = [], []
for _name, _k, _a, _d in PROJ_STAGES:
    PROJ[_name] = len(PROJ_ACT)
    for _ in range(_k):
        PROJ_ACT.append((PROJ_ACT[-1] if PROJ_ACT else 0) + _a)
        PROJ_DVE.append((PROJ_DVE[-1] if PROJ_DVE else 0) + _d)

SOFT = {"att0": 0, "att1": 16, "att2": 48}
OTB = {"att0": 0, "att1": 8, "att2": 16}
NORMS = ["h0", "h1", "h2", "h3", "h4", "h5"]
COL = {}


def col_rows(params):
    out = []

    def put(name, tile, row, view):
        COL[name] = tile * P + row
        out.append((tile, row, view.shape[0], view))

    put("ada_b", 0, 0, params["ada_b"].rearrange("l (r p) -> (l r) p", p=P))
    put("norm1_g", 0, 96, params["norm1_g"].rearrange("l (r p) -> (l r) p", p=P))
    put("norm2_g", 0, 112, params["norm2_g"].rearrange("l (r p) -> (l r) p", p=P))
    put("b_mod_2", 1, 0, params["b_mod_2"].rearrange("l (r p) -> (l r) p", p=P))
    put("conv_w_2", 1, 48, params["conv_w_2"].rearrange("l k (r p) -> (l k r) p", p=P))
    put("conv_b_2", 1, 112, params["conv_b_2"].rearrange("l (r p) -> (l r) p", p=P))
    put("c", 2, 0, params["c"].rearrange("l (r p) -> (l r) p", p=P))
    put("c_2", 2, 8, params["c_2"].rearrange("l (r p) -> (l r) p", p=P))
    put("ssd_norm_w_2", 2, 16, params["ssd_norm_w_2"].rearrange("l (r p) -> (l r) p", p=P))
    put("ev_subln_g", 2, 24, params["ev_subln_g"])
    put("pos", 2, 25, params["od_cmp_pos"].rearrange("o k (r l) d -> (o k r) (l d)", l=2))
    return out


class Semaphores(dict):

    def __init__(self, nc, ctx):
        super().__init__()
        self.nc, self.ctx = nc, ctx

    def __missing__(self, name):
        self[name] = self.ctx.enter_context(self.nc.semaphore(name))
        return self[name]


def two_blocks(nc, params, rope, out):
    with ExitStack() as ctx:
        emit(nc, ctx, params, rope, out)


def emit(nc, ctx, p, rope_dram, out):
    def sb(name, shape):
        return ctx.enter_context(nc.sbuf_tensor(name, shape, F32))

    ring = [sb(f"ring{i}", [P, SLOT]) for i in range(NSLOT)]
    x = sb("x", [P, TT, D])
    hT = sb("hT", [P, C, T])
    gate1 = sb("gate1", [P, D])
    gate2 = sb("gate2", [P, D])
    PBW = 3584
    pb = sb("pb", [P, TT, PBW])
    pb_flat = pb[:].rearrange("p a b -> p (a b)")
    A = sb("A", [P, 24, T])
    A_flat = A[:].rearrange("p a b -> p (a b)")
    OT = sb("OT", [P, C, T])
    OT_flat = OT[:].rearrange("p a b -> p (a b)")
    Pm = sb("Pm", [P, 2, 384])
    PT = sb("PT", [P, 2, 384])
    tmp = sb("tmp", [P, 2, 512])
    S_sb = tmp[:, :, 0:384]
    ident = sb("ident", [P, P])
    mask384 = sb("mask384", [P, 384])
    maskT = sb("maskT", [P, P])
    tri_one = sb("tri_one", [P, T])
    tri = tri_one[:, 0:P]
    tri_gt = sb("tri_gt", [P, P])
    zeros = sb("zeros", [P, P])
    mark = sb("mark", [P, 8])
    maskc = sb("maskc", [P, TT, NCMP])
    cmp_live = sb("cmp_live", [P, TT])
    cosd = sb("cosd", [P, TT, 16])
    sind = sb("sind", [P, TT, 16])
    ropeA, ropeB = (Pm[:, i, 0:256].rearrange("p (a h d) -> p a h d", a=TT, h=8) for i in range(2))
    cols = sb("cols", [P, 3 * P])
    stage = A
    modc = sb("modc", [P, 4, C])
    cact = sb("cact", [P, 2 * C])
    stats = sb("stats", [P, TT, 2, 6])
    mv = sb("mv", [P, TT, 2])
    rstd = sb("rstd", [P, TT])
    nhalf = sb("nhalf", [P, 8])
    nmx = sb("nmx", [P, 2, 2])
    rs = sb("rs", [P, 2, 2])
    rr = sb("rr", [P, 2, 2])
    lam = sb("lam", [P, 8])
    lamrow = sb("lamrow", [P, 4, HD])
    subc = sb("subc", [P, 1])
    obs = sb("obs", [P, 8])
    wr = [sb(f"wr{i}", [P, C, 20]) for i in range(3)]
    br = [sb(f"br{i}", [P, 20]) for i in range(3)]
    w48 = A_flat[:, 4096:4096 + C * 48].rearrange("p (c n) -> p c n", c=C)
    wdf = sb("wdf", [P, C, 24])
    gts = sb("gts", [P, TT, 48])
    rt = sb("rt", [P, TT, 16, 4])
    comb = sb("comb", [P, TT, 16])
    first = sb("first", [P, 4])
    b1c = OT_flat[0:60, 512:1024].rearrange("p (k f) -> p k f", k=2)
    b2v = sb("b2v", [NCMP, HD])
    w2c = sb("w2c", [P, 2, 3, HD])
    b2k = sb("b2k", [P, 1])
    kcmpT = sb("kcmpT", [P, 60])
    vcmp = sb("vcmp", [NCMP, 4, HD])
    cs = sb("cs", [P, 4, 32])
    dts = sb("dts", [P, 6, TT, 24])
    bdf = sb("bdf", [P, 24])
    alog = sb("alog", [P, 16])
    dsk = sb("dsk", [P, 16])
    B = [ctx.enter_context(nc.psum_tensor(f"bank{i}", [P, 512], F32)) for i in range(8)]
    s = Semaphores(nc, ctx)
    for i in range(NSLOT):
        s[f"landed{i}"]
    landed = [s[f"landed{i}"] for i in range(NSLOT)]
    tile_used = s["tile_used"]

    colrows = col_rows(p)

    def col(name, i=0, n=1):
        return cols[:, COL[name] + i:COL[name] + i + n]

    def bc(ap, axis, shape):
        return ap.unsqueeze(axis).broadcast_to(shape)

    def trans_evacuated(eng, k):
        eng.wait_ge(s["tr_act"] if k % 2 == 0 else s["tr_dve"], k // 2 + 1)

    def stage_transposed(eng, name):
        for k in (TRANS_END[name] - 2, TRANS_END[name] - 1):
            if k >= 0:
                trans_evacuated(eng, k)

    def proj_evacuated(eng, m):
        if PROJ_ACT[m]:
            eng.wait_ge(s["proj_act"], PROJ_ACT[m])
        if PROJ_DVE[m]:
            eng.wait_ge(s["proj_dve"], PROJ_DVE[m])

    def tile_ready(eng, n):
        eng.wait_ge(tile_used, n + 1)

    def head(buf, chunk, half):
        return buf[half * HD:(half + 1) * HD, chunk, :]

    def attention_items(stage_name):
        items = []
        u, k, o = SOFT[stage_name], TRANS[stage_name], OTB[stage_name]

        def plain_pv(vbuf, voff, half, bank, start, stop):
            def pv(pt):
                dst = B[bank][half * HD:(half + 1) * HD, 0:T]
                v = [vbuf[:, tt, voff:voff + HD] for tt in range(TT)]
                return [(dst, v[0], pt[:, 0:T], start, False),
                        (dst[:, P:T], v[1], pt[:, T:384], False, stop)]
            return pv

        if stage_name in ("att0", "att2"):
            for h in range(8):
                ot = o + h // 2
                items.append(dict(
                    soft=u, tr=k, kind="plain", q=head(A, h // 2, h % 2), k=head(A, 4 + h // 2, h % 2),
                    pv=plain_pv(pb, (1024 if stage_name == "att0" else 1024) + h * HD, h % 2, ot % 2, True, True),
                    forget=h if stage_name == "att2" else None,
                    ot=ot, ot_first=h % 2 == 0,
                    evac=(OT[:, h // 2, :], B[ot % 2][:, 0:T]) if h % 2 else None, gate=None))
                u, k = u + 1, k + 1
        if stage_name == "att0":
            for h in range(4):
                for m in range(2):
                    ot = o + 4 + h

                    def pv(pt, h=h, ot=ot):
                        bank = B[ot % 2][:, 0:T]
                        v = [pb[:, tt, 2560 + h * P:2560 + (h + 1) * P] for tt in range(TT)]
                        return [(bank[:, 0:P], pt[:, 0:P], v[0], True, True),
                                (bank[:, P:T], pt[:, P:T], v[0], True, False),
                                (bank[:, P:T], pt[:, T:384], v[1], False, True)]
                    items.append(dict(
                        soft=u, tr=k if m else None, kind=f"map{m}", q=head(A, 8 + h, m), k=head(A, 12 + h, m),
                        pv=pv, forget=None, ot=ot, ot_first=True, gate=None,
                        evac=(pb[:, :, h * P:(h + 1) * P], B[ot % 2][:, 0:T].rearrange("p (a b) -> p a b", a=TT))))
                    u += 1
                k += 1
        if stage_name == "att1":
            for h in range(16):
                g = h // 4
                ot = o + h // 2
                for b, (kc0, voff) in enumerate(((16, 3072), (20, 3328))):
                    items.append(dict(
                        soft=u, tr=k, kind="plain", q=head(A, h // 2, h % 2), k=head(A, kc0 + g, h % 2),
                        pv=plain_pv(pb, voff + g * HD, h % 2, ot % 2, b == 0, False), forget=None,
                        ot=ot, ot_first=h % 2 == 0 and b == 0, gate=(h, b + 1), evac=None))
                    u, k = u + 1, k + 1

                def pv(pt, g=g, h=h, ot=ot):
                    dst = B[ot % 2][(h % 2) * HD:(h % 2 + 1) * HD, 0:T]
                    return [(dst, vcmp[:, g, :], pt[0:NCMP, 0:T], False, True)]
                items.append(dict(
                    soft=None, tr=k, kind="cmp", h=h, pv=pv, ot=ot, ot_first=False, gate=None, forget=None,
                    evac=(OT[:, h // 2, :], B[ot % 2][:, 0:T]) if h % 2 else None))
                k += 1
        return items

    ITEMS = {name: attention_items(name) for name in SOFT}
    PV_BASE = {"att0": 0, "att1": 12, "att2": 60}
    for name in SOFT:
        n = PV_BASE[name]
        for it in ITEMS[name]:
            it["pvn"] = n
            if it["tr"] is not None:
                n += 1
    ALL = [it for name in ("att0", "att1", "att2") for it in ITEMS[name]]
    READER = {it["soft"]: it["tr"] for it in ALL if it["soft"] is not None}
    ALL_TR = [it for it in ALL if it["tr"] is not None]
    PREV_PV = {}
    last_on = {}
    for it in ALL_TR:
        PREV_PV[it["tr"]] = last_on.get(it["tr"] % 2)
        last_on[it["tr"] % 2] = it["pvn"]
    OT_DONE = {}
    for it in ALL_TR:
        OT_DONE[it["ot"]] = it["pvn"] + 1

    MOE = {"moe0": dict(U=8, silu=0, hid=0, idx=0), "moe1": dict(U=8, silu=16, hid=8, idx=1),
           "moe2": dict(U=16, silu=32, hid=16, idx=2)}
    hidb = [A[:, 0:4, :], A[:, 4:8, :]]
    silub = [A[:, 8:12, :], A[:, 12:16, :]]
    combT = pb_flat[:, 0:16 * T].rearrange("p (e t) -> p e t", e=16)
    rowp = A[:, 16:24, :].rearrange("p (r a) t -> p r (a t)", r=2)

    cmph = OT_flat[0:60, 0:512].rearrange("p (k f) -> p k f", k=2)
    hidT_c = OT_flat[:, 1024:1264]
    cmpB = pb[:, :, 0:960].rearrange("p k (l g n) -> p k l g n", l=16, g=4)
    pc = pb[:, 0, 1024:1504]
    xT = A_flat[:, 0:16 * 259].rearrange("p (c t) -> p c t", t=259)
    mt = [A_flat[:, 4144 + 512 * b:4656 + 512 * b] for b in range(2)]
    xdte = OT_flat[:, 0:D]
    stT = OT_flat[:, D:2 * D]
    Btok = pb[:, 0, 3072:3584]
    satt = A[:, 8:16, :].rearrange("p (a c) t -> p a (c t)", a=TT)

    def odd_kv(copy, j, tt, bank):
        def twice(c0, src):
            return copy(pb[:, tt, c0:c0 + 512].rearrange("p (g e d) -> p g e d", g=4, e=2),
                        bc(src.rearrange("p (g d) -> p g d", g=4), 2, [P, 4, 2, HD]))
        twice({2: 1024, 3: 2048, 4: 2560}[j], bank[:, 0:256])
        if j == 2:
            return twice(1536, bank[:, 256:512])
        return copy(pb[:, tt, 3072 + 256 * (j - 3):3328 + 256 * (j - 3)], bank[:, 256:512])

    def evacuate_p(eng, it, copy, done):
        k = it["tr"]
        eng.wait_ge(s["tr_ready"], k + 1)
        if PREV_PV[k] is not None:
            eng.wait_ge(s["pv_done"], PREV_PV[k] + 1)
        rows, width = (NCMP, T) if it["kind"] == "cmp" else (P, 384)
        copy(PT[0:rows, k % 2, 0:width], B[4 + k % 2][0:rows, 0:width]).then_inc(s[done], 1)

    def routing_exp(act, name):
        i = MOE[name]["idx"]
        act.wait_ge(s["route_shifted"], i + 1)
        nc.scalar.activation(rt[:, :, 0:2, :], rt[:, :, 0:2, :], ACT.Exp).then_inc(s["route_exp"], 1)
        for j in range(8):
            if j % 2 == 0:
                act.wait_ge(s["combT_ready"], 8 * i + j + 1)
                nc.scalar.copy(combT[:, 2 * j:2 * j + 2, :], B[j % 4][:]).then_inc(s["combT_act"], 1)

    block = ctx.enter_context(nc.Block())

    @block.sync
    def _(sp):
        def slot_free(n):
            if isinstance(n, int):
                if n >= NSLOT:
                    sp.wait_ge(tile_used, n - NSLOT + 1)
            else:
                sp.wait_ge(tile_used, n - (NSLOT - 1))

        def load(n, slot, view, src, wait=True):
            if wait:
                slot_free(n)
            sp.dma_start(view, src).then_inc(landed[slot], 16)

        def kview(slot, width=512):
            return ring[slot][:].rearrange("p (c n) -> p c n", n=width)

        def columns(w, n0, col0, tiles):
            for j in range(tiles):
                n = n0 + j
                load(n, n % NSLOT, kview(n % NSLOT),
                     w.rearrange("(c p) n -> p c n", p=P)[:, :, col0 + 512 * j:col0 + 512 * (j + 1)])

        def ada(name, w):
            n0 = TILE[name]
            wv = w.rearrange("(c p) n -> p c n", p=P)
            with sp.Fori(0, 2) as i:
                for j in range(6):
                    slot = (n0 + j) % NSLOT
                    sp.wait_ge(tile_used, 6 * i + (n0 + j - NSLOT + 1))
                    sp.dma_start(kview(slot), wv[:, :, bass.ds(3072 * i + 512 * j, 512)]).then_inc(landed[slot], 16)

        def moe_small(name, wg, wu, wd):
            n0, U = TILE[name], 8
            gv = wg.rearrange("e (c p) f -> e p c f", p=P)
            uv = wu.rearrange("e (c p) f -> e p c f", p=P)
            dv = wd.rearrange("(u e) (k p) d -> u p (e k) d", p=P, e=2)

            def pick(v, i):
                return v[i] if isinstance(i, int) else v[bass.ds(i, 1)].rearrange("o p c f -> (o p) c f")

            def inputs(u, n, slots):
                for j in range(2):
                    slot = slots[j]
                    slot_free(n + j)
                    kv = ring[slot][:].rearrange("p (g c f) -> p g c f", g=2, f=256)
                    sp.dma_start(kv[:, 0], pick(gv, 2 * u + j)).then_inc(landed[slot], 16)
                    sp.dma_start(kv[:, 1], pick(uv, 2 * u + j)).then_inc(landed[slot], 16)

            def down(u, n, slot):
                slot_free(n)
                sp.dma_start(kview(slot, D), pick(dv, u)).then_inc(landed[slot], 16)
            stream(n0, U, inputs, down)

        def moe_large(name, wg, wu, wd):
            n0, U = TILE[name], 16
            gv = wg.rearrange("e (c p) f -> e p c f", p=P)
            uv = wu.rearrange("e (c p) f -> e p c f", p=P)
            dv = wd.rearrange("e (k p) d -> e p k d", p=P)

            def pick(v, i):
                return v[i] if isinstance(i, int) else v[bass.ds(i, 1)].rearrange("o p c f -> (o p) c f")

            def inputs(u, n, slots):
                for j, v in enumerate((gv, uv)):
                    slot_free(n + j)
                    sp.dma_start(kview(slots[j]), pick(v, u)).then_inc(landed[slots[j]], 16)

            def down(u, n, slot):
                slot_free(n)
                sp.dma_start(kview(slot, D), pick(dv, u)).then_inc(landed[slot], 16)
            stream(n0, U, inputs, down)

        def stream(n0, U, inputs, down):
            inputs(0, n0, [n0 % NSLOT, (n0 + 1) % NSLOT])
            with sp.Fori(0, (U - 2) // 2) as i:
                for j in range(2):
                    u = 1 + j
                    n = unit_tile(n0, u)
                    slots = [(n + a) % NSLOT for a in range(3)]
                    inputs(2 * i + u, 6 * i + n, slots)
                    down(2 * i + (u - 1), 6 * i + (n + 2), slots[2])
            u = U - 1
            n = unit_tile(n0, u)
            inputs(u, n, [n % NSLOT, (n + 1) % NSLOT])
            down(u - 1, n + 2, (n + 2) % NSLOT)
            down(u, n + 3, (n + 3) % NSLOT)

        columns(p["ada_w"][0], TILE["ada0"], 0, 12)
        columns(p["ev_w_in"][0], TILE["evin"], 0, 6)
        columns(p["ev_w_out"][0], TILE["evout"], 0, 2)
        moe_small("moe0", p["moe_w_gate"][0], p["moe_w_up"][0], p["moe_w_down"][0])
        ada("ada1", p["ada_w"][1])
        columns(p["od_w_in"][0], TILE["odin"], 0, 5)
        for j in range(2):
            n = TILE["cmp"] + j
            load(n, n % NSLOT, kview(n % NSLOT, 256), p["od_cmp_w1"][0, j].rearrange("(r p) f -> p r f", p=P))
        columns(p["od_w_out"][0], TILE["odout"], 0, 2)
        moe_small("moe1", p["moe_w_gate"][1], p["moe_w_up"][1], p["moe_w_down"][1])
        ada("ada2", p["w_mod_2"][0])
        columns(p["w_in_2"][0], TILE["xbc"], 1024, 4)
        columns(p["w_in_2"][0], TILE["z"], 0, 2)
        columns(p["w_ssd_o_2"][0], TILE["ssdo"], 0, 2)
        columns(p["w_in_2"][0], TILE["qkv"], 3088, 3)
        n = TILE["atto"]
        load(n, n % NSLOT, kview(n % NSLOT, D), p["w_att_o_2"][0].rearrange("(c p) n -> p c n", p=P))
        columns(p["w_in_2"][0], TILE["gates"], 4632, 4)
        columns(p["w_o_2"][0], TILE["wo"], 0, 2)
        moe_large("moe2", p["w_gate_2"][0], p["w_up_2"][0], p["w_down_2"][0])
        sp.wait_ge(s["result"], 1)
        sp.dma_start(out.rearrange("b (a p) d -> p (b a) d", p=P), x[:]).then_inc(s["stored"], 16)
        sp.wait_ge(s["stored"], 16)

    @block.gpsimd
    def _(pool):
        steps = [0]

        def step(ins):
            steps[0] += 1
            ins.then_inc(s["pool_step"], 1)
            pool.wait_ge(s["pool_step"], steps[0])

        g = nc.gpsimd
        step(g.memset(ident[:], 0.0))
        step(g.affine_select(out=ident[:], in_=ident[:], compare_op=ALU.not_equal, fill=1.0, base=0,
                             pattern=[[-1, P]], channel_multiplier=1))
        g.memset(zeros[:], 0.0)
        g.memset(nhalf[:], -0.5)
        g.memset(tri_one[:], 1.0)
        g.memset(tri_gt[:], 1.0)
        g.memset(maskT[:], 0.0)
        g.memset(mask384[:], 0.0)
        g.memset(maskc[:], 0.0)
        g.memset(cmp_live[:], 1.0)
        for j in range(4):
            ins = g.memset(first[:, j:j + 1], 4.0 - j)
        step(ins)
        g.affine_select(out=tri, in_=tri, compare_op=ALU.is_ge, fill=0.0, base=0,
                        pattern=[[1, P]], channel_multiplier=-1)
        g.affine_select(out=tri_gt[:], in_=tri_gt[:], compare_op=ALU.is_gt, fill=0.0, base=0,
                        pattern=[[-1, P]], channel_multiplier=1)
        g.affine_select(out=maskT[:], in_=maskT[:], compare_op=ALU.is_ge, fill=NEG, base=0,
                        pattern=[[1, P]], channel_multiplier=-1)
        for a in (0, 2 * P):
            g.affine_select(out=mask384[:, a:a + P], in_=mask384[:, a:a + P], compare_op=ALU.is_ge, fill=NEG,
                            base=0, pattern=[[-1, P]], channel_multiplier=1)
        for a in range(TT):
            g.affine_select(out=maskc[:, a, :], in_=maskc[:, a, :], compare_op=ALU.is_ge, fill=NEG,
                            base=P * a - 31, pattern=[[-16, NCMP]], channel_multiplier=1)
        step(g.affine_select(out=cmp_live[:, 0:1], in_=cmp_live[:, 0:1], compare_op=ALU.is_ge, fill=0.0,
                             base=-31, pattern=[[0, 1]], channel_multiplier=1))
        g.memset(mark[:, 0:1], 0.0).then_inc(s["constants"], 1)
        pool.wait_ge(s["small_loads"], 16 * NSMALL)

        ropes = [0]

        def rope(col0, m):
            proj_evacuated(pool, m)
            t = pb[:, :, col0:col0 + 512].rearrange("p a (h d) -> p a h d", d=HD)[:, :, :, 0:16]
            cb = bc(cosd[:], 2, [P, TT, 8, 16])
            sbb = bc(sind[:], 2, [P, TT, 8, 16])
            g.tensor_tensor(ropeA[:], t, cb, ALU.mult)
            step(g.tensor_tensor(ropeB[:], t, sbb, ALU.mult))
            g.tensor_tensor(t[:, :, :, 0:8], ropeA[:, :, :, 0:8], ropeB[:, :, :, 8:16], ALU.subtract)
            step(g.tensor_tensor(t[:, :, :, 8:16], ropeA[:, :, :, 8:16], ropeB[:, :, :, 0:8], ALU.add))
            ropes[0] += 1
            g.memset(mark[:, 0:1], 0.0).then_inc(s["roped"], 1)

        powers = [0]

        def power(dst, src):
            powers[0] += 1
            pool.wait_ge(s["var_ready"], powers[0])
            g.tensor_tensor(dst, src, nhalf[:, 0:src.shape[-1]], ALU.pow).then_inc(s["pow_done"], 1)

        power(rstd[:], rstd[:])
        for c0, j in ((0, 0), (512, 1), (1536, 3), (2048, 4)):
            rope(c0, PROJ["evin"] + j)
        power(obs[:], obs[:])
        power(rstd[:], rstd[:])
        power(rstd[:], rstd[:])
        for c0, j in ((0, 0), (512, 1), (1024, 2), (2048, 3), (2560, 4)):
            rope(c0, PROJ["odin"] + j)
        power(rstd[:], rstd[:])
        power(rstd[:], rstd[:])
        power(rstd[:], rstd[:])
        power(rstd[:], rstd[:])
        power(rstd[:], rstd[:])
        power(rstd[:], rstd[:])
        power(rstd[:], rstd[:])

    @block.scalar
    def _(act):
        a = nc.scalar
        ndma = [0]

        def small(dst, src):
            ndma[0] += 1
            act.dma_start(dst, src).then_inc(s["small_loads"], 16)

        act.dma_start(x[:], p["x"].rearrange("b (a q) d -> q (b a) d", q=P)).then_inc(s["x_loaded"], 16)
        for tile, row, n, view in colrows:
            act.dma_start(stage[row:row + n, tile, 0:P], view).then_inc(s["rows_loaded"], 16)
        act.dma_start(gate1[:], p["ada_b"][0, 2048:3072].partition_broadcast(P)).then_inc(s["gate_bias"], 16)
        act.dma_start(gate2[:], p["ada_b"][0, 5120:6144].partition_broadcast(P)).then_inc(s["gate_bias"], 16)
        small(cosd[:], rope_dram[0].rearrange("(a q) d -> q a d", q=P))
        small(sind[:], rope_dram[1].rearrange("(a q) d -> q a d", q=P))
        small(lamrow[:], p["ev_lambda"][0].partition_broadcast(P))
        for i in range(2):
            small(wr[i][:, :, 0:4], p["moe_wg"][i].rearrange("(c q) n -> q c n", q=P))
            small(wr[i][:, :, 4:20], p["moe_we"][i].rearrange("(c q) n -> q c n", q=P))
            small(br[i][:, 0:4], p["moe_bg"][i].partition_broadcast(P))
            small(br[i][:, 4:20], p["moe_be"][i].partition_broadcast(P))
        small(wr[2][:, :, 0:4], p["w_router_group_2"][0].rearrange("(c q) n -> q c n", q=P))
        small(wr[2][:, :, 4:20], p["w_router_expert_2"][0].rearrange("(c q) n -> q c n", q=P))
        small(br[2][:, 0:4], p["b_router_group_2"][0].partition_broadcast(P))
        small(br[2][:, 4:20], p["b_router_expert_2"][0].partition_broadcast(P))
        small(w48[:], p["od_w_in"][0].rearrange("(c q) n -> q c n", q=P)[:, :, 2560:2608])
        wv = p["w_in_2"][0].rearrange("(c q) n -> q c n", q=P)
        small(wdf[:, :, 0:16], wv[:, :, 3072:3088])
        small(wdf[:, :, 16:24], wv[:, :, 4624:4632])
        small(bdf[:, 0:16], p["dt_bias_2"][0].partition_broadcast(P))
        small(bdf[:, 16:24], p["forget_b_2"][0].partition_broadcast(P))
        small(alog[:], p["a_log_2"][0].partition_broadcast(P))
        small(dsk[:], p["d_skip_2"][0].partition_broadcast(P))
        small(b2v[:], p["od_cmp_b2"][0, 1].partition_broadcast(NCMP))
        for i in range(2):
            small(b2k[i * HD:(i + 1) * HD, :], p["od_cmp_b2"][0, 0].rearrange("(d o) -> d o", o=1))
            small(w2c[:, :, i, :], p["od_cmp_w2"][0, 0].rearrange("(k q) d -> q k d", q=P))
        small(w2c[:, :, 2, :], p["od_cmp_w2"][0, 1].rearrange("(k q) d -> q k d", q=P))
        assert ndma[0] == NSMALL, ndma[0]

        act.wait_ge(s["cols_ready"], 3)
        a.activation(cact[:], cols[:, COL["c"]:COL["c"] + 16], ACT.Silu).then_inc(s["cact_ready"], 1)

        def trans_out(name, op):
            for k in range(TRANS[name], TRANS_END[name]):
                if k % 2 == 0:
                    act.wait_ge(s["tr_ready"], k + 1)
                    op(k - TRANS[name], B[4]).then_inc(s["tr_act"], 1)

        def modulated(shift, scale):
            def op(j, bank):
                for i in range(2):
                    c = 2 * j + i
                    ins = a.activation(hT[:, c, :], bank[:, i * T:(i + 1) * T], ACT.Identity,
                                       bias=modc[:, shift, c:c + 1], scale=modc[:, scale, c:c + 1])
                return ins
            return op

        def chunks_to(dst, c0=0):
            def op(j, bank):
                return a.copy(dst[:, c0 + 2 * j:c0 + 2 * j + 2, :], bank[:])
            return op

        def proj_out(name, j, op, n=None):
            tile_ready(act, TILE[name] + j if n is None else n)
            m = PROJ[name] + j
            op(j, B[2 * (m % 2)], B[2 * (m % 2) + 1]).then_inc(s["proj_act"], 1)

        def to_pb(j, b0, b1):
            return a.copy(pb[:, 0, 512 * j:512 * (j + 1)], b0[:])

        def attention(name):
            items = ITEMS[name]
            pending = []
            for t in range(len(items) + 3):
                if t < len(items) and items[t]["soft"] is not None:
                    u = items[t]["soft"]
                    act.wait_ge(s["max_ready"], u + 1)
                    if u >= 2:
                        if READER[u - 2] is None:
                            act.wait_ge(s["p_ready"], u)
                        else:
                            act.wait_ge(s["tr_ready"], READER[u - 2] + 1)
                    b = u % 2
                    for q in range(2):
                        sl = slice(0, P) if q == 0 else slice(P, 384)
                        ins = a.activation(Pm[:, b, sl], S_sb[:, b, sl], ACT.Exp, bias=nmx[:, b, q:q + 1],
                                           accum_out=rs[:, b, q:q + 1])
                    ins.then_inc(s["exp_done"], 1)
                if 0 <= t - 2 < len(items):
                    it = items[t - 2]
                    if it["tr"] is not None and it["tr"] % 2 == 0:
                        evacuate_p(act, it, a.copy, "tr_act")
                if 0 <= t - 3 < len(items):
                    it = items[t - 3]
                    if it["tr"] is not None and it["evac"] is not None:
                        act.wait_ge(s["pv_done"], it["pvn"] + 1)
                        a.copy(it["evac"][0], it["evac"][1]).then_inc(s["ot_out"], 1)

        def moe_act(name):
            d = MOE[name]
            n0, U, base = TILE[name], d["U"], d["silu"]

            def unit(u, par):
                i0 = isinstance(u, int)
                for b in range(2):
                    n = n0 if (i0 and u == 0) else 3 * u + (n0 - 1)
                    first_tile = b if name != "moe2" else 0
                    act.wait_ge(tile_used, n + (first_tile + 1))
                    if b == 0 and not (i0 and u < 2):
                        act.wait_ge(s["hid_done"], u + (d["hid"] - 1))
                    a.activation(silub[par][:, 2 * b:2 * b + 2, :], B[4 + b][:], ACT.Silu).then_inc(s["silu_done"], 1)
            unit(0, 0)
            unit(1, 1)
            with act.Fori(1, U // 2) as i:
                unit(2 * i, 0)
                unit(2 * i + 1, 1)

        trans_out("h0", modulated(0, 1))
        for j in range(6):
            proj_out("evin", j, to_pb)
        trans_out("qk0", lambda j, bank: a.copy(A[:, 2 * j:2 * j + 2, :], bank[:]))
        act.wait_ge(s["lam_sums"], 1)
        a.activation(lam[:, 2:4], lam[:, 0:2], ACT.Exp).then_inc(s["lam_exp"], 1)
        attention("att0")
        trans_out("ob", lambda j, bank: a.activation(OT[:, 4 + 2 * j:6 + 2 * j, :], bank[:], ACT.Copy, scale=subc[:, 0:1]))
        trans_out("h1", modulated(2, 3))
        routing_exp(act, "moe0")
        moe_act("moe0")
        act.wait_ge(s["moe_added"], 1)
        act.dma_start(gate1[:], p["ada_b"][1, 2048:3072].partition_broadcast(P)).then_inc(s["gate_bias"], 16)
        act.dma_start(gate2[:], p["ada_b"][1, 5120:6144].partition_broadcast(P)).then_inc(s["gate_bias"], 16)
        act.dma_start(b1c, p["od_cmp_b1"][0].partition_broadcast(60)).then_inc(s["b1_loaded"], 16)
        trans_out("h2", modulated(0, 1))

        def odd_out(j, b0, b1):
            if j < 2:
                return a.copy(pb[:, 0, 512 * j:512 * (j + 1)], b0[:])
            return odd_kv(a.copy, j, 0, b0)
        for j in range(5):
            proj_out("odin", j, odd_out)
        act.wait_ge(s["tail_ready"], 1)
        m = PROJ["odin"] + 5
        a.activation(gts[:, 0, :], B[2 * (m % 2)][:, 0:48], ACT.Sigmoid)
        a.activation(gts[:, 1, :], B[2 * (m % 2) + 1][:, 0:48], ACT.Sigmoid).then_inc(s["proj_act"], 1)
        trans_out("qkv1", lambda j, bank: a.copy(A[:, 2 * j:2 * j + 2, :], bank[:]))
        for j in range(2):
            act.wait_ge(s["hidden_biased"], j + 1)
            a.activation(cmph[:, j, :], cmph[:, j, :], GELU).then_inc(s["hidden_done"], 1)
        trans_out("cmph", lambda j, bank: a.copy(hidT_c, bank[:, 0:240]))
        act.wait_ge(s["kcmp_ready"], 1)
        a.activation(kcmpT[:], B[6][:, 0:60], ACT.Identity, bias=b2k[:, 0:1]).then_inc(s["kcmp_out"], 1)
        act.wait_ge(s["cscore_shifted"], 1)
        a.activation(pc, pc, ACT.Exp).then_inc(s["cscore_exp"], 1)
        attention("att1")
        act.wait_ge(s["proj_dve"], PROJ_DVE[PROJ["odout"] + 1])
        act.dma_start(rowp[:, 0, :], p["final_g"].partition_broadcast(P)).then_inc(s["rows_param"], 16)
        trans_out("h3", modulated(2, 3))
        routing_exp(act, "moe1")
        moe_act("moe1")
        act.wait_ge(s["moe_added"], 2)
        act.dma_start(gate1[:], p["b_mod_2"][0, 2048:3072].partition_broadcast(P)).then_inc(s["gate_bias"], 16)
        act.dma_start(gate2[:], p["b_mod_2"][0, 5120:6144].partition_broadcast(P)).then_inc(s["gate_bias"], 16)
        trans_out("h4", modulated(0, 1))
        act.wait_ge(s["dt_abs"], 1)
        a.activation(dts[:, 1], dts[:, 1], ACT.Exp).then_inc(s["dt_exp"], 1)
        act.wait_ge(s["dt_exp"], 1)
        a.activation(dts[:, 2], dts[:, 1], ACT.Ln, bias=1.0).then_inc(s["dt_ln"], 1)
        a.activation(cs[:, 3, 0:16], alog[:], ACT.Exp).then_inc(s["alog_exp"], 1)
        act.wait_ge(s["xT_padded"], 1)
        for j in range(4):
            proj_out("xbc", j, lambda j, b0, b1: a.copy(
                xT[:, 4 * j:4 * j + 2, 3:259], b0[:].rearrange("p (c t) -> p c t", t=T)))
        act.wait_ge(s["cs_ready"], 1)
        a.activation(cs[:, 1, :], B[7][:, 32:64], ACT.Exp)
        a.activation(cs[:, 2, :], B[7][:, 0:32], ACT.Exp)
        a.copy(cs[:, 0, :], B[7][:, 0:32]).then_inc(s["cs_out"], 1)
        for cc in range(16):
            act.wait_ge(s["conv_done"], cc + 1)
            a.activation(xT[:, cc, 3:259], tmp[:, cc % 2, 0:T], ACT.Silu).then_inc(s["conv_act"], 1)
        trans_out("xs", lambda j, bank: a.copy(pb[:, j // 2, 512 * (j % 2):512 * (j % 2) + 512], bank[:]))
        trans_out("btok", lambda j, bank: a.copy(Btok, bank[:]))
        for g in range(4):
            act.wait_ge(s["state_ready"], g + 1)
            a.copy(stT[:, 256 * g:256 * (g + 1)], B[2 + g % 2][:, 0:256]).then_inc(s["state_out"], 1)
        for q in range(8):
            act.wait_ge(s["seg_shifted"], q + 1)
            a.activation(mt[q % 2], mt[q % 2], ACT.Exp).then_inc(s["decay_done"], 1)
        act.wait_ge(s["xh_used"], 1)

        def silu_z(j, b0, b1):
            a.activation(pb[:, 0, 512 * j:512 * j + 512], b0[:], ACT.Silu)
            return a.activation(pb[:, 1, 512 * j:512 * j + 512], b1[:], ACT.Silu)
        for j in range(2):
            proj_out("z", j, silu_z)

        def gated_out(j, bank):
            for i in range(2):
                c = 2 * j + i
                ins = a.activation(OT[:, c, :], bank[:, i * T:(i + 1) * T], ACT.Copy,
                                   scale=col("ssd_norm_w_2", c))
            return ins
        trans_out("gated", gated_out)
        for j in range(2):
            proj_out("ssdo", j, lambda j, b0, b1: a.copy(pb[:, 0, 2048 + 512 * j:2560 + 512 * j], b0[:]))
        for j in range(3):
            proj_out("qkv", j, to_pb)
        trans_out("qk2", lambda j, bank: a.copy(A[:, 2 * j:2 * j + 2, :], bank[:]))
        attention("att2")
        for j in range(2):
            proj_out("atto", j, to_pb, n=TILE["atto"])

        def sigmoid_gate(j, b0, b1):
            if j < 2:
                dst = [pb[:, tt, 1024 + 512 * j:1536 + 512 * j] for tt in range(TT)]
            else:
                dst = [satt[:, tt, 512 * (j - 2):512 * (j - 1)] for tt in range(TT)]
            a.activation(dst[0], b0[:], ACT.Sigmoid)
            return a.activation(dst[1], b1[:], ACT.Sigmoid)
        for j in range(4):
            proj_out("gates", j, sigmoid_gate)
        trans_out("merged", lambda j, bank: a.copy(OT[:, 2 * j:2 * j + 2, :], bank[:]))
        act.wait_ge(s["final_scaled"], 1)
        act.dma_start(rowp[:, 0, :], p["ln1_g_2"][0].partition_broadcast(P)).then_inc(s["rows_param"], 16)
        act.dma_start(rowp[:, 1, :], p["ln1_b_2"][0].partition_broadcast(P)).then_inc(s["rows_param"], 16)
        trans_out("h5", modulated(2, 3))
        act.wait_ge(s["ln_scaled"], 1)
        act.dma_start(rowp[:, 0, :], p["ln2_g_2"][0].partition_broadcast(P)).then_inc(s["rows_param"], 16)
        act.dma_start(rowp[:, 1, :], p["ln2_b_2"][0].partition_broadcast(P)).then_inc(s["rows_param"], 16)
        routing_exp(act, "moe2")
        moe_act("moe2")

    @block.vector
    def _(dve):
        v = nc.vector
        steps = [0]

        def step(ins):
            steps[0] += 1
            ins.then_inc(s["dve_step"], 1)
            dve.wait_ge(s["dve_step"], steps[0])

        def trans_out(name, op):
            for k in range(TRANS[name], TRANS_END[name]):
                if k % 2 == 1:
                    dve.wait_ge(s["tr_ready"], k + 1)
                    op(k - TRANS[name], B[5]).then_inc(s["tr_dve"], 1)

        def modulated(shift, scale):
            def op(j, bank):
                for i in range(2):
                    c = 2 * j + i
                    ins = v.tensor_scalar(hT[:, c, :], bank[:, i * T:(i + 1) * T], modc[:, scale, c:c + 1],
                                          modc[:, shift, c:c + 1], ALU.mult, ALU.add)
                return ins
            return op

        def proj_out(name, j, op, n=None):
            tile_ready(dve, TILE[name] + j if n is None else n)
            m = PROJ[name] + j
            op(j, B[2 * (m % 2)], B[2 * (m % 2) + 1]).then_inc(s["proj_dve"], 1)

        def to_pb(j, b0, b1):
            return v.tensor_copy(pb[:, 1, 512 * j:512 * (j + 1)], b1[:])

        evals = [0]

        def scale_factor(src, eps, center):
            for tt in range(TT):
                for h in range(2):
                    ins = v.bn_stats(stats[:, tt, h, :], src[:, tt, 512 * h:512 * (h + 1)])
            step(ins)
            for tt in range(TT):
                ins = v.bn_aggr(mv[:, tt, :], stats[:, tt].rearrange("p a b -> p (a b)"))
            step(ins)
            if center:
                var = mv[:, :, 1]
            else:
                step(v.tensor_tensor(rstd[:], mv[:, :, 0], mv[:, :, 0], ALU.mult))
                step(v.tensor_tensor(rstd[:], rstd[:], mv[:, :, 1], ALU.add))
                var = rstd[:]
            v.tensor_scalar(rstd[:], var, eps, None, ALU.add).then_inc(s["var_ready"], 1)
            evals[0] += 1
            dve.wait_ge(s["pow_done"], evals[0])

        def normalise(dst, src, eps, center):
            scale_factor(src, eps, center)
            for tt in range(TT):
                if center:
                    ins = v.tensor_scalar(dst[:, tt, :], src[:, tt, :], mv[:, tt, 0:1], rstd[:, tt:tt + 1],
                                          ALU.subtract, ALU.mult)
                else:
                    ins = v.tensor_scalar(dst[:, tt, :], src[:, tt, :], rstd[:, tt:tt + 1], None, ALU.mult)
            return ins

        def modulation(i, name, bias, bias0, gain, gain0, one):
            for j in range(12):
                kind, half = j // 2, j % 2
                tile_ready(dve, TILE[name] + j)
                bank = B[j % 4]
                if kind in (2, 5):
                    gate = gate1 if kind == 2 else gate2
                    if j == 4:
                        dve.wait_ge(s["gate_bias"], 32 * (i + 1))
                    gs = gate[:, 512 * half:512 * (half + 1)]
                    v.scalar_tensor_tensor(gs, bank[:], one, gs, ALU.add, ALU.add).then_inc(s["ada_out"], 1)
                    continue
                dst = modc[:, {0: 0, 1: 1, 3: 2, 4: 3}[kind], 4 * half:4 * half + 4]
                t = tmp[:, j % 2, :].rearrange("p (a b) -> p a b", b=P)
                v.tensor_tensor(t, bank[:].rearrange("p (a b) -> p a b", b=P), bc(ident[:], 1, [P, 4, P]),
                                ALU.mult).then_inc(s["ada_out"], 1)
                dve.wait_ge(s["ada_out"], 12 * i + j + 1)
                step(v.tensor_reduce(dst, t, AX.X, ALU.add))
                step(v.tensor_tensor(dst, dst, col(bias, bias0 + 8 * kind + 4 * half, 4), ALU.add))
                if kind in (1, 4):
                    if gain is None:
                        step(v.tensor_scalar(dst, dst, 1.0, None, ALU.add))
                    else:
                        step(v.scalar_tensor_tensor(dst, dst, 1.0,
                                                    col(gain[kind // 4], gain0 + 4 * half, 4), ALU.add, ALU.mult))
            v.memset(mark[:, 1:2], 0.0).then_inc(s["mod_ready"], 1)

        def attention(name):
            items = ITEMS[name]
            for t in range(len(items) + 3):
                if t < len(items) and items[t]["soft"] is not None:
                    u = items[t]["soft"]
                    b = u % 2
                    dve.wait_ge(s["s_ready"], u + 1)
                    if u >= 2:
                        dve.wait_ge(s["exp_done"], u - 1)
                    v.scalar_tensor_tensor(S_sb[:, b, :], B[6 + b][:, 0:384], SCALE, mask384[:], ALU.mult,
                                           ALU.add).then_inc(s["s_masked"], 1)
                    dve.wait_ge(s["s_masked"], u + 1)
                    v.tensor_reduce(nmx[:, b, 0:1], S_sb[:, b, 0:P], AX.X, ALU.max, negate=True)
                    v.tensor_reduce(nmx[:, b, 1:2], S_sb[:, b, P:384], AX.X, ALU.max,
                                    negate=True).then_inc(s["max_ready"], 1)
                if 0 <= t - 1 < len(items) and items[t - 1]["soft"] is not None:
                    it = items[t - 1]
                    u = it["soft"]
                    b = u % 2
                    dve.wait_ge(s["exp_done"], u + 1)
                    step(v.reciprocal(rr[:, b, :], rs[:, b, :]))
                    if it["gate"] is not None:
                        h, branch = it["gate"]
                        step(v.tensor_tensor(rr[:, b, :], rr[:, b, :], gts[:, :, 3 * h + branch], ALU.mult))
                    if it["kind"] == "map1":
                        step(v.tensor_scalar(rr[:, b, :], rr[:, b, :], lam[:, 4:5], None, ALU.mult))
                    for q in range(2):
                        sl = slice(0, P) if q == 0 else slice(P, 384)
                        if it["kind"] == "map1":
                            ins = v.scalar_tensor_tensor(Pm[:, b, sl], Pm[:, b, sl], rr[:, b, q:q + 1],
                                                         Pm[:, 1 - b, sl], ALU.mult, ALU.add)
                        else:
                            ins = v.tensor_scalar(Pm[:, b, sl], Pm[:, b, sl], rr[:, b, q:q + 1], None, ALU.mult)
                    ins.then_inc(s["p_ready"], 1)
                    if it["kind"] == "map0":
                        dve.wait_ge(s["p_ready"], u + 1)
                if 0 <= t - 2 < len(items):
                    it = items[t - 2]
                    if it["tr"] is not None and it["tr"] % 2 == 1:
                        evacuate_p(dve, it, v.tensor_copy, "tr_dve")

        def residual(name, gate, alpha=None):
            for j in range(2):
                def op(j, b0, b1):
                    gs = gate[:, 512 * j:512 * (j + 1)]
                    for tt, bank in enumerate((b0, b1)):
                        step(v.tensor_tensor(tmp[:, tt, :], bank[:], gs, ALU.mult))
                        xs = x[:, tt, 512 * j:512 * (j + 1)]
                        if alpha is None:
                            ins = v.tensor_tensor(xs, xs, tmp[:, tt, :], ALU.add)
                        else:
                            ins = v.scalar_tensor_tensor(xs, xs, alpha, tmp[:, tt, :], ALU.mult, ALU.add)
                    return ins
                proj_out(name, j, op)
            dve.wait_ge(s["proj_dve"], PROJ_DVE[PROJ[name] + 1])

        def first_of_max(dst, vals, m, n):
            step(v.tensor_reduce(m, vals, AX.X, ALU.max))
            step(v.tensor_tensor(dst, vals, bc(m, 3, [P, TT, n, 4]), ALU.is_equal))
            step(v.tensor_tensor(dst, dst, first[:].unsqueeze(1).unsqueeze(1).broadcast_to([P, TT, n, 4]), ALU.mult))
            step(v.tensor_reduce(rt[:, :, 15, 0:n], dst, AX.X, ALU.max))
            step(v.tensor_tensor(dst, dst, bc(rt[:, :, 15, 0:n], 3, [P, TT, n, 4]), ALU.is_equal))

        def routing(name):
            i = MOE[name]["idx"]
            dve.wait_ge(s["router_ready"], i + 1)
            lg = rt[:, :, 8:13, :]
            for tt in range(TT):
                ins = v.tensor_tensor(lg[:, tt].rearrange("p a b -> p (a b)"), B[7][:, 32 * tt:32 * tt + 20],
                                      br[i][:], ALU.add)
            ins.then_inc(s["router_out"], 1)
            dve.wait_ge(s["router_out"], i + 1)
            m1, m2 = rt[:, :, 7, 0:1], rt[:, :, 7, 1:2]
            gl = rt[:, :, 8:9, :]
            goh = rt[:, :, 2:3, :]
            first_of_max(goh, gl, m1, 1)
            step(v.tensor_tensor(rt[:, :, 0:1, :], gl, bc(m1, 3, [P, TT, 1, 4]), ALU.subtract))
            prod = rt[:, :, 9:13, :]
            step(v.tensor_tensor(prod, prod, bc(rt[:, :, 2, :], 3, [P, TT, 4, 4]), ALU.mult))
            el = rt[:, :, 3:4, :]
            step(v.tensor_reduce(rt[:, :, 3, :], prod.rearrange("p t g e -> p t e g"), AX.X, ALU.add))
            first_of_max(rt[:, :, 4:5, :], el, m1, 1)
            for tt in range(TT):
                ins = v.scalar_tensor_tensor(rt[:, tt, 6, :], rt[:, tt, 4, :], NEG, rt[:, tt, 3, :], ALU.mult, ALU.add)
            step(ins)
            first_of_max(rt[:, :, 5:6, :], rt[:, :, 6:7, :], m2, 1)
            step(v.memset(rt[:, :, 1, :], 0.0))
            step(v.tensor_tensor(rt[:, :, 1, 0:1], m2, m1, ALU.subtract))
            v.memset(mark[:, 1:2], 0.0).then_inc(s["route_shifted"], 1)
            dve.wait_ge(s["route_exp"], i + 1)
            step(v.tensor_reduce(rt[:, :, 7, 0:1], rt[:, :, 0:1, :], AX.X, ALU.add))
            step(v.tensor_scalar(rt[:, :, 7, 1:2], rt[:, :, 1, 0:1], 1.0, None, ALU.add))
            step(v.reciprocal(rt[:, :, 7, 0:2], rt[:, :, 7, 0:2]))
            step(v.tensor_tensor(rt[:, :, 7, 2:3], rt[:, :, 7, 0:1], rt[:, :, 7, 1:2], ALU.mult))
            step(v.tensor_tensor(rt[:, :, 7, 3:4], rt[:, :, 7, 2:3], rt[:, :, 1, 0:1], ALU.mult))
            step(v.tensor_tensor(rt[:, :, 4, :], rt[:, :, 4, :], rt[:, :, 7, 2:3].broadcast_to([P, TT, 4]), ALU.mult))
            step(v.tensor_tensor(rt[:, :, 5, :], rt[:, :, 5, :], rt[:, :, 7, 3:4].broadcast_to([P, TT, 4]), ALU.mult))
            step(v.tensor_tensor(rt[:, :, 4, :], rt[:, :, 4, :], rt[:, :, 5, :], ALU.add))
            v.tensor_tensor(comb[:].rearrange("p t (g e) -> p t g e", g=4), bc(rt[:, :, 2, :], 3, [P, TT, 4, 4]),
                            bc(rt[:, :, 4, :], 2, [P, TT, 4, 4]), ALU.mult).then_inc(s["comb_ready"], 1)
            for j in range(8):
                if j % 2 == 1:
                    dve.wait_ge(s["combT_ready"], 8 * i + j + 1)
                    v.tensor_copy(combT[:, 2 * j:2 * j + 2, :], B[j % 4][:]).then_inc(s["combT_dve"], 1)
            dve.wait_ge(s["combT_act"], 4 * (i + 1))
            dve.wait_ge(s["combT_dve"], 4 * (i + 1))

        def experts(name, gate, alpha=None):
            d = MOE[name]
            n0, U = TILE[name], d["U"]
            large = name == "moe2"

            def unit(u, par):
                i0 = isinstance(u, int)
                n = n0 if (i0 and u == 0) else 3 * u + (n0 - 1)
                for b in range(2):
                    dve.wait_ge(tile_used, n + (2 if large else b + 1))
                    dve.wait_ge(s["silu_done"], 2 * u + (d["silu"] + b + 1))
                    if b == 0 and not (i0 and u < 2):
                        dve.wait_ge(tile_used, 3 * u + (n0 - 1))
                    sil = silub[par][:, 2 * b:2 * b + 2, :]
                    v.tensor_tensor(sil, sil, B[6 + b][:].rearrange("p (c t) -> p c t", t=T),
                                    ALU.mult).then_inc(s["up_done"], 1)
                    dve.wait_ge(s["up_done"], 2 * u + (d["silu"] + b + 1))
                    e = u if large else 2 * u + b
                    w = combT[:, e, :].unsqueeze(1) if isinstance(e, int) else combT[:, bass.ds(e, 1), :]
                    ins = v.tensor_tensor(hidb[par][:, 2 * b:2 * b + 2, :], sil, w.broadcast_to([P, 2, T]), ALU.mult)
                ins.then_inc(s["hid_done"], 1)
            unit(0, 0)
            unit(1, 1)
            with dve.Fori(1, U // 2) as i:
                unit(2 * i, 0)
                unit(2 * i + 1, 1)
            tile_ready(dve, n0 + 3 * U - 1)
            for tt in range(TT):
                for h in range(2):
                    step(v.tensor_tensor(tmp[:, h, :], B[2 * tt + h][:], gate[:, 512 * h:512 * (h + 1)], ALU.mult))
                    xs = x[:, tt, 512 * h:512 * (h + 1)]
                    if alpha is None:
                        ins = v.tensor_tensor(xs, xs, tmp[:, h, :], ALU.add)
                    else:
                        ins = v.scalar_tensor_tensor(xs, xs, alpha, tmp[:, h, :], ALU.mult, ALU.add)
            ins.then_inc(s["moe_added"], 1)
            dve.wait_ge(s["moe_added"], d["idx"] + 1)

        def gain_bias(rows, bias):
            dve.wait_ge(s["rows_param"], 16 * rows)
            for tt in range(TT):
                ins = v.tensor_tensor(x[:, tt, :], x[:, tt, :], rowp[:, 0, :], ALU.mult)
            step(ins)
            if bias:
                for tt in range(TT):
                    ins = v.tensor_tensor(x[:, tt, :], x[:, tt, :], rowp[:, 1, :], ALU.add)
                step(ins)

        dve.wait_ge(s["constants"], 1)
        for t in range(3):
            dve.wait_ge(s["cols_transposed"], t + 1)
            n = (P, P, 57)[t]
            v.tensor_copy(cols[:, P * t:P * t + n], B[4 + t][:, 0:n]).then_inc(s["cols_ready"], 1)

        dve.wait_ge(s["x_loaded"], 16)
        normalise(pb[:, :, 0:D], x[:], RMS_EPS, False).then_inc(s["xn_ready"], 1)
        dve.wait_ge(s["small_loads"], 16 * NSMALL)
        step(v.tensor_tensor(lamrow[:, 0:2, :], lamrow[:, 0::2, :], lamrow[:, 1::2, :], ALU.mult))
        v.tensor_reduce(lam[:, 0:2], lamrow[:, 0:2, :], AX.X, ALU.add).then_inc(s["lam_sums"], 1)
        dve.wait_ge(s["cols_ready"], 3)
        v.tensor_scalar(subc[:], col("ev_subln_g"), 1.0 - LAMBDA_INIT, None, ALU.mult)
        modulation(0, "ada0", "ada_b", 0, ("norm1_g", "norm2_g"), 0, 0.0)
        trans_out("h0", modulated(0, 1))
        for j in range(6):
            proj_out("evin", j, to_pb)
        trans_out("qk0", lambda j, bank: v.tensor_copy(A[:, 2 * j:2 * j + 2, :], bank[:]))
        dve.wait_ge(s["lam_exp"], 1)
        step(v.tensor_tensor(lam[:, 4:5], lam[:, 3:4], lam[:, 2:3], ALU.subtract))
        step(v.tensor_scalar(lam[:, 4:5], lam[:, 4:5], LAMBDA_INIT, None, ALU.subtract))
        attention("att0")
        dve.wait_ge(s["ot_out"], 8)
        ob = pb[:, :, 0:512]
        step(v.tensor_tensor(tmp[:], ob, ob, ALU.mult))
        step(v.tensor_reduce(obs[:].rearrange("p (a h) -> p a h", a=TT),
                             tmp[:].rearrange("p a (h e) -> p a h e", e=P), AX.X, ALU.add))
        v.tensor_scalar(obs[:], obs[:], 1.0 / P, RMS_EPS, ALU.mult, ALU.add).then_inc(s["var_ready"], 1)
        evals[0] += 1
        dve.wait_ge(s["pow_done"], evals[0])
        obh = ob.rearrange("p a (h e) -> p a h e", e=P)
        v.tensor_tensor(obh, obh, bc(obs[:].rearrange("p (a h) -> p a h", a=TT), 3, [P, TT, 4, P]),
                        ALU.mult).then_inc(s["ob_ready"], 1)
        trans_out("ob", lambda j, bank: v.tensor_scalar(OT[:, 4 + 2 * j:6 + 2 * j, :],
                                                        bank[:].rearrange("p (c t) -> p c t", t=T),
                                                        subc[:, 0:1], None, ALU.mult))
        residual("evout", gate1)
        normalise(pb[:, :, 0:D], x[:], RMS_EPS, False).then_inc(s["xn_ready"], 1)
        trans_out("h1", modulated(2, 3))
        routing("moe0")
        experts("moe0", gate2)
        normalise(pb[:, :, 0:D], x[:], RMS_EPS, False).then_inc(s["xn_ready"], 1)
        modulation(1, "ada1", "ada_b", 48, ("norm1_g", "norm2_g"), 8, 0.0)
        trans_out("h2", modulated(0, 1))

        def odd_out(j, b0, b1):
            if j < 2:
                return v.tensor_copy(pb[:, 1, 512 * j:512 * (j + 1)], b1[:])
            return odd_kv(v.tensor_copy, j, 1, b1)
        for j in range(5):
            proj_out("odin", j, odd_out)
        v.memset(mark[:, 1:2], 0.0).then_inc(s["proj_dve"], 1)
        trans_out("qkv1", lambda j, bank: v.tensor_copy(A[:, 2 * j:2 * j + 2, :], bank[:]))
        stage_transposed(dve, "qkv1")
        for kv in range(2):
            for par in range(2):
                rows = slice(par * HD, (par + 1) * HD)
                for g in range(4):
                    src = A[rows, 8 + 4 * kv + g, :]
                    for half in range(2):
                        sv = src[:, 16 * half:16 * half + 16 * NCMP].rearrange(
                            "p (n l e) -> p e l n", e=2, l=8)[:, par]
                        pos = bc(cols[rows, COL["pos"] + 16 * kv + 8 * half:COL["pos"] + 16 * kv + 8 * half + 8],
                                 2, [HD, 8, NCMP])
                        ins = v.tensor_tensor(cmpB[rows, kv, 8 * half:8 * half + 8, g, :], sv, pos, ALU.add)
            ins.then_inc(s["blocks_ready"], 1)
        dve.wait_ge(s["b1_loaded"], 16)
        for kv in range(2):
            tile_ready(dve, TILE["cmp"] + kv)
            v.tensor_tensor(cmph[:, kv, :], B[kv][0:60, 0:256], b1c[:, kv, :], ALU.add).then_inc(s["hidden_biased"], 1)
        dve.wait_ge(s["vcmp_ready"], 1)
        v.tensor_tensor(vcmp[:], B[7][0:NCMP, 0:256].rearrange("p (g d) -> p g d", g=4),
                        bc(b2v[:], 1, [NCMP, 4, HD]), ALU.add).then_inc(s["vcmp_out"], 1)
        dve.wait_ge(s["cscore_ready"], 1)
        pc3 = pc.rearrange("p (b n) -> p b n", n=NCMP)
        for tt in range(TT):
            for par in range(2):
                ins = v.scalar_tensor_tensor(
                    pc3[:, 16 * tt + par:16 * tt + 16:2],
                    B[6 + par][:, 120 * tt:120 * tt + 120].rearrange("p (h n) -> p h n", n=NCMP), SCALE,
                    bc(maskc[:, tt, :], 1, [P, 8, NCMP]), ALU.mult, ALU.add)
        ins.then_inc(s["cscore_out"], 1)
        dve.wait_ge(s["cscore_out"], 1)
        step(v.tensor_reduce(cs[:, 0, :], pc3, AX.X, ALU.max))
        v.tensor_tensor(pc3, pc3, bc(cs[:, 0, :], 2, [P, 32, NCMP]), ALU.subtract).then_inc(s["cscore_shifted"], 1)
        dve.wait_ge(s["cscore_exp"], 1)
        step(v.tensor_reduce(cs[:, 1, :], pc3, AX.X, ALU.add))
        step(v.reciprocal(cs[:, 1, :], cs[:, 1, :]))
        for tt in range(TT):
            ins = v.scalar_tensor_tensor(cs[:, 2, 16 * tt:16 * tt + 16], gts[:, tt, 0::3], cmp_live[:, tt:tt + 1],
                                         cs[:, 1, 16 * tt:16 * tt + 16], ALU.mult, ALU.mult)
        step(ins)
        v.tensor_tensor(pc3, pc3, bc(cs[:, 2, :], 2, [P, 32, NCMP]), ALU.mult).then_inc(s["pc_ready"], 1)
        attention("att1")
        residual("odout", gate1)
        normalise(pb[:, :, 0:D], x[:], RMS_EPS, False).then_inc(s["xn_ready"], 1)
        trans_out("h3", modulated(2, 3))
        routing("moe1")
        experts("moe1", gate2)
        step(normalise(x, x, RMS_EPS, False))
        gain_bias(1, False)
        v.memset(mark[:, 1:2], 0.0).then_inc(s["final_scaled"], 1)
        normalise(pb[:, :, 0:D], x[:], LN_EPS, True).then_inc(s["xn_ready"], 1)
        modulation(2, "ada2", "b_mod_2", 0, None, 0, 1.0)
        trans_out("h4", modulated(0, 1))
        dve.wait_ge(s["dt_ready"], 1)
        for tt in range(TT):
            ins = v.tensor_tensor(dts[:, 0, tt, :], B[6][:, 32 * tt:32 * tt + 24], bdf[:], ALU.add)
        step(ins)
        step(v.tensor_scalar(dts[:, 0, :, 16:24], dts[:, 0, :, 16:24], -1.0, None, ALU.mult))
        step(v.scalar_tensor_tensor(dts[:, 1], dts[:, 0], -1.0, dts[:, 0], ALU.mult, ALU.max))
        v.tensor_scalar(dts[:, 1], dts[:, 1], -1.0, None, ALU.mult).then_inc(s["dt_abs"], 1)
        v.memset(xT[:, :, 0:3], 0.0).then_inc(s["xT_padded"], 1)
        dve.wait_ge(s["dt_ln"], 1)
        step(v.scalar_tensor_tensor(dts[:, 3], dts[:, 0], 0.0, dts[:, 2], ALU.max, ALU.add))
        dve.wait_ge(s["alog_exp"], 1)
        for tt in range(TT):
            v.scalar_tensor_tensor(dts[:, 4, tt, 0:16], dts[:, 3, tt, 0:16], -1.0, cs[:, 3, 0:16],
                                   ALU.mult, ALU.mult)
        v.tensor_scalar(dts[:, 5, :, 16:24], dts[:, 3, :, 16:24], 1.0 / SCALE, None,
                        ALU.mult).then_inc(s["a_ready"], 1)
        for j in range(4):
            proj_out("xbc", j, lambda j, b0, b1: v.tensor_copy(
                xT[:, 4 * j + 2:4 * j + 4, 3:259], b1[:].rearrange("p (c t) -> p c t", t=T)))
        proj_evacuated(dve, PROJ["xbc"] + 3)
        for cc in range(16):
            acc = tmp[:, cc % 2, 0:T]
            if cc >= 2:
                dve.wait_ge(s["conv_act"], cc - 1)
            step(v.tensor_scalar(acc, xT[:, cc, 3:259], col("conv_w_2", 48 + cc), col("conv_b_2", cc),
                                 ALU.mult, ALU.add))
            for k in (2, 1):
                step(v.scalar_tensor_tensor(acc, xT[:, cc, k:k + T], col("conv_w_2", 16 * k + cc), acc,
                                            ALU.mult, ALU.add))
            v.scalar_tensor_tensor(acc, xT[:, cc, 0:T], col("conv_w_2", cc), acc, ALU.mult,
                                   ALU.add).then_inc(s["conv_done"], 1)
        trans_out("xs", lambda j, bank: v.tensor_copy(pb[:, j // 2, 512 * (j % 2):512 * (j % 2) + 512], bank[:]))
        trans_out("btok", lambda j, bank: v.tensor_copy(Btok, bank[:]))
        stage_transposed(dve, "xs")
        dve.wait_ge(s["cs_out"], 1)
        for tt in range(TT):
            xh = pb[:, tt, 0:D].rearrange("p (h e) -> p h e", e=HD)
            v.tensor_tensor(pb[:, tt, 2 * D:3 * D].rearrange("p (h e) -> p h e", e=HD), xh,
                            bc(dsk[:], 2, [P, 16, HD]), ALU.mult)
            ins = v.tensor_tensor(pb[:, tt, D:2 * D].rearrange("p (h e) -> p h e", e=HD), xh,
                                  bc(dts[:, 3, tt, 0:16], 2, [P, 16, HD]), ALU.mult)
        ins.then_inc(s["xh_used"], 1)
        dve.wait_ge(s["xh_used"], 1)
        v.tensor_tensor(xdte.rearrange("p (h e) -> p h e", e=HD),
                        pb[:, 0, D:2 * D].rearrange("p (h e) -> p h e", e=HD),
                        bc(cs[:, 1, 0:16], 2, [P, 16, HD]), ALU.mult).then_inc(s["xdt_ready"], 1)
        for q in range(9):
            if q < 8:
                tt, g = q // 4, q % 4
                dve.wait_ge(s["seg_ready"], q + 1)
                m3 = mt[q % 2].rearrange("p (r l) -> p r l", r=4)
                if q >= 2:
                    dve.wait_ge(s["y_ready"], q - 1)
                v.tensor_tensor(m3, B[6 + q % 2][:].rearrange("p (r l) -> p r l", r=4),
                                bc(maskT[:], 1, [P, 4, P]), ALU.add).then_inc(s["seg_out"], 1)
                dve.wait_ge(s["seg_out"], q + 1)
                v.tensor_tensor(m3, m3, bc(cs[:, 0, 16 * tt + 4 * g:16 * tt + 4 * g + 4], 2, [P, 4, P]),
                                ALU.subtract).then_inc(s["seg_shifted"], 1)
            if q >= 1:
                r = q - 1
                tt, g = r // 4, r % 4
                ys = pb[:, tt, 2 * D + 256 * g:2 * D + 256 * (g + 1)]
                m3 = mt[r % 2].rearrange("p (r l) -> p r l", r=4)
                dve.wait_ge(s["decay_done"], r + 1)
                v.tensor_tensor(m3, m3, bc(B[r % 2][:, 0:P], 1, [P, 4, P]), ALU.mult).then_inc(s["m_ready"], 1)
                dve.wait_ge(s["y_ready"], r + 1)
                bank = B[2 + r % 2]
                step(v.tensor_tensor(ys, ys, bank[:, 0:256], ALU.add))
                if tt == 1:
                    step(v.tensor_tensor(tmp[:, 0, 0:256].rearrange("p (r e) -> p r e", e=HD),
                                         bank[:, 256:512].rearrange("p (r e) -> p r e", e=HD),
                                         bc(cs[:, 2, 16 + 4 * g:20 + 4 * g], 2, [P, 4, HD]), ALU.mult))
                    step(v.tensor_tensor(ys, ys, tmp[:, 0, 0:256], ALU.add))
                v.memset(mark[:, 1:2], 0.0).then_inc(s["y_out"], 1)
        yv = pb[:, :, 2 * D:3 * D]
        dve.wait_ge(s["proj_act"], PROJ_ACT[PROJ["z"] + 1])
        step(v.tensor_tensor(yv, yv, pb[:, :, 0:D], ALU.mult))
        normalise(yv, yv, LN_EPS, False).then_inc(s["gated_ready"], 1)

        def gated_out(j, bank):
            for i in range(2):
                c = 2 * j + i
                ins = v.tensor_scalar(OT[:, c, :], bank[:, i * T:(i + 1) * T], col("ssd_norm_w_2", c), None,
                                      ALU.mult)
            return ins
        trans_out("gated", gated_out)
        for j in range(2):
            proj_out("ssdo", j, lambda j, b0, b1: v.tensor_copy(pb[:, 1, 2048 + 512 * j:2560 + 512 * j], b1[:]))
        for j in range(3):
            proj_out("qkv", j, to_pb)
        trans_out("qk2", lambda j, bank: v.tensor_copy(A[:, 2 * j:2 * j + 2, :], bank[:]))
        attention("att2")
        for j in range(2):
            proj_out("atto", j, to_pb, n=TILE["atto"])
        proj_evacuated(dve, PROJ["gates"] + 3)
        mg = pb[:, :, D:2 * D]
        v.tensor_tensor(mg, mg, pb[:, :, 2 * D:3 * D], ALU.mult)
        step(v.tensor_tensor(satt, satt, pb[:, :, 0:D], ALU.mult))
        v.tensor_tensor(mg, mg, satt, ALU.add).then_inc(s["merged_ready"], 1)
        trans_out("merged", lambda j, bank: v.tensor_copy(OT[:, 2 * j:2 * j + 2, :], bank[:]))
        residual("wo", gate1, ALPHA)
        step(normalise(x, x, LN_EPS, True))
        gain_bias(3, True)
        v.memset(mark[:, 1:2], 0.0).then_inc(s["ln_scaled"], 1)
        normalise(pb[:, :, 0:D], x[:], LN_EPS, True).then_inc(s["xn_ready"], 1)
        trans_out("h5", modulated(2, 3))
        routing("moe2")
        experts("moe2", gate2, ALPHA)
        step(normalise(x, x, LN_EPS, True))
        gain_bias(5, True)
        v.memset(mark[:, 2:3], 0.0).then_inc(s["result"], 1)

    @block.tensor
    def _(pe):
        mm = nc.tensor.matmul

        def transposes(name, sources):
            for k in range(TRANS[name], TRANS_END[name]):
                if k >= 2:
                    trans_evacuated(pe, k - 2)
                for dst, src in sources(k - TRANS[name], B[4 + k % 2]):
                    n = src.shape[0]
                    ins = nc.tensor.transpose(dst, src, ident[0:n, 0:n])
                ins.then_inc(s["tr_ready"], 1)

        def from_tokens(src, column=lambda c: P * c):
            def sources(j, bank):
                return [(bank[:, i * T + tt * P:i * T + (tt + 1) * P],
                         src[:, tt, column(2 * j + i):column(2 * j + i) + P]) for i in range(2) for tt in range(TT)]
            return sources

        def landed_tile(n):
            pe.wait_ge(landed[n % NSLOT], LANDED[n])
            return ring[n % NSLOT][:].rearrange("p (c n) -> p c n", n=512)

        def bank_pair_free(m):
            if m >= 2:
                proj_evacuated(pe, m - 2)

        def project(name, tiles, lhs):
            for j in range(tiles):
                m = PROJ[name] + j
                w = landed_tile(TILE[name] + j)
                if j >= 2:
                    bank_pair_free(m)
                for tt in range(TT):
                    for c in range(C):
                        ins = mm(B[2 * (m % 2) + tt][:], lhs[:, c, tt * P:(tt + 1) * P], w[:, c, :],
                                 start=c == 0, stop=c == C - 1)
                ins.then_inc(tile_used, 1)

        def modulation(name, i, i0):
            for j in range(12):
                w = landed_tile(TILE[name] + j)
                if j >= 4:
                    pe.wait_ge(s["ada_out"], 12 * i + j - 3)
                for c in range(C):
                    ins = mm(B[j % 4][:], cact[:, i0 + c:i0 + c + 1].broadcast_to([P, P]), w[:, c, :],
                             start=c == 0, stop=c == C - 1)
                ins.then_inc(tile_used, 1)

        def attention(name):
            items = ITEMS[name]
            for t in range(len(items) + 2):
                if t < len(items) and items[t]["soft"] is not None:
                    it = items[t]
                    u = it["soft"]
                    bank = B[6 + u % 2]
                    if u >= 2:
                        pe.wait_ge(s["s_masked"], u - 1)
                    q, k, f = it["q"], it["k"], it["forget"]
                    ins = mm(bank[:, 0:P], q[:, 0:P], k[:, 0:P], start=True, stop=f is None)
                    if f is not None:
                        fb = [dts[:, 5, tt, 16 + f:17 + f].broadcast_to([P, P]) for tt in range(TT)]
                        mm(bank[:, 0:P], fb[0], tri, start=False, stop=True)
                    ins = mm(bank[:, P:384], q[:, P:T], k[:, 0:T], start=True, stop=f is None)
                    if f is not None:
                        mm(bank[:, P:384], fb[0], tri_one[:], start=False, stop=False)
                        ins = mm(bank[:, T:384], fb[1], tri, start=False, stop=True)
                    ins.then_inc(s["s_ready"], 1)
                if 0 <= t - 1 < len(items) and items[t - 1]["tr"] is not None:
                    it = items[t - 1]
                    k = it["tr"]
                    bank = B[4 + k % 2]
                    trans_evacuated(pe, k - 2)
                    if it["kind"] == "cmp":
                        pe.wait_ge(s["pc_ready"], 1)
                        for tt in range(TT):
                            src = pc[:, (16 * tt + it["h"]) * NCMP:(16 * tt + it["h"] + 1) * NCMP]
                            ins = nc.tensor.transpose(bank[0:NCMP, tt * P:(tt + 1) * P], src, ident[:])
                    else:
                        pe.wait_ge(s["p_ready"], it["soft"] + 1)
                        for j in range(3):
                            ins = nc.tensor.transpose(bank[:, j * P:(j + 1) * P],
                                                      Pm[:, it["soft"] % 2, j * P:(j + 1) * P], ident[:])
                    ins.then_inc(s["tr_ready"], 1)
                if 0 <= t - 2 < len(items) and items[t - 2]["tr"] is not None:
                    it = items[t - 2]
                    k = it["tr"]
                    trans_evacuated(pe, k)
                    if it["ot_first"] and it["ot"] >= 2:
                        pe.wait_ge(s["ot_out"], it["ot"] - 1)
                    for dst, lhs, rhs, start, stop in it["pv"](PT[:, k % 2, :]):
                        ins = mm(dst, lhs, rhs, start=start, stop=stop)
                    ins.then_inc(s["pv_done"], 1)

        def experts(name, hname):
            d = MOE[name]
            i, n0, U = d["idx"], TILE[name], d["U"]
            large = name == "moe2"
            stage_transposed(pe, hname)
            if i == 0:
                pe.wait_ge(s["small_loads"], 16 * NSMALL)
            for tt in range(TT):
                for c in range(C):
                    ins = mm(B[7][:, 32 * tt:32 * tt + 20], hT[:, c, tt * P:(tt + 1) * P], wr[i][:, c, :],
                             start=c == 0, stop=c == C - 1)
            ins.then_inc(s["router_ready"], 1)

            def landed_at(n_static, u_offset, u):
                slot = n_static % NSLOT
                if isinstance(u, int):
                    pe.wait_ge(landed[slot], LANDED[n_static + 3 * (u - u_offset)])
                else:
                    per = LANDED[n_static + 6] - LANDED[n_static]
                    pe.wait_ge(landed[slot], u * per + LANDED[n_static])
                return ring[slot][:]

            def inputs(n, turn, u, static_u):
                for b in range(2):
                    w = landed_at(n + b, 0, turn)
                    if large:
                        wv = w.rearrange("p (c f) -> p c f", f=512)
                        parts = [(B[(4, 6)[b] + h], (2 * h + k) * P, k) for h in range(2) for k in range(2)]
                    else:
                        wv = w.rearrange("p (g c f) -> p g c f", g=2, f=256)
                        parts = [(B[(4, 6)[g] + b], g, k) for g in range(2) for k in range(2)]
                    if b == 0 and not (static_u and u == 0):
                        pe.wait_ge(s["silu_done"], 2 * u + d["silu"])
                        if not large:
                            pe.wait_ge(s["hid_done"], u + d["hid"])
                    if large and b == 1 and not (static_u and u == 0):
                        pe.wait_ge(s["hid_done"], u + d["hid"])
                    for bank, a, k in parts:
                        for c in range(C):
                            lhs = wv[:, c, a:a + P] if large else wv[:, a, c, k * P:(k + 1) * P]
                            ins = mm(bank[:, k * T:(k + 1) * T], lhs, hT[:, c, :], start=c == 0, stop=c == C - 1)
                    ins.then_inc(tile_used, 1)

            def down(n, turn, u, par, last=False):
                w = landed_at(n, 0, turn).rearrange("p (k m) -> p k m", m=D)
                pe.wait_ge(s["hid_done"], u + (d["hid"] + 1))
                for tt in range(TT):
                    for h in range(2):
                        for k in range(4):
                            ins = mm(B[2 * tt + h][:], hidb[par][:, k, tt * P:(tt + 1) * P],
                                     w[:, k, 512 * h:512 * (h + 1)], start=False, stop=last and k == 3)
                ins.then_inc(tile_used, 1)

            pe.wait_ge(s["router_out"], i + 1)
            inputs(n0, 0, 0, True)
            pe.wait_ge(s["comb_ready"], i + 1)
            for j in range(8):
                if j >= 4:
                    pe.wait_ge(s["combT_act"] if j % 2 == 0 else s["combT_dve"], 4 * i + (j - 4) // 2 + 1)
                for a in range(2):
                    for tt in range(TT):
                        ins = mm(B[j % 4][:, a * T + tt * P:a * T + (tt + 1) * P],
                                 comb[:, tt, 2 * j + a:2 * j + a + 1].broadcast_to([P, P]), ident[:],
                                 start=True, stop=True)
                ins.then_inc(s["combT_ready"], 1)
            pe.wait_ge(s["combT_act"], 4 * i + 4)
            pe.wait_ge(s["combT_dve"], 4 * i + 4)
            for b in range(4):
                mm(B[b][:], zeros[:], bc(ident[:], 1, [P, 4, P]), start=True, stop=False)
            with pe.Fori(0, (U - 2) // 2) as t:
                for j in range(2):
                    n = unit_tile(n0, 1 + j)
                    inputs(n, t, 2 * t + (1 + j), False)
                    down(n + 2, t, 2 * t + j, j)
            n = unit_tile(n0, U - 1)
            inputs(n, 0, U - 1, True)
            down(n + 2, 0, U - 2, 0)
            down(n + 3, 0, U - 1, 1, last=True)

        pe.wait_ge(s["constants"], 1)
        pe.wait_ge(s["rows_loaded"], 16 * len(colrows))
        for t in range(3):
            rows = (P, P, 57)[t]
            nc.tensor.transpose(B[4 + t][:, 0:rows], stage[0:rows, t, 0:P],
                                ident[0:rows, 0:rows]).then_inc(s["cols_transposed"], 1)

        pe.wait_ge(s["cact_ready"], 1)
        modulation("ada0", 0, 0)
        pe.wait_ge(s["mod_ready"], 1)
        pe.wait_ge(s["xn_ready"], 1)
        xn = pb[:, :, 0:D]
        transposes("h0", from_tokens(xn))
        stage_transposed(pe, "h0")
        project("evin", 6, hT)
        pe.wait_ge(s["roped"], 4)
        transposes("qk0", from_tokens(pb, lambda c: P * c if c < 8 else 1536 + P * (c - 8)))
        stage_transposed(pe, "qk0")
        proj_evacuated(pe, PROJ["evin"] + 5)
        attention("att0")
        pe.wait_ge(s["ob_ready"], 1)
        transposes("ob", from_tokens(pb))
        stage_transposed(pe, "ob")
        pe.wait_ge(s["ot_out"], 8)
        project("evout", 2, OT)
        pe.wait_ge(s["xn_ready"], 2)
        transposes("h1", from_tokens(xn))
        experts("moe0", "h1")
        pe.wait_ge(s["moe_added"], 1)
        modulation("ada1", 1, 0)
        pe.wait_ge(s["mod_ready"], 2)
        pe.wait_ge(s["xn_ready"], 3)
        transposes("h2", from_tokens(xn))
        stage_transposed(pe, "h2")
        project("odin", 5, hT)
        m = PROJ["odin"] + 5
        bank_pair_free(m)
        for tt in range(TT):
            for c in range(C):
                ins = mm(B[2 * (m % 2) + tt][:, 0:48], hT[:, c, tt * P:(tt + 1) * P], w48[:, c, :],
                         start=c == 0, stop=c == C - 1)
        ins.then_inc(s["tail_ready"], 1)
        pe.wait_ge(s["roped"], 9)
        proj_evacuated(pe, PROJ["odin"] + 5)
        transposes("qkv1", from_tokens(pb))
        for kv in range(2):
            n = TILE["cmp"] + kv
            pe.wait_ge(landed[n % NSLOT], LANDED[n])
            pe.wait_ge(s["blocks_ready"], kv + 1)
            w = ring[n % NSLOT][:].rearrange("p (c f) -> p c f", f=256)
            for l in range(16):
                ins = mm(B[kv][0:60, 0:256], cmpB[:, kv, l].rearrange("p g n -> p (g n)"), w[:, l, :],
                         start=l == 0, stop=l == 15)
            ins.then_inc(tile_used, 1)
        pe.wait_ge(s["hidden_done"], 2)
        transposes("cmph", lambda j, bank: [(bank[:, 60 * (2 * kv + k):60 * (2 * kv + k + 1)],
                                             cmph[:, kv, k * P:(k + 1) * P]) for kv in range(2) for k in range(2)])
        stage_transposed(pe, "cmph")
        hT4 = hidT_c.rearrange("p (v k g n) -> p v k g n", v=2, k=2, g=4)
        for k in range(2):
            ins = mm(B[6][:, 0:60], w2c[:, k, 0:2, :].rearrange("p e d -> p (e d)"),
                     hT4[:, 0, k].rearrange("p g n -> p (g n)"), start=k == 0, stop=k == 1)
        ins.then_inc(s["kcmp_ready"], 1)
        for g in range(4):
            for k in range(2):
                ins = mm(B[7][0:NCMP, g * HD:(g + 1) * HD], hT4[:, 1, k, g, :], w2c[:, k, 2, :],
                         start=k == 0, stop=k == 1)
        ins.then_inc(s["vcmp_ready"], 1)
        pe.wait_ge(s["kcmp_out"], 1)
        pe.wait_ge(s["vcmp_out"], 1)
        for tt in range(TT):
            for h in range(16):
                rows = slice((h % 2) * HD, (h % 2 + 1) * HD)
                slot = 8 * tt + h // 2
                ins = mm(B[6 + h % 2][:, slot * NCMP:(slot + 1) * NCMP],
                         A[rows, h // 2, tt * P:(tt + 1) * P], kcmpT[rows, (h // 4) * NCMP:(h // 4 + 1) * NCMP],
                         start=True, stop=True)
        ins.then_inc(s["cscore_ready"], 1)
        pe.wait_ge(s["cscore_out"], 1)
        attention("att1")
        pe.wait_ge(s["ot_out"], 16)
        project("odout", 2, OT)
        pe.wait_ge(s["xn_ready"], 4)
        transposes("h3", from_tokens(xn))
        experts("moe1", "h3")
        pe.wait_ge(s["moe_added"], 2)
        modulation("ada2", 2, C)
        pe.wait_ge(s["mod_ready"], 3)
        pe.wait_ge(s["xn_ready"], 5)
        transposes("h4", from_tokens(xn))
        stage_transposed(pe, "h4")
        for tt in range(TT):
            for c in range(C):
                ins = mm(B[6][:, 32 * tt:32 * tt + 24], hT[:, c, tt * P:(tt + 1) * P], wdf[:, c, :],
                         start=c == 0, stop=c == C - 1)
        ins.then_inc(s["dt_ready"], 1)
        for j in range(4):
            m = PROJ["xbc"] + j
            w = landed_tile(TILE["xbc"] + j)
            if j >= 2:
                bank_pair_free(m)
            for a in range(4):
                for c in range(C):
                    ins = mm(B[2 * (m % 2) + a // 2][:, (a % 2) * T:(a % 2 + 1) * T], w[:, c, a * P:(a + 1) * P],
                             hT[:, c, :], start=c == 0, stop=c == C - 1)
            ins.then_inc(tile_used, 1)
        pe.wait_ge(s["a_ready"], 1)
        for tt in range(TT):
            mm(B[7][:, 16 * tt:16 * tt + 16], tri, dts[:, 4, tt, 0:16], start=True, stop=True)
            ins = mm(B[7][:, 32 + 16 * tt:48 + 16 * tt], tri_gt[:], dts[:, 4, tt, 0:16], start=True, stop=True)
        ins.then_inc(s["cs_ready"], 1)
        pe.wait_ge(s["conv_act"], 16)
        transposes("xs", lambda j, bank: [(bank[:, P * a:P * (a + 1)],
                                           xT[:, 4 * (j % 2) + a, 3 + P * (j // 2):3 + P * (j // 2 + 1)])
                                          for a in range(4)])
        transposes("btok", lambda j, bank: [(bank[:, P * g:P * (g + 1)], xT[:, 8 + g, 3:3 + P]) for g in range(4)])
        stage_transposed(pe, "btok")
        pe.wait_ge(s["xdt_ready"], 1)
        pe.wait_ge(s["cs_out"], 1)
        for g in range(4):
            if g >= 2:
                pe.wait_ge(s["state_out"], g - 1)
            mm(B[2 + g % 2][:, 0:256], Btok[:, P * g:P * (g + 1)], xdte[:, 256 * g:256 * (g + 1)],
               start=True, stop=True).then_inc(s["state_ready"], 1)
        pe.wait_ge(s["state_out"], 4)
        for q in range(9):
            if q < 8:
                tt, g = q // 4, q % 4
                if q >= 2:
                    pe.wait_ge(s["seg_out"], q - 1)
                    pe.wait_ge(s["m_ready"], q - 1)
                for r in range(4):
                    mm(B[6 + q % 2][:, r * P:(r + 1) * P],
                       dts[:, 4, tt, 4 * g + r:4 * g + r + 1].broadcast_to([P, P]), tri, start=True, stop=True)
                tok = slice(3 + tt * P, 3 + (tt + 1) * P)
                mm(B[q % 2][:, 0:P], xT[:, 8 + g, tok], xT[:, 12 + g, tok], start=True,
                   stop=True).then_inc(s["seg_ready"], 1)
            if q >= 1:
                r0 = q - 1
                tt, g = r0 // 4, r0 % 4
                bank = B[2 + r0 % 2]
                if r0 >= 2:
                    pe.wait_ge(s["y_out"], r0 - 1)
                if tt == 1:
                    mm(bank[:, 256:512], xT[:, 12 + g, 3 + P:3 + 2 * P], stT[:, 256 * g:256 * (g + 1)],
                       start=True, stop=True)
                pe.wait_ge(s["m_ready"], r0 + 1)
                for r in range(4):
                    h = 4 * g + r
                    ins = mm(bank[:, r * HD:(r + 1) * HD], mt[r0 % 2][:, r * P:(r + 1) * P],
                             pb[:, tt, D + h * HD:D + (h + 1) * HD], start=True, stop=True)
                ins.then_inc(s["y_ready"], 1)
        pe.wait_ge(s["y_out"], 8)
        project("z", 2, hT)
        pe.wait_ge(s["gated_ready"], 1)
        transposes("gated", from_tokens(pb, lambda c: 2 * D + P * c))
        stage_transposed(pe, "gated")
        project("ssdo", 2, OT)
        bank_pair_free(PROJ["qkv"])
        bank_pair_free(PROJ["qkv"] + 1)
        project("qkv", 3, hT)
        proj_evacuated(pe, PROJ["qkv"] + 2)
        transposes("qk2", from_tokens(pb))
        stage_transposed(pe, "qk2")
        attention("att2")
        pe.wait_ge(s["ot_out"], 20)
        n = TILE["atto"]
        pe.wait_ge(landed[n % NSLOT], LANDED[n])
        w = ring[n % NSLOT][:].rearrange("p (c n) -> p c n", n=D)
        for j in range(2):
            m = PROJ["atto"] + j
            for tt in range(TT):
                for c in range(4):
                    ins = mm(B[2 * (m % 2) + tt][:], OT[:, c, tt * P:(tt + 1) * P],
                             w[:, c, 512 * j:512 * (j + 1)], start=c == 0, stop=c == 3)
        ins.then_inc(tile_used, 1)
        bank_pair_free(PROJ["gates"])
        bank_pair_free(PROJ["gates"] + 1)
        project("gates", 4, hT)
        pe.wait_ge(s["merged_ready"], 1)
        transposes("merged", from_tokens(pb, lambda c: D + P * c))
        stage_transposed(pe, "merged")
        project("wo", 2, OT)
        pe.wait_ge(s["xn_ready"], 6)
        transposes("h5", from_tokens(xn))
        experts("moe2", "h5")


_NAMES = ("x c norm1_g norm2_g final_g ada_w ada_b ev_w_in ev_w_out ev_lambda ev_subln_g od_w_in od_w_out "
          "od_cmp_pos od_cmp_w1 od_cmp_b1 od_cmp_w2 od_cmp_b2 moe_wg moe_bg moe_we moe_be moe_w_gate moe_w_up "
          "moe_w_down c_2 w_mod_2 b_mod_2 w_in_2 conv_w_2 conv_b_2 dt_bias_2 a_log_2 d_skip_2 ssd_norm_w_2 "
          "forget_b_2 w_ssd_o_2 w_att_o_2 w_o_2 ln1_g_2 ln1_b_2 w_router_group_2 b_router_group_2 "
          "w_router_expert_2 b_router_expert_2 w_gate_2 w_up_2 w_down_2 ln2_g_2 ln2_b_2").split()


def rope_table():
    inv = (np.float32(500000.0) ** (-np.arange(0, 16, 2, dtype=np.float32) / np.float32(16))).astype(np.float32)
    ang = np.arange(T, dtype=np.float32)[:, None] * inv[None, :]
    return np.stack([np.tile(np.cos(ang), (1, 2)), np.tile(np.sin(ang), (1, 2))]).astype(np.float32)


def kernel(**inputs):
    import numpy as _np
    import concourse.bacc as _bacc
    from concourse import mybir as _mybir
    from concourse.bass_utils import run_bass_kernel_spmd as _run

    nc = _bacc.Bacc("TRN2", target_bir_lowering=False, num_devices=1)
    arrays, params = {}, {}
    for name in _NAMES:
        a = _np.ascontiguousarray(inputs[name])
        arrays[f"in_{name}"] = a
        params[name] = nc.dram_tensor(f"in_{name}", a.shape, _mybir.dt.from_np(a.dtype), kind="ExternalInput").ap()
    table = rope_table()
    arrays["rope_table"] = table
    rope = nc.dram_tensor("rope_table", table.shape, _mybir.dt.float32, kind="ExternalInput").ap()
    out = nc.dram_tensor("out_0", (1, T, D), _mybir.dt.float32, kind="ExternalOutput").ap()
    two_blocks(nc, params, rope, out)
    r = _run(nc, [arrays], core_ids=[0])
    return r.results[0]["out_0"]
```

```python
import math
from contextlib import ExitStack

import numpy as np

import concourse.bass as bass
from concourse import mybir

F32 = mybir.dt.float32
ALU = mybir.AluOpType
ACT = mybir.ActivationFunctionType
AX = mybir.AxisListType

P = 128
T = 256
TT = T // P
D = 1024
C = D // P
HD = 64
HALF_ROPE = 8
SCALE = HD ** -0.5
NEG = -1e30
RMS_EPS = 1e-6
LN_EPS = 1e-5
ALPHA = 2 ** 0.25
LAMBDA_INIT = 0.8 - 0.6 * math.exp(0.0)
NSLOT = 6
SLOT = 4096
NSMALL = 28
NCMP = (T - 32) // 16 + 1
GELU = ACT.Gelu_apprx_tanh

PHASES = [("ada0", 12), ("evin", 6), ("evout", 2), ("moe0", 24),
          ("ada1", 12), ("odin", 5), ("cmp", 2), ("odout", 2), ("moe1", 24),
          ("ada2", 12), ("xbc", 4), ("z", 2), ("ssdo", 2), ("qkv", 3), ("atto", 1),
          ("gates", 4), ("wo", 2), ("moe2", 48)]
TILE = {}
_n = 0
for _name, _k in PHASES:
    TILE[_name] = _n
    _n += _k
NTILES = _n
LOADS_PER_TILE = {}
for _n in range(NTILES):
    LOADS_PER_TILE[_n] = 1
for _moe in ("moe0", "moe1"):
    _u = 8
    for _n in range(TILE[_moe], TILE[_moe] + 3 * _u):
        _r = _n - TILE[_moe]
        _down = _r == 3 * _u - 1 or (_r >= 2 and (_r - 2) % 3 == 2)
        LOADS_PER_TILE[_n] = 1 if _down else 2
for _n in range(TILE["cmp"], TILE["cmp"] + 2):
    LOADS_PER_TILE[_n] = 1
LANDED = {}
_count = [0] * NSLOT
for _n in range(NTILES):
    _count[_n % NSLOT] += 16 * LOADS_PER_TILE[_n]
    LANDED[_n] = _count[_n % NSLOT]

TRANS = {}


def unit_tile(base, u):
    return base + (3 * u - 1 if u else 0)

TRANS_STAGES = [("h0", 4), ("qk0", 8), ("att0", 12), ("ob", 2), ("h1", 4),
                ("h2", 4), ("qkv1", 12), ("cmph", 1), ("att1", 48), ("h3", 4),
                ("h4", 4), ("xs", 4), ("btok", 1), ("gated", 4), ("qk2", 4), ("att2", 8),
                ("merged", 4), ("h5", 4)]
_n = 0
for _name, _k in TRANS_STAGES:
    TRANS[_name] = _n
    _n += _k
TRANS_END = {_name: TRANS[_name] + _k for _name, _k in TRANS_STAGES}

PROJ_STAGES = [("evin", 6, 1, 1), ("evout", 2, 0, 1), ("odin", 6, 1, 1), ("odout", 2, 0, 1),
               ("xbc", 4, 1, 1), ("z", 2, 1, 0), ("ssdo", 2, 1, 1), ("qkv", 3, 1, 1),
               ("atto", 2, 1, 1), ("gates", 4, 1, 0), ("wo", 2, 0, 1)]
PROJ = {}
PROJ_ACT, PROJ_DVE = [], []
for _name, _k, _a, _d in PROJ_STAGES:
    PROJ[_name] = len(PROJ_ACT)
    for _ in range(_k):
        PROJ_ACT.append((PROJ_ACT[-1] if PROJ_ACT else 0) + _a)
        PROJ_DVE.append((PROJ_DVE[-1] if PROJ_DVE else 0) + _d)

SOFT = {"att0": 0, "att1": 16, "att2": 48}
OTB = {"att0": 0, "att1": 8, "att2": 16}
NORMS = ["h0", "h1", "h2", "h3", "h4", "h5"]
COL = {}


def col_rows(params):
    out = []

    def put(name, tile, row, view):
        COL[name] = tile * P + row
        out.append((tile, row, view.shape[0], view))

    put("ada_b", 0, 0, params["ada_b"].rearrange("l (r p) -> (l r) p", p=P))
    put("norm1_g", 0, 96, params["norm1_g"].rearrange("l (r p) -> (l r) p", p=P))
    put("norm2_g", 0, 112, params["norm2_g"].rearrange("l (r p) -> (l r) p", p=P))
    put("b_mod_2", 1, 0, params["b_mod_2"].rearrange("l (r p) -> (l r) p", p=P))
    put("conv_w_2", 1, 48, params["conv_w_2"].rearrange("l k (r p) -> (l k r) p", p=P))
    put("conv_b_2", 1, 112, params["conv_b_2"].rearrange("l (r p) -> (l r) p", p=P))
    put("c", 2, 0, params["c"].rearrange("l (r p) -> (l r) p", p=P))
    put("c_2", 2, 8, params["c_2"].rearrange("l (r p) -> (l r) p", p=P))
    put("ssd_norm_w_2", 2, 16, params["ssd_norm_w_2"].rearrange("l (r p) -> (l r) p", p=P))
    put("ev_subln_g", 2, 24, params["ev_subln_g"])
    put("pos", 2, 25, params["od_cmp_pos"].rearrange("o k (r l) d -> (o k r) (l d)", l=2))
    return out


class Semaphores(dict):

    def __init__(self, nc, ctx):
        super().__init__()
        self.nc, self.ctx = nc, ctx

    def __missing__(self, name):
        self[name] = self.ctx.enter_context(self.nc.semaphore(name))
        return self[name]


def two_blocks(nc, params, rope, out):
    with ExitStack() as ctx:
        emit(nc, ctx, params, rope, out)


def emit(nc, ctx, p, rope_dram, out):
    def sb(name, shape):
        return ctx.enter_context(nc.sbuf_tensor(name, shape, F32))

    ring = [sb(f"ring{i}", [P, SLOT]) for i in range(NSLOT)]
    x = sb("x", [P, TT, D])
    hT = sb("hT", [P, C, T])
    gate1 = sb("gate1", [P, D])
    gate2 = sb("gate2", [P, D])
    PBW = 3584
    pb = sb("pb", [P, TT, PBW])
    pb_flat = pb[:].rearrange("p a b -> p (a b)")
    A = sb("A", [P, 24, T])
    A_flat = A[:].rearrange("p a b -> p (a b)")
    OT = sb("OT", [P, C, T])
    OT_flat = OT[:].rearrange("p a b -> p (a b)")
    Pm = sb("Pm", [P, 2, 384])
    PT = sb("PT", [P, 2, 384])
    tmp = sb("tmp", [P, 2, 512])
    S_sb = tmp[:, :, 0:384]
    ident = sb("ident", [P, P])
    mask384 = sb("mask384", [P, 384])
    maskT = sb("maskT", [P, P])
    tri_one = sb("tri_one", [P, T])
    tri = tri_one[:, 0:P]
    tri_gt = sb("tri_gt", [P, P])
    zeros = sb("zeros", [P, P])
    mark = sb("mark", [P, 8])
    maskc = sb("maskc", [P, TT, NCMP])
    cmp_live = sb("cmp_live", [P, TT])
    cosd = sb("cosd", [P, TT, 16])
    sind = sb("sind", [P, TT, 16])
    ropeA, ropeB = (Pm[:, i, 0:256].rearrange("p (a h d) -> p a h d", a=TT, h=8) for i in range(2))
    cols = sb("cols", [P, 3 * P])
    stage = A
    modc = sb("modc", [P, 4, C])
    cact = sb("cact", [P, 2 * C])
    stats = sb("stats", [P, TT, 2, 6])
    mv = sb("mv", [P, TT, 2])
    rstd = sb("rstd", [P, TT])
    nhalf = sb("nhalf", [P, 8])
    nmx = sb("nmx", [P, 2, 2])
    rs = sb("rs", [P, 2, 2])
    rr = sb("rr", [P, 2, 2])
    lam = sb("lam", [P, 8])
    lamrow = sb("lamrow", [P, 4, HD])
    subc = sb("subc", [P, 1])
    obs = sb("obs", [P, 8])
    wr = [sb(f"wr{i}", [P, C, 20]) for i in range(3)]
    br = [sb(f"br{i}", [P, 20]) for i in range(3)]
    w48 = A_flat[:, 4096:4096 + C * 48].rearrange("p (c n) -> p c n", c=C)
    wdf = sb("wdf", [P, C, 24])
    gts = sb("gts", [P, TT, 48])
    rt = sb("rt", [P, TT, 16, 4])
    comb = sb("comb", [P, TT, 16])
    chosen = sb("chosen", [P, TT, 16])
    place = sb("place", [P, TT, 16])
    slot_no = sb("slot_no", [P, 96])
    count = sb("count", [P, 2])
    flag = ctx.enter_context(nc.sbuf_tensor("flag", [P, 3], mybir.dt.int32))
    first = sb("first", [P, 4])
    b1c = OT_flat[0:60, 512:1024].rearrange("p (k f) -> p k f", k=2)
    b2v = sb("b2v", [NCMP, HD])
    w2c = sb("w2c", [P, 2, 3, HD])
    b2k = sb("b2k", [P, 1])
    kcmpT = sb("kcmpT", [P, 60])
    vcmp = sb("vcmp", [NCMP, 4, HD])
    cs = sb("cs", [P, 4, 32])
    dts = sb("dts", [P, 6, TT, 24])
    bdf = sb("bdf", [P, 24])
    alog = sb("alog", [P, 16])
    dsk = sb("dsk", [P, 16])
    B = [ctx.enter_context(nc.psum_tensor(f"bank{i}", [P, 512], F32)) for i in range(8)]
    s = Semaphores(nc, ctx)
    for i in range(NSLOT):
        s[f"landed{i}"]
    landed = [s[f"landed{i}"] for i in range(NSLOT)]
    tile_used = s["tile_used"]

    colrows = col_rows(p)

    def col(name, i=0, n=1):
        return cols[:, COL[name] + i:COL[name] + i + n]

    def bc(ap, axis, shape):
        return ap.unsqueeze(axis).broadcast_to(shape)

    def trans_evacuated(eng, k):
        eng.wait_ge(s["tr_act"] if k % 2 == 0 else s["tr_dve"], k // 2 + 1)

    def stage_transposed(eng, name):
        for k in (TRANS_END[name] - 2, TRANS_END[name] - 1):
            if k >= 0:
                trans_evacuated(eng, k)

    def proj_evacuated(eng, m):
        if PROJ_ACT[m]:
            eng.wait_ge(s["proj_act"], PROJ_ACT[m])
        if PROJ_DVE[m]:
            eng.wait_ge(s["proj_dve"], PROJ_DVE[m])

    def tile_ready(eng, n):
        eng.wait_ge(tile_used, n + 1)

    def head(buf, chunk, half):
        return buf[half * HD:(half + 1) * HD, chunk, :]

    def attention_items(stage_name):
        items = []
        u, k, o = SOFT[stage_name], TRANS[stage_name], OTB[stage_name]

        def plain_pv(vbuf, voff, half, bank, start, stop):
            def pv(pt):
                dst = B[bank][half * HD:(half + 1) * HD, 0:T]
                v = [vbuf[:, tt, voff:voff + HD] for tt in range(TT)]
                return [(dst, v[0], pt[:, 0:T], start, False),
                        (dst[:, P:T], v[1], pt[:, T:384], False, stop)]
            return pv

        if stage_name in ("att0", "att2"):
            for h in range(8):
                ot = o + h // 2
                items.append(dict(
                    soft=u, tr=k, kind="plain", q=head(A, h // 2, h % 2), k=head(A, 4 + h // 2, h % 2),
                    pv=plain_pv(pb, (1024 if stage_name == "att0" else 1024) + h * HD, h % 2, ot % 2, True, True),
                    forget=h if stage_name == "att2" else None,
                    ot=ot, ot_first=h % 2 == 0,
                    evac=(OT[:, h // 2, :], B[ot % 2][:, 0:T]) if h % 2 else None, gate=None))
                u, k = u + 1, k + 1
        if stage_name == "att0":
            for h in range(4):
                for m in range(2):
                    ot = o + 4 + h

                    def pv(pt, h=h, ot=ot):
                        bank = B[ot % 2][:, 0:T]
                        v = [pb[:, tt, 2560 + h * P:2560 + (h + 1) * P] for tt in range(TT)]
                        return [(bank[:, 0:P], pt[:, 0:P], v[0], True, True),
                                (bank[:, P:T], pt[:, P:T], v[0], True, False),
                                (bank[:, P:T], pt[:, T:384], v[1], False, True)]
                    items.append(dict(
                        soft=u, tr=k if m else None, kind=f"map{m}", q=head(A, 8 + h, m), k=head(A, 12 + h, m),
                        pv=pv, forget=None, ot=ot, ot_first=True, gate=None,
                        evac=(pb[:, :, h * P:(h + 1) * P], B[ot % 2][:, 0:T].rearrange("p (a b) -> p a b", a=TT))))
                    u += 1
                k += 1
        if stage_name == "att1":
            for h in range(16):
                g = h // 4
                ot = o + h // 2
                for b, (kc0, voff) in enumerate(((16, 3072), (20, 3328))):
                    items.append(dict(
                        soft=u, tr=k, kind="plain", q=head(A, h // 2, h % 2), k=head(A, kc0 + g, h % 2),
                        pv=plain_pv(pb, voff + g * HD, h % 2, ot % 2, b == 0, False), forget=None,
                        ot=ot, ot_first=h % 2 == 0 and b == 0, gate=(h, b + 1), evac=None))
                    u, k = u + 1, k + 1

                def pv(pt, g=g, h=h, ot=ot):
                    dst = B[ot % 2][(h % 2) * HD:(h % 2 + 1) * HD, 0:T]
                    return [(dst, vcmp[:, g, :], pt[0:NCMP, 0:T], False, True)]
                items.append(dict(
                    soft=None, tr=k, kind="cmp", h=h, pv=pv, ot=ot, ot_first=False, gate=None, forget=None,
                    evac=(OT[:, h // 2, :], B[ot % 2][:, 0:T]) if h % 2 else None))
                k += 1
        return items

    ITEMS = {name: attention_items(name) for name in SOFT}
    PV_BASE = {"att0": 0, "att1": 12, "att2": 60}
    for name in SOFT:
        n = PV_BASE[name]
        for it in ITEMS[name]:
            it["pvn"] = n
            if it["tr"] is not None:
                n += 1
    ALL = [it for name in ("att0", "att1", "att2") for it in ITEMS[name]]
    READER = {it["soft"]: it["tr"] for it in ALL if it["soft"] is not None}
    ALL_TR = [it for it in ALL if it["tr"] is not None]
    PREV_PV = {}
    last_on = {}
    for it in ALL_TR:
        PREV_PV[it["tr"]] = last_on.get(it["tr"] % 2)
        last_on[it["tr"] % 2] = it["pvn"]
    OT_DONE = {}
    for it in ALL_TR:
        OT_DONE[it["ot"]] = it["pvn"] + 1

    MOE = {"moe0": dict(U=8, unit=0, ga=0, idx=0, slots=64, width=128, passes=2, eu=2),
           "moe1": dict(U=8, unit=8, ga=16, idx=1, slots=64, width=128, passes=2, eu=2),
           "moe2": dict(U=16, unit=16, ga=32, idx=2, slots=96, width=96, passes=2, eu=1)}
    hg = [A_flat[:, 1024 * b:1024 * (b + 1)] for b in range(2)]
    hidb = [A_flat[:, 2048 + 384 * b:2432 + 384 * b] for b in range(2)]
    silub = [A_flat[:, 2816 + 384 * b:3200 + 384 * b] for b in range(2)]
    swT = [A_flat[:, 3584 + T * b:3584 + T * (b + 1)] for b in range(2)]
    ye = [OT_flat[:, D * b:D * (b + 1)] for b in range(2)]
    swb = [pb[:, :, 2560 + P * b:2560 + P * (b + 1)] for b in range(2)]
    hid_all = A[:, 0:4, :]
    silu_all = A[:, 4:8, :]
    combT = pb_flat[:, 0:16 * T].rearrange("p (e t) -> p e t", e=16)
    rowp = A[:, 16:24, :].rearrange("p (r a) t -> p r (a t)", r=2)

    cmph = OT_flat[0:60, 0:512].rearrange("p (k f) -> p k f", k=2)
    hidT_c = OT_flat[:, 1024:1264]
    cmpB = pb[:, :, 0:960].rearrange("p k (l g n) -> p k l g n", l=16, g=4)
    pc = pb[:, 0, 1024:1504]
    xT = A_flat[:, 0:16 * 259].rearrange("p (c t) -> p c t", t=259)
    mt = [A_flat[:, 4144 + 512 * b:4656 + 512 * b] for b in range(2)]
    xdte = OT_flat[:, 0:D]
    stT = OT_flat[:, D:2 * D]
    Btok = pb[:, 0, 3072:3584]
    satt = A[:, 8:16, :].rearrange("p (a c) t -> p a (c t)", a=TT)

    def odd_kv(copy, j, tt, bank):
        def twice(c0, src):
            return copy(pb[:, tt, c0:c0 + 512].rearrange("p (g e d) -> p g e d", g=4, e=2),
                        bc(src.rearrange("p (g d) -> p g d", g=4), 2, [P, 4, 2, HD]))
        twice({2: 1024, 3: 2048, 4: 2560}[j], bank[:, 0:256])
        if j == 2:
            return twice(1536, bank[:, 256:512])
        return copy(pb[:, tt, 3072 + 256 * (j - 3):3328 + 256 * (j - 3)], bank[:, 256:512])

    def evacuate_p(eng, it, copy, done):
        k = it["tr"]
        eng.wait_ge(s["tr_ready"], k + 1)
        if PREV_PV[k] is not None:
            eng.wait_ge(s["pv_done"], PREV_PV[k] + 1)
        rows, width = (NCMP, T) if it["kind"] == "cmp" else (P, 384)
        copy(PT[0:rows, k % 2, 0:width], B[4 + k % 2][0:rows, 0:width]).then_inc(s[done], 1)

    def routing_exp(act, name):
        i = MOE[name]["idx"]
        act.wait_ge(s["route_shifted"], i + 1)
        nc.scalar.activation(rt[:, :, 0:2, :], rt[:, :, 0:2, :], ACT.Exp).then_inc(s["route_exp"], 1)

    def overflows(eng, name):
        i = MOE[name]["idx"]
        eng.wait_ge(s["flag_ready"], i + 1)
        return eng.value_load(flag[0:1, i:i + 1], min_val=0, max_val=1)

    block = ctx.enter_context(nc.Block())

    @block.sync
    def _(sp):
        def slot_free(n):
            if isinstance(n, int):
                if n >= NSLOT:
                    sp.wait_ge(tile_used, n - NSLOT + 1)
            else:
                sp.wait_ge(tile_used, n - (NSLOT - 1))

        def load(n, slot, view, src, wait=True):
            if wait:
                slot_free(n)
            sp.dma_start(view, src).then_inc(landed[slot], 16)

        def kview(slot, width=512):
            return ring[slot][:].rearrange("p (c n) -> p c n", n=width)

        def columns(w, n0, col0, tiles):
            for j in range(tiles):
                n = n0 + j
                load(n, n % NSLOT, kview(n % NSLOT),
                     w.rearrange("(c p) n -> p c n", p=P)[:, :, col0 + 512 * j:col0 + 512 * (j + 1)])

        def ada(name, w):
            n0 = TILE[name]
            wv = w.rearrange("(c p) n -> p c n", p=P)
            with sp.Fori(0, 2) as i:
                for j in range(6):
                    slot = (n0 + j) % NSLOT
                    sp.wait_ge(tile_used, 6 * i + (n0 + j - NSLOT + 1))
                    sp.dma_start(kview(slot), wv[:, :, bass.ds(3072 * i + 512 * j, 512)]).then_inc(landed[slot], 16)

        def moe_small(name, wg, wu, wd):
            n0, U = TILE[name], 8
            gv = wg.rearrange("e (c p) f -> e p c f", p=P)
            uv = wu.rearrange("e (c p) f -> e p c f", p=P)
            dv = wd.rearrange("(u e) (k p) d -> u p (e k) d", p=P, e=2)

            def pick(v, i):
                return v[i] if isinstance(i, int) else v[bass.ds(i, 1)].rearrange("o p c f -> (o p) c f")

            def inputs(u, n, slots):
                for j in range(2):
                    slot = slots[j]
                    slot_free(n + j)
                    kv = ring[slot][:].rearrange("p (g c f) -> p g c f", g=2, f=256)
                    sp.dma_start(kv[:, 0], pick(gv, 2 * u + j)).then_inc(landed[slot], 16)
                    sp.dma_start(kv[:, 1], pick(uv, 2 * u + j)).then_inc(landed[slot], 16)

            def down(u, n, slot):
                slot_free(n)
                sp.dma_start(kview(slot, D), pick(dv, u)).then_inc(landed[slot], 16)
            stream(n0, U, inputs, down)

        def moe_large(name, wg, wu, wd):
            n0, U = TILE[name], 16
            gv = wg.rearrange("e (c p) f -> e p c f", p=P)
            uv = wu.rearrange("e (c p) f -> e p c f", p=P)
            dv = wd.rearrange("e (k p) d -> e p k d", p=P)

            def pick(v, i):
                return v[i] if isinstance(i, int) else v[bass.ds(i, 1)].rearrange("o p c f -> (o p) c f")

            def inputs(u, n, slots):
                for j, v in enumerate((gv, uv)):
                    slot_free(n + j)
                    sp.dma_start(kview(slots[j]), pick(v, u)).then_inc(landed[slots[j]], 16)

            def down(u, n, slot):
                slot_free(n)
                sp.dma_start(kview(slot, D), pick(dv, u)).then_inc(landed[slot], 16)
            stream(n0, U, inputs, down)

        def stream(n0, U, inputs, down):
            inputs(0, n0, [n0 % NSLOT, (n0 + 1) % NSLOT])
            with sp.Fori(0, (U - 2) // 2) as i:
                for j in range(2):
                    u = 1 + j
                    n = unit_tile(n0, u)
                    slots = [(n + a) % NSLOT for a in range(3)]
                    inputs(2 * i + u, 6 * i + n, slots)
                    down(2 * i + (u - 1), 6 * i + (n + 2), slots[2])
            u = U - 1
            n = unit_tile(n0, u)
            inputs(u, n, [n % NSLOT, (n + 1) % NSLOT])
            down(u - 1, n + 2, (n + 2) % NSLOT)
            down(u, n + 3, (n + 3) % NSLOT)

        def moe_rest(name, wg, wu, wd):
            i, n_end = MOE[name]["idx"], TILE[name] + 3 * MOE[name]["U"]
            F = wg.shape[-1]
            nk = F // P
            gv = wg.rearrange("e (c p) f -> e p c f", p=P)
            uv = wu.rearrange("e (c p) f -> e p c f", p=P)
            dv = wd.rearrange("e (k p) d -> e p k d", p=P)
            over = overflows(sp, name)
            with sp.If(over > 0):
                sp.wait_ge(tile_used, n_end)
                with sp.Fori(0, 16) as e:
                    sp.wait_ge(s[f"rest_used{i}"], e + 1)
                    for slot, v, n in ((0, gv, C), (1, uv, C), (2, dv, nk)):
                        dst = ring[slot][:, 0:n * v.shape[-1]].rearrange("p (c f) -> p c f", c=n)
                        sp.dma_start(dst, v[bass.ds(e, 1)].rearrange("o p c f -> (o p) c f")).then_inc(
                            s[f"rest_landed{i}"], 16)
                sp.wait_ge(s[f"rest_used{i}"], 17)

        columns(p["ada_w"][0], TILE["ada0"], 0, 12)
        columns(p["ev_w_in"][0], TILE["evin"], 0, 6)
        columns(p["ev_w_out"][0], TILE["evout"], 0, 2)
        moe_small("moe0", p["moe_w_gate"][0], p["moe_w_up"][0], p["moe_w_down"][0])
        moe_rest("moe0", p["moe_w_gate"][0], p["moe_w_up"][0], p["moe_w_down"][0])
        ada("ada1", p["ada_w"][1])
        columns(p["od_w_in"][0], TILE["odin"], 0, 5)
        for j in range(2):
            n = TILE["cmp"] + j
            load(n, n % NSLOT, kview(n % NSLOT, 256), p["od_cmp_w1"][0, j].rearrange("(r p) f -> p r f", p=P))
        columns(p["od_w_out"][0], TILE["odout"], 0, 2)
        moe_small("moe1", p["moe_w_gate"][1], p["moe_w_up"][1], p["moe_w_down"][1])
        moe_rest("moe1", p["moe_w_gate"][1], p["moe_w_up"][1], p["moe_w_down"][1])
        ada("ada2", p["w_mod_2"][0])
        columns(p["w_in_2"][0], TILE["xbc"], 1024, 4)
        columns(p["w_in_2"][0], TILE["z"], 0, 2)
        columns(p["w_ssd_o_2"][0], TILE["ssdo"], 0, 2)
        columns(p["w_in_2"][0], TILE["qkv"], 3088, 3)
        n = TILE["atto"]
        load(n, n % NSLOT, kview(n % NSLOT, D), p["w_att_o_2"][0].rearrange("(c p) n -> p c n", p=P))
        columns(p["w_in_2"][0], TILE["gates"], 4632, 4)
        columns(p["w_o_2"][0], TILE["wo"], 0, 2)
        moe_large("moe2", p["w_gate_2"][0], p["w_up_2"][0], p["w_down_2"][0])
        moe_rest("moe2", p["w_gate_2"][0], p["w_up_2"][0], p["w_down_2"][0])
        sp.wait_ge(s["result"], 1)
        sp.dma_start(out.rearrange("b (a p) d -> p (b a) d", p=P), x[:]).then_inc(s["stored"], 16)
        sp.wait_ge(s["stored"], 16)

    @block.gpsimd
    def _(pool):
        steps = [0]

        def step(ins):
            steps[0] += 1
            ins.then_inc(s["pool_step"], 1)
            pool.wait_ge(s["pool_step"], steps[0])

        g = nc.gpsimd
        step(g.memset(ident[:], 0.0))
        step(g.affine_select(out=ident[:], in_=ident[:], compare_op=ALU.not_equal, fill=1.0, base=0,
                             pattern=[[-1, P]], channel_multiplier=1))
        g.memset(zeros[:], 0.0)
        g.iota(slot_no[:], pattern=[[1, 96]], base=1, channel_multiplier=0, allow_small_or_imprecise_dtypes=True)
        g.memset(nhalf[:], -0.5)
        g.memset(tri_one[:], 1.0)
        g.memset(tri_gt[:], 1.0)
        g.memset(maskT[:], 0.0)
        g.memset(mask384[:], 0.0)
        g.memset(maskc[:], 0.0)
        g.memset(cmp_live[:], 1.0)
        for j in range(4):
            ins = g.memset(first[:, j:j + 1], 4.0 - j)
        step(ins)
        g.affine_select(out=tri, in_=tri, compare_op=ALU.is_ge, fill=0.0, base=0,
                        pattern=[[1, P]], channel_multiplier=-1)
        g.affine_select(out=tri_gt[:], in_=tri_gt[:], compare_op=ALU.is_gt, fill=0.0, base=0,
                        pattern=[[-1, P]], channel_multiplier=1)
        g.affine_select(out=maskT[:], in_=maskT[:], compare_op=ALU.is_ge, fill=NEG, base=0,
                        pattern=[[1, P]], channel_multiplier=-1)
        for a in (0, 2 * P):
            g.affine_select(out=mask384[:, a:a + P], in_=mask384[:, a:a + P], compare_op=ALU.is_ge, fill=NEG,
                            base=0, pattern=[[-1, P]], channel_multiplier=1)
        for a in range(TT):
            g.affine_select(out=maskc[:, a, :], in_=maskc[:, a, :], compare_op=ALU.is_ge, fill=NEG,
                            base=P * a - 31, pattern=[[-16, NCMP]], channel_multiplier=1)
        step(g.affine_select(out=cmp_live[:, 0:1], in_=cmp_live[:, 0:1], compare_op=ALU.is_ge, fill=0.0,
                             base=-31, pattern=[[0, 1]], channel_multiplier=1))
        g.memset(mark[:, 0:1], 0.0).then_inc(s["constants"], 1)
        pool.wait_ge(s["small_loads"], 16 * NSMALL)

        ropes = [0]

        def rope(col0, m):
            proj_evacuated(pool, m)
            t = pb[:, :, col0:col0 + 512].rearrange("p a (h d) -> p a h d", d=HD)[:, :, :, 0:16]
            cb = bc(cosd[:], 2, [P, TT, 8, 16])
            sbb = bc(sind[:], 2, [P, TT, 8, 16])
            g.tensor_tensor(ropeA[:], t, cb, ALU.mult)
            step(g.tensor_tensor(ropeB[:], t, sbb, ALU.mult))
            g.tensor_tensor(t[:, :, :, 0:8], ropeA[:, :, :, 0:8], ropeB[:, :, :, 8:16], ALU.subtract)
            step(g.tensor_tensor(t[:, :, :, 8:16], ropeA[:, :, :, 8:16], ropeB[:, :, :, 0:8], ALU.add))
            ropes[0] += 1
            g.memset(mark[:, 0:1], 0.0).then_inc(s["roped"], 1)

        powers = [0]

        def power(dst, src):
            powers[0] += 1
            pool.wait_ge(s["var_ready"], powers[0])
            g.tensor_tensor(dst, src, nhalf[:, 0:src.shape[-1]], ALU.pow).then_inc(s["pow_done"], 1)

        power(rstd[:], rstd[:])
        for c0, j in ((0, 0), (512, 1), (1536, 3), (2048, 4)):
            rope(c0, PROJ["evin"] + j)
        power(obs[:], obs[:])
        power(rstd[:], rstd[:])
        power(rstd[:], rstd[:])
        for c0, j in ((0, 0), (512, 1), (1024, 2), (2048, 3), (2560, 4)):
            rope(c0, PROJ["odin"] + j)
        power(rstd[:], rstd[:])
        power(rstd[:], rstd[:])
        power(rstd[:], rstd[:])
        power(rstd[:], rstd[:])
        power(rstd[:], rstd[:])
        power(rstd[:], rstd[:])
        power(rstd[:], rstd[:])

    @block.scalar
    def _(act):
        a = nc.scalar
        ndma = [0]

        def small(dst, src):
            ndma[0] += 1
            act.dma_start(dst, src).then_inc(s["small_loads"], 16)

        act.dma_start(x[:], p["x"].rearrange("b (a q) d -> q (b a) d", q=P)).then_inc(s["x_loaded"], 16)
        for tile, row, n, view in colrows:
            act.dma_start(stage[row:row + n, tile, 0:P], view).then_inc(s["rows_loaded"], 16)
        act.dma_start(gate1[:], p["ada_b"][0, 2048:3072].partition_broadcast(P)).then_inc(s["gate_bias"], 16)
        act.dma_start(gate2[:], p["ada_b"][0, 5120:6144].partition_broadcast(P)).then_inc(s["gate_bias"], 16)
        small(cosd[:], rope_dram[0].rearrange("(a q) d -> q a d", q=P))
        small(sind[:], rope_dram[1].rearrange("(a q) d -> q a d", q=P))
        small(lamrow[:], p["ev_lambda"][0].partition_broadcast(P))
        for i in range(2):
            small(wr[i][:, :, 0:4], p["moe_wg"][i].rearrange("(c q) n -> q c n", q=P))
            small(wr[i][:, :, 4:20], p["moe_we"][i].rearrange("(c q) n -> q c n", q=P))
            small(br[i][:, 0:4], p["moe_bg"][i].partition_broadcast(P))
            small(br[i][:, 4:20], p["moe_be"][i].partition_broadcast(P))
        small(wr[2][:, :, 0:4], p["w_router_group_2"][0].rearrange("(c q) n -> q c n", q=P))
        small(wr[2][:, :, 4:20], p["w_router_expert_2"][0].rearrange("(c q) n -> q c n", q=P))
        small(br[2][:, 0:4], p["b_router_group_2"][0].partition_broadcast(P))
        small(br[2][:, 4:20], p["b_router_expert_2"][0].partition_broadcast(P))
        small(w48[:], p["od_w_in"][0].rearrange("(c q) n -> q c n", q=P)[:, :, 2560:2608])
        wv = p["w_in_2"][0].rearrange("(c q) n -> q c n", q=P)
        small(wdf[:, :, 0:16], wv[:, :, 3072:3088])
        small(wdf[:, :, 16:24], wv[:, :, 4624:4632])
        small(bdf[:, 0:16], p["dt_bias_2"][0].partition_broadcast(P))
        small(bdf[:, 16:24], p["forget_b_2"][0].partition_broadcast(P))
        small(alog[:], p["a_log_2"][0].partition_broadcast(P))
        small(dsk[:], p["d_skip_2"][0].partition_broadcast(P))
        small(b2v[:], p["od_cmp_b2"][0, 1].partition_broadcast(NCMP))
        for i in range(2):
            small(b2k[i * HD:(i + 1) * HD, :], p["od_cmp_b2"][0, 0].rearrange("(d o) -> d o", o=1))
            small(w2c[:, :, i, :], p["od_cmp_w2"][0, 0].rearrange("(k q) d -> q k d", q=P))
        small(w2c[:, :, 2, :], p["od_cmp_w2"][0, 1].rearrange("(k q) d -> q k d", q=P))
        assert ndma[0] == NSMALL, ndma[0]

        act.wait_ge(s["cols_ready"], 3)
        a.activation(cact[:], cols[:, COL["c"]:COL["c"] + 16], ACT.Silu).then_inc(s["cact_ready"], 1)

        def trans_out(name, op):
            for k in range(TRANS[name], TRANS_END[name]):
                if k % 2 == 0:
                    act.wait_ge(s["tr_ready"], k + 1)
                    op(k - TRANS[name], B[4]).then_inc(s["tr_act"], 1)

        def modulated(shift, scale):
            def op(j, bank):
                for i in range(2):
                    c = 2 * j + i
                    ins = a.activation(hT[:, c, :], bank[:, i * T:(i + 1) * T], ACT.Identity,
                                       bias=modc[:, shift, c:c + 1], scale=modc[:, scale, c:c + 1])
                return ins
            return op

        def chunks_to(dst, c0=0):
            def op(j, bank):
                return a.copy(dst[:, c0 + 2 * j:c0 + 2 * j + 2, :], bank[:])
            return op

        def proj_out(name, j, op, n=None):
            tile_ready(act, TILE[name] + j if n is None else n)
            m = PROJ[name] + j
            op(j, B[2 * (m % 2)], B[2 * (m % 2) + 1]).then_inc(s["proj_act"], 1)

        def to_pb(j, b0, b1):
            return a.copy(pb[:, 0, 512 * j:512 * (j + 1)], b0[:])

        def attention(name):
            items = ITEMS[name]
            pending = []
            for t in range(len(items) + 3):
                if t < len(items) and items[t]["soft"] is not None:
                    u = items[t]["soft"]
                    act.wait_ge(s["max_ready"], u + 1)
                    if u >= 2:
                        if READER[u - 2] is None:
                            act.wait_ge(s["p_ready"], u)
                        else:
                            act.wait_ge(s["tr_ready"], READER[u - 2] + 1)
                    b = u % 2
                    for q in range(2):
                        sl = slice(0, P) if q == 0 else slice(P, 384)
                        ins = a.activation(Pm[:, b, sl], S_sb[:, b, sl], ACT.Exp, bias=nmx[:, b, q:q + 1],
                                           accum_out=rs[:, b, q:q + 1])
                    ins.then_inc(s["exp_done"], 1)
                if 0 <= t - 2 < len(items):
                    it = items[t - 2]
                    if it["tr"] is not None and it["tr"] % 2 == 0:
                        evacuate_p(act, it, a.copy, "tr_act")
                if 0 <= t - 3 < len(items):
                    it = items[t - 3]
                    if it["tr"] is not None and it["evac"] is not None:
                        act.wait_ge(s["pv_done"], it["pvn"] + 1)
                        a.copy(it["evac"][0], it["evac"][1]).then_inc(s["ot_out"], 1)

        def moe_act(name):
            d = MOE[name]
            n0, U, base, w = TILE[name], d["U"], d["unit"], d["width"]
            cw = 4 * d["slots"]

            def silu(u, par):
                n = n0 if isinstance(u, int) and u == 0 else 3 * u + (n0 - 1)
                act.wait_ge(tile_used, n + 2)
                a.activation(silub[par][:, 0:cw], B[4][:, 0:cw], ACT.Silu).then_inc(s["silu_done"], 1)

            def outputs(u, par):
                for h in range(2):
                    if h == 0:
                        act.wait_ge(s["ye_ready"], u + (base + 1))
                    else:
                        act.wait_ge(tile_used, 3 * u + (n0 + (3 if isinstance(u, int) and u == U - 1 else 5)))
                    a.copy(ye[par][0:w, 512 * h:512 * (h + 1)], B[7][0:w, :]).then_inc(s["ye_out"], 1)

            def weights(u, par):
                act.wait_ge(s["swT_ready"], u + (base + 1))
                a.copy(swT[par][0:w, :], B[6][0:w, 0:T]).then_inc(s["swT_out"], 1)
            silu(0, 0)
            silu(1, 1)
            outputs(0, 0)
            weights(0, 0)
            with act.Fori(0, (U - 4) // 2) as t:
                for j in range(2):
                    silu(2 * t + (2 + j), j)
                    outputs(2 * t + (1 + j), 1 - j)
                    weights(2 * t + (1 + j), 1 - j)
            for u in (U - 2, U - 1):
                silu(u, u % 2)
                outputs(u - 1, (u - 1) % 2)
                weights(u - 1, (u - 1) % 2)
            outputs(U - 1, 1)
            weights(U - 1, 1)
            i = d["idx"]
            nb = 2 if name == "moe2" else 1
            over = overflows(act, name)
            with act.If(over > 0):
                for j in range(8):
                    act.wait_ge(s[f"combT_ready{i}"], j + 1)
                    a.copy(combT[:, 2 * j:2 * j + 2, :], B[j % 4][:]).then_inc(s[f"combT_out{i}"], 1)
                with act.Fori(0, 16) as e:
                    for k in range(nb):
                        act.wait_ge(s[f"rest_inputs{i}"], e + 1)
                        a.activation(silu_all[:, 2 * k:2 * k + 2, :], B[4 + k][:], ACT.Silu).then_inc(
                            s[f"rest_silu{i}"], 1)

        trans_out("h0", modulated(0, 1))
        for j in range(6):
            proj_out("evin", j, to_pb)
        trans_out("qk0", lambda j, bank: a.copy(A[:, 2 * j:2 * j + 2, :], bank[:]))
        act.wait_ge(s["lam_sums"], 1)
        a.activation(lam[:, 2:4], lam[:, 0:2], ACT.Exp).then_inc(s["lam_exp"], 1)
        attention("att0")
        trans_out("ob", lambda j, bank: a.activation(OT[:, 4 + 2 * j:6 + 2 * j, :], bank[:], ACT.Copy, scale=subc[:, 0:1]))
        trans_out("h1", modulated(2, 3))
        routing_exp(act, "moe0")
        moe_act("moe0")
        act.wait_ge(s["moe_added"], 1)
        act.dma_start(gate1[:], p["ada_b"][1, 2048:3072].partition_broadcast(P)).then_inc(s["gate_bias"], 16)
        act.dma_start(gate2[:], p["ada_b"][1, 5120:6144].partition_broadcast(P)).then_inc(s["gate_bias"], 16)
        act.dma_start(b1c, p["od_cmp_b1"][0].partition_broadcast(60)).then_inc(s["b1_loaded"], 16)
        trans_out("h2", modulated(0, 1))

        def odd_out(j, b0, b1):
            if j < 2:
                return a.copy(pb[:, 0, 512 * j:512 * (j + 1)], b0[:])
            return odd_kv(a.copy, j, 0, b0)
        for j in range(5):
            proj_out("odin", j, odd_out)
        act.wait_ge(s["tail_ready"], 1)
        m = PROJ["odin"] + 5
        a.activation(gts[:, 0, :], B[2 * (m % 2)][:, 0:48], ACT.Sigmoid)
        a.activation(gts[:, 1, :], B[2 * (m % 2) + 1][:, 0:48], ACT.Sigmoid).then_inc(s["proj_act"], 1)
        trans_out("qkv1", lambda j, bank: a.copy(A[:, 2 * j:2 * j + 2, :], bank[:]))
        for j in range(2):
            act.wait_ge(s["hidden_biased"], j + 1)
            a.activation(cmph[:, j, :], cmph[:, j, :], GELU).then_inc(s["hidden_done"], 1)
        trans_out("cmph", lambda j, bank: a.copy(hidT_c, bank[:, 0:240]))
        act.wait_ge(s["kcmp_ready"], 1)
        a.activation(kcmpT[:], B[6][:, 0:60], ACT.Identity, bias=b2k[:, 0:1]).then_inc(s["kcmp_out"], 1)
        act.wait_ge(s["cscore_shifted"], 1)
        a.activation(pc, pc, ACT.Exp).then_inc(s["cscore_exp"], 1)
        attention("att1")
        act.wait_ge(s["proj_dve"], PROJ_DVE[PROJ["odout"] + 1])
        act.dma_start(rowp[:, 0, :], p["final_g"].partition_broadcast(P)).then_inc(s["rows_param"], 16)
        trans_out("h3", modulated(2, 3))
        routing_exp(act, "moe1")
        moe_act("moe1")
        act.wait_ge(s["moe_added"], 2)
        act.dma_start(gate1[:], p["b_mod_2"][0, 2048:3072].partition_broadcast(P)).then_inc(s["gate_bias"], 16)
        act.dma_start(gate2[:], p["b_mod_2"][0, 5120:6144].partition_broadcast(P)).then_inc(s["gate_bias"], 16)
        trans_out("h4", modulated(0, 1))
        act.wait_ge(s["dt_abs"], 1)
        a.activation(dts[:, 1], dts[:, 1], ACT.Exp).then_inc(s["dt_exp"], 1)
        act.wait_ge(s["dt_exp"], 1)
        a.activation(dts[:, 2], dts[:, 1], ACT.Ln, bias=1.0).then_inc(s["dt_ln"], 1)
        a.activation(cs[:, 3, 0:16], alog[:], ACT.Exp).then_inc(s["alog_exp"], 1)
        act.wait_ge(s["xT_padded"], 1)
        for j in range(4):
            proj_out("xbc", j, lambda j, b0, b1: a.copy(
                xT[:, 4 * j:4 * j + 2, 3:259], b0[:].rearrange("p (c t) -> p c t", t=T)))
        act.wait_ge(s["cs_ready"], 1)
        a.activation(cs[:, 1, :], B[7][:, 32:64], ACT.Exp)
        a.activation(cs[:, 2, :], B[7][:, 0:32], ACT.Exp)
        a.copy(cs[:, 0, :], B[7][:, 0:32]).then_inc(s["cs_out"], 1)
        for cc in range(16):
            act.wait_ge(s["conv_done"], cc + 1)
            a.activation(xT[:, cc, 3:259], tmp[:, cc % 2, 0:T], ACT.Silu).then_inc(s["conv_act"], 1)
        trans_out("xs", lambda j, bank: a.copy(pb[:, j // 2, 512 * (j % 2):512 * (j % 2) + 512], bank[:]))
        trans_out("btok", lambda j, bank: a.copy(Btok, bank[:]))
        for g in range(4):
            act.wait_ge(s["state_ready"], g + 1)
            a.copy(stT[:, 256 * g:256 * (g + 1)], B[2 + g % 2][:, 0:256]).then_inc(s["state_out"], 1)
        for q in range(8):
            act.wait_ge(s["seg_shifted"], q + 1)
            a.activation(mt[q % 2], mt[q % 2], ACT.Exp).then_inc(s["decay_done"], 1)
        act.wait_ge(s["xh_used"], 1)

        def silu_z(j, b0, b1):
            a.activation(pb[:, 0, 512 * j:512 * j + 512], b0[:], ACT.Silu)
            return a.activation(pb[:, 1, 512 * j:512 * j + 512], b1[:], ACT.Silu)
        for j in range(2):
            proj_out("z", j, silu_z)

        def gated_out(j, bank):
            for i in range(2):
                c = 2 * j + i
                ins = a.activation(OT[:, c, :], bank[:, i * T:(i + 1) * T], ACT.Copy,
                                   scale=col("ssd_norm_w_2", c))
            return ins
        trans_out("gated", gated_out)
        for j in range(2):
            proj_out("ssdo", j, lambda j, b0, b1: a.copy(pb[:, 0, 2048 + 512 * j:2560 + 512 * j], b0[:]))
        for j in range(3):
            proj_out("qkv", j, to_pb)
        trans_out("qk2", lambda j, bank: a.copy(A[:, 2 * j:2 * j + 2, :], bank[:]))
        attention("att2")
        for j in range(2):
            proj_out("atto", j, to_pb, n=TILE["atto"])

        def sigmoid_gate(j, b0, b1):
            if j < 2:
                dst = [pb[:, tt, 1024 + 512 * j:1536 + 512 * j] for tt in range(TT)]
            else:
                dst = [satt[:, tt, 512 * (j - 2):512 * (j - 1)] for tt in range(TT)]
            a.activation(dst[0], b0[:], ACT.Sigmoid)
            return a.activation(dst[1], b1[:], ACT.Sigmoid)
        for j in range(4):
            proj_out("gates", j, sigmoid_gate)
        trans_out("merged", lambda j, bank: a.copy(OT[:, 2 * j:2 * j + 2, :], bank[:]))
        act.wait_ge(s["final_scaled"], 1)
        act.dma_start(rowp[:, 0, :], p["ln1_g_2"][0].partition_broadcast(P)).then_inc(s["rows_param"], 16)
        act.dma_start(rowp[:, 1, :], p["ln1_b_2"][0].partition_broadcast(P)).then_inc(s["rows_param"], 16)
        trans_out("h5", modulated(2, 3))
        act.wait_ge(s["ln_scaled"], 1)
        act.dma_start(rowp[:, 0, :], p["ln2_g_2"][0].partition_broadcast(P)).then_inc(s["rows_param"], 16)
        act.dma_start(rowp[:, 1, :], p["ln2_b_2"][0].partition_broadcast(P)).then_inc(s["rows_param"], 16)
        routing_exp(act, "moe2")
        moe_act("moe2")

    @block.vector
    def _(dve):
        v = nc.vector
        steps = [0]

        def step(ins):
            steps[0] += 1
            ins.then_inc(s["dve_step"], 1)
            dve.wait_ge(s["dve_step"], steps[0])

        def trans_out(name, op):
            for k in range(TRANS[name], TRANS_END[name]):
                if k % 2 == 1:
                    dve.wait_ge(s["tr_ready"], k + 1)
                    op(k - TRANS[name], B[5]).then_inc(s["tr_dve"], 1)

        def modulated(shift, scale):
            def op(j, bank):
                for i in range(2):
                    c = 2 * j + i
                    ins = v.tensor_scalar(hT[:, c, :], bank[:, i * T:(i + 1) * T], modc[:, scale, c:c + 1],
                                          modc[:, shift, c:c + 1], ALU.mult, ALU.add)
                return ins
            return op

        def proj_out(name, j, op, n=None):
            tile_ready(dve, TILE[name] + j if n is None else n)
            m = PROJ[name] + j
            op(j, B[2 * (m % 2)], B[2 * (m % 2) + 1]).then_inc(s["proj_dve"], 1)

        def to_pb(j, b0, b1):
            return v.tensor_copy(pb[:, 1, 512 * j:512 * (j + 1)], b1[:])

        evals = [0]

        def scale_factor(src, eps, center):
            for tt in range(TT):
                for h in range(2):
                    ins = v.bn_stats(stats[:, tt, h, :], src[:, tt, 512 * h:512 * (h + 1)])
            step(ins)
            for tt in range(TT):
                ins = v.bn_aggr(mv[:, tt, :], stats[:, tt].rearrange("p a b -> p (a b)"))
            step(ins)
            if center:
                var = mv[:, :, 1]
            else:
                step(v.tensor_tensor(rstd[:], mv[:, :, 0], mv[:, :, 0], ALU.mult))
                step(v.tensor_tensor(rstd[:], rstd[:], mv[:, :, 1], ALU.add))
                var = rstd[:]
            v.tensor_scalar(rstd[:], var, eps, None, ALU.add).then_inc(s["var_ready"], 1)
            evals[0] += 1
            dve.wait_ge(s["pow_done"], evals[0])

        def normalise(dst, src, eps, center):
            scale_factor(src, eps, center)
            for tt in range(TT):
                if center:
                    ins = v.tensor_scalar(dst[:, tt, :], src[:, tt, :], mv[:, tt, 0:1], rstd[:, tt:tt + 1],
                                          ALU.subtract, ALU.mult)
                else:
                    ins = v.tensor_scalar(dst[:, tt, :], src[:, tt, :], rstd[:, tt:tt + 1], None, ALU.mult)
            return ins

        def modulation(i, name, bias, bias0, gain, gain0, one):
            for j in range(12):
                kind, half = j // 2, j % 2
                tile_ready(dve, TILE[name] + j)
                bank = B[j % 4]
                if kind in (2, 5):
                    gate = gate1 if kind == 2 else gate2
                    if j == 4:
                        dve.wait_ge(s["gate_bias"], 32 * (i + 1))
                    gs = gate[:, 512 * half:512 * (half + 1)]
                    v.scalar_tensor_tensor(gs, bank[:], one, gs, ALU.add, ALU.add).then_inc(s["ada_out"], 1)
                    continue
                dst = modc[:, {0: 0, 1: 1, 3: 2, 4: 3}[kind], 4 * half:4 * half + 4]
                t = tmp[:, j % 2, :].rearrange("p (a b) -> p a b", b=P)
                v.tensor_tensor(t, bank[:].rearrange("p (a b) -> p a b", b=P), bc(ident[:], 1, [P, 4, P]),
                                ALU.mult).then_inc(s["ada_out"], 1)
                dve.wait_ge(s["ada_out"], 12 * i + j + 1)
                step(v.tensor_reduce(dst, t, AX.X, ALU.add))
                step(v.tensor_tensor(dst, dst, col(bias, bias0 + 8 * kind + 4 * half, 4), ALU.add))
                if kind in (1, 4):
                    if gain is None:
                        step(v.tensor_scalar(dst, dst, 1.0, None, ALU.add))
                    else:
                        step(v.scalar_tensor_tensor(dst, dst, 1.0,
                                                    col(gain[kind // 4], gain0 + 4 * half, 4), ALU.add, ALU.mult))
            v.memset(mark[:, 1:2], 0.0).then_inc(s["mod_ready"], 1)

        def attention(name):
            items = ITEMS[name]
            for t in range(len(items) + 3):
                if t < len(items) and items[t]["soft"] is not None:
                    u = items[t]["soft"]
                    b = u % 2
                    dve.wait_ge(s["s_ready"], u + 1)
                    if u >= 2:
                        dve.wait_ge(s["exp_done"], u - 1)
                    v.scalar_tensor_tensor(S_sb[:, b, :], B[6 + b][:, 0:384], SCALE, mask384[:], ALU.mult,
                                           ALU.add).then_inc(s["s_masked"], 1)
                    dve.wait_ge(s["s_masked"], u + 1)
                    v.tensor_reduce(nmx[:, b, 0:1], S_sb[:, b, 0:P], AX.X, ALU.max, negate=True)
                    v.tensor_reduce(nmx[:, b, 1:2], S_sb[:, b, P:384], AX.X, ALU.max,
                                    negate=True).then_inc(s["max_ready"], 1)
                if 0 <= t - 1 < len(items) and items[t - 1]["soft"] is not None:
                    it = items[t - 1]
                    u = it["soft"]
                    b = u % 2
                    dve.wait_ge(s["exp_done"], u + 1)
                    step(v.reciprocal(rr[:, b, :], rs[:, b, :]))
                    if it["gate"] is not None:
                        h, branch = it["gate"]
                        step(v.tensor_tensor(rr[:, b, :], rr[:, b, :], gts[:, :, 3 * h + branch], ALU.mult))
                    if it["kind"] == "map1":
                        step(v.tensor_scalar(rr[:, b, :], rr[:, b, :], lam[:, 4:5], None, ALU.mult))
                    for q in range(2):
                        sl = slice(0, P) if q == 0 else slice(P, 384)
                        if it["kind"] == "map1":
                            ins = v.scalar_tensor_tensor(Pm[:, b, sl], Pm[:, b, sl], rr[:, b, q:q + 1],
                                                         Pm[:, 1 - b, sl], ALU.mult, ALU.add)
                        else:
                            ins = v.tensor_scalar(Pm[:, b, sl], Pm[:, b, sl], rr[:, b, q:q + 1], None, ALU.mult)
                    ins.then_inc(s["p_ready"], 1)
                    if it["kind"] == "map0":
                        dve.wait_ge(s["p_ready"], u + 1)
                if 0 <= t - 2 < len(items):
                    it = items[t - 2]
                    if it["tr"] is not None and it["tr"] % 2 == 1:
                        evacuate_p(dve, it, v.tensor_copy, "tr_dve")

        def residual(name, gate, alpha=None):
            for j in range(2):
                def op(j, b0, b1):
                    gs = gate[:, 512 * j:512 * (j + 1)]
                    for tt, bank in enumerate((b0, b1)):
                        step(v.tensor_tensor(tmp[:, tt, :], bank[:], gs, ALU.mult))
                        xs = x[:, tt, 512 * j:512 * (j + 1)]
                        if alpha is None:
                            ins = v.tensor_tensor(xs, xs, tmp[:, tt, :], ALU.add)
                        else:
                            ins = v.scalar_tensor_tensor(xs, xs, alpha, tmp[:, tt, :], ALU.mult, ALU.add)
                    return ins
                proj_out(name, j, op)
            dve.wait_ge(s["proj_dve"], PROJ_DVE[PROJ[name] + 1])

        def first_of_max(dst, vals, m, n):
            step(v.tensor_reduce(m, vals, AX.X, ALU.max))
            step(v.tensor_tensor(dst, vals, bc(m, 3, [P, TT, n, 4]), ALU.is_equal))
            step(v.tensor_tensor(dst, dst, first[:].unsqueeze(1).unsqueeze(1).broadcast_to([P, TT, n, 4]), ALU.mult))
            step(v.tensor_reduce(rt[:, :, 15, 0:n], dst, AX.X, ALU.max))
            step(v.tensor_tensor(dst, dst, bc(rt[:, :, 15, 0:n], 3, [P, TT, n, 4]), ALU.is_equal))

        def selection(name):
            return pb[:, :, D:D + 16 * MOE[name]["slots"]]

        def routing(name):
            i = MOE[name]["idx"]
            dve.wait_ge(s["router_ready"], i + 1)
            lg = rt[:, :, 8:13, :]
            for tt in range(TT):
                ins = v.tensor_tensor(lg[:, tt].rearrange("p a b -> p (a b)"), B[7][:, 32 * tt:32 * tt + 20],
                                      br[i][:], ALU.add)
            ins.then_inc(s["router_out"], 1)
            dve.wait_ge(s["router_out"], i + 1)
            m1, m2 = rt[:, :, 7, 0:1], rt[:, :, 7, 1:2]
            gl = rt[:, :, 8:9, :]
            goh = rt[:, :, 2:3, :]
            first_of_max(goh, gl, m1, 1)
            step(v.tensor_tensor(rt[:, :, 0:1, :], gl, bc(m1, 3, [P, TT, 1, 4]), ALU.subtract))
            prod = rt[:, :, 9:13, :]
            step(v.tensor_tensor(prod, prod, bc(rt[:, :, 2, :], 3, [P, TT, 4, 4]), ALU.mult))
            el = rt[:, :, 3:4, :]
            step(v.tensor_reduce(rt[:, :, 3, :], prod.rearrange("p t g e -> p t e g"), AX.X, ALU.add))
            first_of_max(rt[:, :, 4:5, :], el, m1, 1)
            for tt in range(TT):
                ins = v.scalar_tensor_tensor(rt[:, tt, 6, :], rt[:, tt, 4, :], NEG, rt[:, tt, 3, :], ALU.mult, ALU.add)
            step(ins)
            first_of_max(rt[:, :, 5:6, :], rt[:, :, 6:7, :], m2, 1)
            step(v.memset(rt[:, :, 1, :], 0.0))
            step(v.tensor_tensor(rt[:, :, 1, 0:1], m2, m1, ALU.subtract))
            v.memset(mark[:, 1:2], 0.0).then_inc(s["route_shifted"], 1)
            dve.wait_ge(s["route_exp"], i + 1)
            step(v.tensor_reduce(rt[:, :, 7, 0:1], rt[:, :, 0:1, :], AX.X, ALU.add))
            step(v.tensor_scalar(rt[:, :, 7, 1:2], rt[:, :, 1, 0:1], 1.0, None, ALU.add))
            step(v.reciprocal(rt[:, :, 7, 0:2], rt[:, :, 7, 0:2]))
            step(v.tensor_tensor(rt[:, :, 7, 2:3], rt[:, :, 7, 0:1], rt[:, :, 7, 1:2], ALU.mult))
            step(v.tensor_tensor(rt[:, :, 7, 3:4], rt[:, :, 7, 2:3], rt[:, :, 1, 0:1], ALU.mult))
            step(v.tensor_tensor(rt[:, :, 4, :], rt[:, :, 4, :], rt[:, :, 7, 2:3].broadcast_to([P, TT, 4]), ALU.mult))
            step(v.tensor_tensor(rt[:, :, 5, :], rt[:, :, 5, :], rt[:, :, 7, 3:4].broadcast_to([P, TT, 4]), ALU.mult))
            step(v.tensor_tensor(rt[:, :, 4, :], rt[:, :, 4, :], rt[:, :, 5, :], ALU.add))
            v.tensor_tensor(comb[:].rearrange("p t (g e) -> p t g e", g=4), bc(rt[:, :, 2, :], 3, [P, TT, 4, 4]),
                            bc(rt[:, :, 4, :], 2, [P, TT, 4, 4]), ALU.mult).then_inc(s["comb_ready"], 1)
            dve.wait_ge(s["comb_ready"], i + 1)
            v.tensor_scalar(chosen[:], comb[:], 0.0, None, ALU.is_gt).then_inc(s["chosen_ready"], 1)
            dve.wait_ge(s["chosen_ready"], i + 1)
            dve.wait_ge(s["place_ready"], i + 1)
            n = MOE[name]["slots"]
            step(v.tensor_tensor(place[:].rearrange("p a e -> p (a e)"), B[7][:, 0:32],
                                 chosen[:].rearrange("p a e -> p (a e)"), ALU.mult))
            for tt in range(TT):
                v.tensor_tensor(selection(name)[:, tt].rearrange("p (e k) -> p e k", k=n),
                                bc(place[:, tt, :], 2, [P, 16, n]), bc(slot_no[:, 0:n], 1, [P, 16, n]),
                                ALU.is_equal).then_inc(s["selected"], 1)
            step(v.tensor_reduce(count[:, 0:1], B[7][:, 32:48], AX.X, ALU.max))
            v.tensor_scalar(flag[:, i:i + 1], count[:, 0:1], float(n), None, ALU.is_gt).then_inc(s["flag_ready"], 1)

        def experts(name, gate, alpha=None):
            d = MOE[name]
            i, n0, U, base, w, n = d["idx"], TILE[name], d["U"], d["unit"], d["width"], d["slots"]
            cw = 4 * n
            shift, scale = 2, 3

            def gathered(u, par):
                for g in range(2):
                    dve.wait_ge(s["gather_ready"], 2 * u + (d["ga"] + g + 1))
                    for c in range(4):
                        cc = 4 * g + c
                        ins = v.tensor_scalar(hg[par][:, cc * w:(cc + 1) * w], B[6][:, c * w:(c + 1) * w],
                                              modc[:, scale, cc:cc + 1], modc[:, shift, cc:cc + 1], ALU.mult, ALU.add)
                    ins.then_inc(s["gathered"], 1)

            def hidden(u, par):
                dve.wait_ge(s["silu_done"], u + (base + 1))
                v.tensor_tensor(hidb[par][:, 0:cw], silub[par][:, 0:cw], B[5][:, 0:cw],
                                ALU.mult).then_inc(s["hid_done"], 1)

            def weighted(u, par):
                sel = selection(name)
                if isinstance(u, int):
                    su, cu = sel[:, :, w * u:w * (u + 1)], comb[:, :, d["eu"] * u:d["eu"] * (u + 1)]
                else:
                    su, cu = sel[:, :, bass.ds(w * u, w)], comb[:, :, bass.ds(d["eu"] * u, d["eu"])]
                for tt in range(TT):
                    ins = v.tensor_tensor(swb[par][:, tt, 0:w].rearrange("p (e k) -> p e k", k=n),
                                          su[:, tt].rearrange("p (e k) -> p e k", k=n),
                                          bc(cu[:, tt], 2, [P, d["eu"], n]), ALU.mult)
                ins.then_inc(s["sw_ready"], 1)

            gathered(0, 0)
            hidden(0, 0)
            gathered(1, 1)
            weighted(0, 0)
            hidden(1, 1)
            gathered(2, 0)
            with dve.Fori(0, (U - 4) // 2) as t:
                for j in range(2):
                    weighted(2 * t + (1 + j), 1 - j)
                    hidden(2 * t + (2 + j), j)
                    gathered(2 * t + (3 + j), 1 - j)
            weighted(U - 3, 1)
            hidden(U - 2, 0)
            gathered(U - 1, 1)
            weighted(U - 2, 0)
            hidden(U - 1, 1)
            weighted(U - 1, 1)
            dve.wait_ge(s["moe_summed"], i + 1)
            for tt in range(TT):
                for h in range(2):
                    step(v.tensor_tensor(tmp[:, h, :], B[2 * tt + h][:], gate[:, 512 * h:512 * (h + 1)], ALU.mult))
                    xs = x[:, tt, 512 * h:512 * (h + 1)]
                    if alpha is None:
                        ins = v.tensor_tensor(xs, xs, tmp[:, h, :], ALU.add)
                    else:
                        ins = v.scalar_tensor_tensor(xs, xs, alpha, tmp[:, h, :], ALU.mult, ALU.add)
            ins.then_inc(s["moe_main"], 1)
            dve.wait_ge(s["moe_main"], i + 1)
            large = name == "moe2"
            over = overflows(dve, name)
            with dve.If(over > 0):
                v.tensor_scalar(chosen[:].rearrange("p a e -> p (a e)"), place[:].rearrange("p a e -> p (a e)"),
                                float(n), None, ALU.is_gt).then_inc(s[f"rest_step{i}"], 1)
                dve.wait_ge(s[f"rest_step{i}"], 1)
                v.tensor_tensor(comb[:], comb[:], chosen[:], ALU.mult).then_inc(s[f"rest_start{i}"], 1)
                dve.wait_ge(s[f"combT_out{i}"], 8)
                nb = 2 if large else 1
                with dve.Fori(0, 16) as e:
                    for k in range(nb):
                        dve.wait_ge(s[f"rest_silu{i}"], nb * e + (k + 1))
                        sil = silu_all[:, 2 * k:2 * k + 2, :]
                        v.tensor_tensor(sil, sil, B[6 + k][:].rearrange("p (c t) -> p c t", t=T),
                                        ALU.mult).then_inc(s[f"rest_up{i}"], 1)
                        dve.wait_ge(s[f"rest_up{i}"], nb * e + (k + 1))
                        ins = v.tensor_tensor(hid_all[:, 2 * k:2 * k + 2, :], sil,
                                              combT[:, bass.ds(e, 1), :].broadcast_to([P, 2, T]), ALU.mult)
                    ins.then_inc(s[f"rest_hid{i}"], 1)
                dve.wait_ge(s[f"rest_summed{i}"], 1)
                for tt in range(TT):
                    for h in range(2):
                        v.tensor_tensor(tmp[:, h, :], B[2 * tt + h][:], gate[:, 512 * h:512 * (h + 1)],
                                        ALU.mult).then_inc(s[f"rest_step{i}"], 1)
                        dve.wait_ge(s[f"rest_step{i}"], 2 + 2 * tt + h)
                        xs = x[:, tt, 512 * h:512 * (h + 1)]
                        v.tensor_tensor(xs, xs, tmp[:, h, :], ALU.add).then_inc(s[f"rest_added{i}"], 1)
                dve.wait_ge(s[f"rest_added{i}"], 4)
            v.memset(mark[:, 3:4], 0.0).then_inc(s["moe_added"], 1)

        def gain_bias(rows, bias):
            dve.wait_ge(s["rows_param"], 16 * rows)
            for tt in range(TT):
                ins = v.tensor_tensor(x[:, tt, :], x[:, tt, :], rowp[:, 0, :], ALU.mult)
            step(ins)
            if bias:
                for tt in range(TT):
                    ins = v.tensor_tensor(x[:, tt, :], x[:, tt, :], rowp[:, 1, :], ALU.add)
                step(ins)

        dve.wait_ge(s["constants"], 1)
        for t in range(3):
            dve.wait_ge(s["cols_transposed"], t + 1)
            n = (P, P, 57)[t]
            v.tensor_copy(cols[:, P * t:P * t + n], B[4 + t][:, 0:n]).then_inc(s["cols_ready"], 1)

        dve.wait_ge(s["x_loaded"], 16)
        normalise(pb[:, :, 0:D], x[:], RMS_EPS, False).then_inc(s["xn_ready"], 1)
        dve.wait_ge(s["small_loads"], 16 * NSMALL)
        step(v.tensor_tensor(lamrow[:, 0:2, :], lamrow[:, 0::2, :], lamrow[:, 1::2, :], ALU.mult))
        v.tensor_reduce(lam[:, 0:2], lamrow[:, 0:2, :], AX.X, ALU.add).then_inc(s["lam_sums"], 1)
        dve.wait_ge(s["cols_ready"], 3)
        v.tensor_scalar(subc[:], col("ev_subln_g"), 1.0 - LAMBDA_INIT, None, ALU.mult)
        modulation(0, "ada0", "ada_b", 0, ("norm1_g", "norm2_g"), 0, 0.0)
        trans_out("h0", modulated(0, 1))
        for j in range(6):
            proj_out("evin", j, to_pb)
        trans_out("qk0", lambda j, bank: v.tensor_copy(A[:, 2 * j:2 * j + 2, :], bank[:]))
        dve.wait_ge(s["lam_exp"], 1)
        step(v.tensor_tensor(lam[:, 4:5], lam[:, 3:4], lam[:, 2:3], ALU.subtract))
        step(v.tensor_scalar(lam[:, 4:5], lam[:, 4:5], LAMBDA_INIT, None, ALU.subtract))
        attention("att0")
        dve.wait_ge(s["ot_out"], 8)
        ob = pb[:, :, 0:512]
        step(v.tensor_tensor(tmp[:], ob, ob, ALU.mult))
        step(v.tensor_reduce(obs[:].rearrange("p (a h) -> p a h", a=TT),
                             tmp[:].rearrange("p a (h e) -> p a h e", e=P), AX.X, ALU.add))
        v.tensor_scalar(obs[:], obs[:], 1.0 / P, RMS_EPS, ALU.mult, ALU.add).then_inc(s["var_ready"], 1)
        evals[0] += 1
        dve.wait_ge(s["pow_done"], evals[0])
        obh = ob.rearrange("p a (h e) -> p a h e", e=P)
        v.tensor_tensor(obh, obh, bc(obs[:].rearrange("p (a h) -> p a h", a=TT), 3, [P, TT, 4, P]),
                        ALU.mult).then_inc(s["ob_ready"], 1)
        trans_out("ob", lambda j, bank: v.tensor_scalar(OT[:, 4 + 2 * j:6 + 2 * j, :],
                                                        bank[:].rearrange("p (c t) -> p c t", t=T),
                                                        subc[:, 0:1], None, ALU.mult))
        residual("evout", gate1)
        normalise(pb[:, :, 0:D], x[:], RMS_EPS, False).then_inc(s["xn_ready"], 1)
        trans_out("h1", modulated(2, 3))
        routing("moe0")
        experts("moe0", gate2)
        normalise(pb[:, :, 0:D], x[:], RMS_EPS, False).then_inc(s["xn_ready"], 1)
        modulation(1, "ada1", "ada_b", 48, ("norm1_g", "norm2_g"), 8, 0.0)
        trans_out("h2", modulated(0, 1))

        def odd_out(j, b0, b1):
            if j < 2:
                return v.tensor_copy(pb[:, 1, 512 * j:512 * (j + 1)], b1[:])
            return odd_kv(v.tensor_copy, j, 1, b1)
        for j in range(5):
            proj_out("odin", j, odd_out)
        v.memset(mark[:, 1:2], 0.0).then_inc(s["proj_dve"], 1)
        trans_out("qkv1", lambda j, bank: v.tensor_copy(A[:, 2 * j:2 * j + 2, :], bank[:]))
        stage_transposed(dve, "qkv1")
        for kv in range(2):
            for par in range(2):
                rows = slice(par * HD, (par + 1) * HD)
                for g in range(4):
                    src = A[rows, 8 + 4 * kv + g, :]
                    for half in range(2):
                        sv = src[:, 16 * half:16 * half + 16 * NCMP].rearrange(
                            "p (n l e) -> p e l n", e=2, l=8)[:, par]
                        pos = bc(cols[rows, COL["pos"] + 16 * kv + 8 * half:COL["pos"] + 16 * kv + 8 * half + 8],
                                 2, [HD, 8, NCMP])
                        ins = v.tensor_tensor(cmpB[rows, kv, 8 * half:8 * half + 8, g, :], sv, pos, ALU.add)
            ins.then_inc(s["blocks_ready"], 1)
        dve.wait_ge(s["b1_loaded"], 16)
        for kv in range(2):
            tile_ready(dve, TILE["cmp"] + kv)
            v.tensor_tensor(cmph[:, kv, :], B[kv][0:60, 0:256], b1c[:, kv, :], ALU.add).then_inc(s["hidden_biased"], 1)
        dve.wait_ge(s["vcmp_ready"], 1)
        v.tensor_tensor(vcmp[:], B[7][0:NCMP, 0:256].rearrange("p (g d) -> p g d", g=4),
                        bc(b2v[:], 1, [NCMP, 4, HD]), ALU.add).then_inc(s["vcmp_out"], 1)
        dve.wait_ge(s["cscore_ready"], 1)
        pc3 = pc.rearrange("p (b n) -> p b n", n=NCMP)
        for tt in range(TT):
            for par in range(2):
                ins = v.scalar_tensor_tensor(
                    pc3[:, 16 * tt + par:16 * tt + 16:2],
                    B[6 + par][:, 120 * tt:120 * tt + 120].rearrange("p (h n) -> p h n", n=NCMP), SCALE,
                    bc(maskc[:, tt, :], 1, [P, 8, NCMP]), ALU.mult, ALU.add)
        ins.then_inc(s["cscore_out"], 1)
        dve.wait_ge(s["cscore_out"], 1)
        step(v.tensor_reduce(cs[:, 0, :], pc3, AX.X, ALU.max))
        v.tensor_tensor(pc3, pc3, bc(cs[:, 0, :], 2, [P, 32, NCMP]), ALU.subtract).then_inc(s["cscore_shifted"], 1)
        dve.wait_ge(s["cscore_exp"], 1)
        step(v.tensor_reduce(cs[:, 1, :], pc3, AX.X, ALU.add))
        step(v.reciprocal(cs[:, 1, :], cs[:, 1, :]))
        for tt in range(TT):
            ins = v.scalar_tensor_tensor(cs[:, 2, 16 * tt:16 * tt + 16], gts[:, tt, 0::3], cmp_live[:, tt:tt + 1],
                                         cs[:, 1, 16 * tt:16 * tt + 16], ALU.mult, ALU.mult)
        step(ins)
        v.tensor_tensor(pc3, pc3, bc(cs[:, 2, :], 2, [P, 32, NCMP]), ALU.mult).then_inc(s["pc_ready"], 1)
        attention("att1")
        residual("odout", gate1)
        normalise(pb[:, :, 0:D], x[:], RMS_EPS, False).then_inc(s["xn_ready"], 1)
        trans_out("h3", modulated(2, 3))
        routing("moe1")
        experts("moe1", gate2)
        step(normalise(x, x, RMS_EPS, False))
        gain_bias(1, False)
        v.memset(mark[:, 1:2], 0.0).then_inc(s["final_scaled"], 1)
        normalise(pb[:, :, 0:D], x[:], LN_EPS, True).then_inc(s["xn_ready"], 1)
        modulation(2, "ada2", "b_mod_2", 0, None, 0, 1.0)
        trans_out("h4", modulated(0, 1))
        dve.wait_ge(s["dt_ready"], 1)
        for tt in range(TT):
            ins = v.tensor_tensor(dts[:, 0, tt, :], B[6][:, 32 * tt:32 * tt + 24], bdf[:], ALU.add)
        step(ins)
        step(v.tensor_scalar(dts[:, 0, :, 16:24], dts[:, 0, :, 16:24], -1.0, None, ALU.mult))
        step(v.scalar_tensor_tensor(dts[:, 1], dts[:, 0], -1.0, dts[:, 0], ALU.mult, ALU.max))
        v.tensor_scalar(dts[:, 1], dts[:, 1], -1.0, None, ALU.mult).then_inc(s["dt_abs"], 1)
        v.memset(xT[:, :, 0:3], 0.0).then_inc(s["xT_padded"], 1)
        dve.wait_ge(s["dt_ln"], 1)
        step(v.scalar_tensor_tensor(dts[:, 3], dts[:, 0], 0.0, dts[:, 2], ALU.max, ALU.add))
        dve.wait_ge(s["alog_exp"], 1)
        for tt in range(TT):
            v.scalar_tensor_tensor(dts[:, 4, tt, 0:16], dts[:, 3, tt, 0:16], -1.0, cs[:, 3, 0:16],
                                   ALU.mult, ALU.mult)
        v.tensor_scalar(dts[:, 5, :, 16:24], dts[:, 3, :, 16:24], 1.0 / SCALE, None,
                        ALU.mult).then_inc(s["a_ready"], 1)
        for j in range(4):
            proj_out("xbc", j, lambda j, b0, b1: v.tensor_copy(
                xT[:, 4 * j + 2:4 * j + 4, 3:259], b1[:].rearrange("p (c t) -> p c t", t=T)))
        proj_evacuated(dve, PROJ["xbc"] + 3)
        for cc in range(16):
            acc = tmp[:, cc % 2, 0:T]
            if cc >= 2:
                dve.wait_ge(s["conv_act"], cc - 1)
            step(v.tensor_scalar(acc, xT[:, cc, 3:259], col("conv_w_2", 48 + cc), col("conv_b_2", cc),
                                 ALU.mult, ALU.add))
            for k in (2, 1):
                step(v.scalar_tensor_tensor(acc, xT[:, cc, k:k + T], col("conv_w_2", 16 * k + cc), acc,
                                            ALU.mult, ALU.add))
            v.scalar_tensor_tensor(acc, xT[:, cc, 0:T], col("conv_w_2", cc), acc, ALU.mult,
                                   ALU.add).then_inc(s["conv_done"], 1)
        trans_out("xs", lambda j, bank: v.tensor_copy(pb[:, j // 2, 512 * (j % 2):512 * (j % 2) + 512], bank[:]))
        trans_out("btok", lambda j, bank: v.tensor_copy(Btok, bank[:]))
        stage_transposed(dve, "xs")
        dve.wait_ge(s["cs_out"], 1)
        for tt in range(TT):
            xh = pb[:, tt, 0:D].rearrange("p (h e) -> p h e", e=HD)
            v.tensor_tensor(pb[:, tt, 2 * D:3 * D].rearrange("p (h e) -> p h e", e=HD), xh,
                            bc(dsk[:], 2, [P, 16, HD]), ALU.mult)
            ins = v.tensor_tensor(pb[:, tt, D:2 * D].rearrange("p (h e) -> p h e", e=HD), xh,
                                  bc(dts[:, 3, tt, 0:16], 2, [P, 16, HD]), ALU.mult)
        ins.then_inc(s["xh_used"], 1)
        dve.wait_ge(s["xh_used"], 1)
        v.tensor_tensor(xdte.rearrange("p (h e) -> p h e", e=HD),
                        pb[:, 0, D:2 * D].rearrange("p (h e) -> p h e", e=HD),
                        bc(cs[:, 1, 0:16], 2, [P, 16, HD]), ALU.mult).then_inc(s["xdt_ready"], 1)
        for q in range(9):
            if q < 8:
                tt, g = q // 4, q % 4
                dve.wait_ge(s["seg_ready"], q + 1)
                m3 = mt[q % 2].rearrange("p (r l) -> p r l", r=4)
                if q >= 2:
                    dve.wait_ge(s["y_ready"], q - 1)
                v.tensor_tensor(m3, B[6 + q % 2][:].rearrange("p (r l) -> p r l", r=4),
                                bc(maskT[:], 1, [P, 4, P]), ALU.add).then_inc(s["seg_out"], 1)
                dve.wait_ge(s["seg_out"], q + 1)
                v.tensor_tensor(m3, m3, bc(cs[:, 0, 16 * tt + 4 * g:16 * tt + 4 * g + 4], 2, [P, 4, P]),
                                ALU.subtract).then_inc(s["seg_shifted"], 1)
            if q >= 1:
                r = q - 1
                tt, g = r // 4, r % 4
                ys = pb[:, tt, 2 * D + 256 * g:2 * D + 256 * (g + 1)]
                m3 = mt[r % 2].rearrange("p (r l) -> p r l", r=4)
                dve.wait_ge(s["decay_done"], r + 1)
                v.tensor_tensor(m3, m3, bc(B[r % 2][:, 0:P], 1, [P, 4, P]), ALU.mult).then_inc(s["m_ready"], 1)
                dve.wait_ge(s["y_ready"], r + 1)
                bank = B[2 + r % 2]
                step(v.tensor_tensor(ys, ys, bank[:, 0:256], ALU.add))
                if tt == 1:
                    step(v.tensor_tensor(tmp[:, 0, 0:256].rearrange("p (r e) -> p r e", e=HD),
                                         bank[:, 256:512].rearrange("p (r e) -> p r e", e=HD),
                                         bc(cs[:, 2, 16 + 4 * g:20 + 4 * g], 2, [P, 4, HD]), ALU.mult))
                    step(v.tensor_tensor(ys, ys, tmp[:, 0, 0:256], ALU.add))
                v.memset(mark[:, 1:2], 0.0).then_inc(s["y_out"], 1)
        yv = pb[:, :, 2 * D:3 * D]
        dve.wait_ge(s["proj_act"], PROJ_ACT[PROJ["z"] + 1])
        step(v.tensor_tensor(yv, yv, pb[:, :, 0:D], ALU.mult))
        normalise(yv, yv, LN_EPS, False).then_inc(s["gated_ready"], 1)

        def gated_out(j, bank):
            for i in range(2):
                c = 2 * j + i
                ins = v.tensor_scalar(OT[:, c, :], bank[:, i * T:(i + 1) * T], col("ssd_norm_w_2", c), None,
                                      ALU.mult)
            return ins
        trans_out("gated", gated_out)
        for j in range(2):
            proj_out("ssdo", j, lambda j, b0, b1: v.tensor_copy(pb[:, 1, 2048 + 512 * j:2560 + 512 * j], b1[:]))
        for j in range(3):
            proj_out("qkv", j, to_pb)
        trans_out("qk2", lambda j, bank: v.tensor_copy(A[:, 2 * j:2 * j + 2, :], bank[:]))
        attention("att2")
        for j in range(2):
            proj_out("atto", j, to_pb, n=TILE["atto"])
        proj_evacuated(dve, PROJ["gates"] + 3)
        mg = pb[:, :, D:2 * D]
        v.tensor_tensor(mg, mg, pb[:, :, 2 * D:3 * D], ALU.mult)
        step(v.tensor_tensor(satt, satt, pb[:, :, 0:D], ALU.mult))
        v.tensor_tensor(mg, mg, satt, ALU.add).then_inc(s["merged_ready"], 1)
        trans_out("merged", lambda j, bank: v.tensor_copy(OT[:, 2 * j:2 * j + 2, :], bank[:]))
        residual("wo", gate1, ALPHA)
        step(normalise(x, x, LN_EPS, True))
        gain_bias(3, True)
        v.memset(mark[:, 1:2], 0.0).then_inc(s["ln_scaled"], 1)
        normalise(pb[:, :, 0:D], x[:], LN_EPS, True).then_inc(s["xn_ready"], 1)
        trans_out("h5", modulated(2, 3))
        routing("moe2")
        experts("moe2", gate2, ALPHA)
        step(normalise(x, x, LN_EPS, True))
        gain_bias(5, True)
        v.memset(mark[:, 2:3], 0.0).then_inc(s["result"], 1)

    @block.tensor
    def _(pe):
        mm = nc.tensor.matmul

        def transposes(name, sources):
            for k in range(TRANS[name], TRANS_END[name]):
                if k >= 2:
                    trans_evacuated(pe, k - 2)
                for dst, src in sources(k - TRANS[name], B[4 + k % 2]):
                    n = src.shape[0]
                    ins = nc.tensor.transpose(dst, src, ident[0:n, 0:n])
                ins.then_inc(s["tr_ready"], 1)

        def from_tokens(src, column=lambda c: P * c):
            def sources(j, bank):
                return [(bank[:, i * T + tt * P:i * T + (tt + 1) * P],
                         src[:, tt, column(2 * j + i):column(2 * j + i) + P]) for i in range(2) for tt in range(TT)]
            return sources

        def landed_tile(n):
            pe.wait_ge(landed[n % NSLOT], LANDED[n])
            return ring[n % NSLOT][:].rearrange("p (c n) -> p c n", n=512)

        def bank_pair_free(m):
            if m >= 2:
                proj_evacuated(pe, m - 2)

        def project(name, tiles, lhs):
            for j in range(tiles):
                m = PROJ[name] + j
                w = landed_tile(TILE[name] + j)
                if j >= 2:
                    bank_pair_free(m)
                for tt in range(TT):
                    for c in range(C):
                        ins = mm(B[2 * (m % 2) + tt][:], lhs[:, c, tt * P:(tt + 1) * P], w[:, c, :],
                                 start=c == 0, stop=c == C - 1)
                ins.then_inc(tile_used, 1)

        def modulation(name, i, i0):
            for j in range(12):
                w = landed_tile(TILE[name] + j)
                if j >= 4:
                    pe.wait_ge(s["ada_out"], 12 * i + j - 3)
                for c in range(C):
                    ins = mm(B[j % 4][:], cact[:, i0 + c:i0 + c + 1].broadcast_to([P, P]), w[:, c, :],
                             start=c == 0, stop=c == C - 1)
                ins.then_inc(tile_used, 1)

        def attention(name):
            items = ITEMS[name]
            for t in range(len(items) + 2):
                if t < len(items) and items[t]["soft"] is not None:
                    it = items[t]
                    u = it["soft"]
                    bank = B[6 + u % 2]
                    if u >= 2:
                        pe.wait_ge(s["s_masked"], u - 1)
                    q, k, f = it["q"], it["k"], it["forget"]
                    ins = mm(bank[:, 0:P], q[:, 0:P], k[:, 0:P], start=True, stop=f is None)
                    if f is not None:
                        fb = [dts[:, 5, tt, 16 + f:17 + f].broadcast_to([P, P]) for tt in range(TT)]
                        mm(bank[:, 0:P], fb[0], tri, start=False, stop=True)
                    ins = mm(bank[:, P:384], q[:, P:T], k[:, 0:T], start=True, stop=f is None)
                    if f is not None:
                        mm(bank[:, P:384], fb[0], tri_one[:], start=False, stop=False)
                        ins = mm(bank[:, T:384], fb[1], tri, start=False, stop=True)
                    ins.then_inc(s["s_ready"], 1)
                if 0 <= t - 1 < len(items) and items[t - 1]["tr"] is not None:
                    it = items[t - 1]
                    k = it["tr"]
                    bank = B[4 + k % 2]
                    trans_evacuated(pe, k - 2)
                    if it["kind"] == "cmp":
                        pe.wait_ge(s["pc_ready"], 1)
                        for tt in range(TT):
                            src = pc[:, (16 * tt + it["h"]) * NCMP:(16 * tt + it["h"] + 1) * NCMP]
                            ins = nc.tensor.transpose(bank[0:NCMP, tt * P:(tt + 1) * P], src, ident[:])
                    else:
                        pe.wait_ge(s["p_ready"], it["soft"] + 1)
                        for j in range(3):
                            ins = nc.tensor.transpose(bank[:, j * P:(j + 1) * P],
                                                      Pm[:, it["soft"] % 2, j * P:(j + 1) * P], ident[:])
                    ins.then_inc(s["tr_ready"], 1)
                if 0 <= t - 2 < len(items) and items[t - 2]["tr"] is not None:
                    it = items[t - 2]
                    k = it["tr"]
                    trans_evacuated(pe, k)
                    if it["ot_first"] and it["ot"] >= 2:
                        pe.wait_ge(s["ot_out"], it["ot"] - 1)
                    for dst, lhs, rhs, start, stop in it["pv"](PT[:, k % 2, :]):
                        ins = mm(dst, lhs, rhs, start=start, stop=stop)
                    ins.then_inc(s["pv_done"], 1)

        def experts(name, hname):
            d = MOE[name]
            i, n0, U = d["idx"], TILE[name], d["U"]
            large = name == "moe2"
            stage_transposed(pe, hname)
            if i == 0:
                pe.wait_ge(s["small_loads"], 16 * NSMALL)
            for tt in range(TT):
                for c in range(C):
                    ins = mm(B[7][:, 32 * tt:32 * tt + 20], hT[:, c, tt * P:(tt + 1) * P], wr[i][:, c, :],
                             start=c == 0, stop=c == C - 1)
            ins.then_inc(s["router_ready"], 1)

            sel = pb[:, :, D:D + 16 * d["slots"]]
            base, w, n, eu = d["unit"], d["width"], d["slots"], d["eu"]

            def landed_at(n_static, turn):
                slot = n_static % NSLOT
                if isinstance(turn, int):
                    pe.wait_ge(landed[slot], LANDED[n_static + 6 * turn])
                else:
                    per = LANDED[n_static + 6] - LANDED[n_static]
                    pe.wait_ge(landed[slot], turn * per + LANDED[n_static])
                return ring[slot][:]

            def inputs(n_tile, turn, u, par, first_unit=False):
                pe.wait_ge(s["gathered"], 2 * u + (d["ga"] + 2))
                if not first_unit:
                    pe.wait_ge(s["hid_done"], u + base)
                h3 = hg[par][:, 0:C * w].rearrange("p (c k) -> p c k", c=C)
                for b in range(2):
                    ws = landed_at(n_tile + b, turn)
                    if large:
                        wv = ws.rearrange("p (c f) -> p c f", f=512)
                        parts = [(B[4 + b], k, wv[:, :, k * P:(k + 1) * P], h3) for k in range(4)]
                    else:
                        wv = ws.rearrange("p (g c f) -> p g c f", g=2, f=256)
                        parts = [(B[4 + g], 2 * b + k, wv[:, g, :, k * P:(k + 1) * P], h3[:, :, n * b:n * (b + 1)])
                                 for g in range(2) for k in range(2)]
                    for bank, k, lhs, rhs in parts:
                        for c in range(C):
                            ins = mm(bank[:, k * n:(k + 1) * n], lhs[:, c, :], rhs[:, c, :],
                                     start=c == 0, stop=c == C - 1)
                    ins.then_inc(tile_used, 1)

            def gather(u, g, any_before=True):
                if g == 0 and any_before:
                    if not (isinstance(u, int) and u + base == 2):
                        pe.wait_ge(s["swT_out"], u + (base - 2))
                elif not (isinstance(u, int) and 2 * u + d["ga"] + g == 0):
                    pe.wait_ge(s["gathered"], 2 * u + (d["ga"] + g))
                su = sel[:, :, w * u:w * (u + 1)] if isinstance(u, int) else sel[:, :, bass.ds(w * u, w)]
                for c in range(4):
                    cc = 4 * g + c
                    for tt in range(TT):
                        ins = mm(B[6][:, c * w:(c + 1) * w], xn[:, tt, cc * P:(cc + 1) * P], su[:, tt, :],
                                 start=tt == 0, stop=tt == TT - 1)
                ins.then_inc(s["gather_ready"], 1)

            def down(n_tile, turn, u, par, h):
                ws = landed_at(n_tile, turn).rearrange("p (k m) -> p k m", m=D)
                if h == 0:
                    pe.wait_ge(s["hid_done"], u + (base + 1))
                if not (isinstance(u, int) and u == 0 and h == 0 and base == 0):
                    pe.wait_ge(s["ye_out"], 2 * u + (2 * base + h))
                for k in range(4 // eu):
                    for b in range(eu):
                        kk = k if large else 2 * b + k
                        ins = mm(B[7][n * b:n * (b + 1), :], hidb[par][:, kk * n:(kk + 1) * n],
                                 ws[:, kk, 512 * h:512 * (h + 1)], start=k == 0, stop=k == 4 // eu - 1)
                ins.then_inc(tile_used if h else s["ye_ready"], 1)

            def weights(u, par):
                pe.wait_ge(s["sw_ready"], u + (base + 1))
                for tt in range(TT):
                    ins = nc.tensor.transpose(B[6][0:w, tt * P:(tt + 1) * P], swb[par][:, tt, 0:w], ident[:])
                ins.then_inc(s["swT_ready"], 1)

            def scatter(u, par, last=False):
                pe.wait_ge(s["ye_out"], 2 * u + (2 * base + 2))
                pe.wait_ge(s["swT_out"], u + (base + 1))
                for tt in range(TT):
                    for h in range(2):
                        ins = mm(B[2 * tt + h][:], swT[par][0:w, tt * P:(tt + 1) * P],
                                 ye[par][0:w, 512 * h:512 * (h + 1)], start=False, stop=last)
                if last:
                    ins.then_inc(s["moe_summed"], 1)

            def turn_step(n_tile, turn, u, par, gather_next=True, before=True, scatter_old=True):
                inputs(n_tile, turn, u, par)
                if gather_next:
                    gather(u + 1, 0)
                down(n_tile + 2, turn, u - 1, 1 - par, 0)
                if gather_next:
                    gather(u + 1, 1)
                down(n_tile + 2, turn, u - 1, 1 - par, 1)
                if scatter_old:
                    scatter(u - 2, par)
                if gather_next:
                    pe.wait_ge(s["gathered"], 2 * u + (d["ga"] + 4))
                else:
                    pe.wait_ge(s["swT_out"], u + (base - 1))
                weights(u - 1, 1 - par)

            pe.wait_ge(s["chosen_ready"], i + 1)
            mm(B[7][:, 0:16], tri, chosen[:, 0, :], start=True, stop=True)
            ones = tri_one[:, P:T]
            mm(B[7][:, 16:32], ones, chosen[:, 0, :], start=True, stop=False)
            mm(B[7][:, 16:32], tri, chosen[:, 1, :], start=False, stop=True)
            mm(B[7][:, 32:48], ones, chosen[:, 0, :], start=True, stop=False)
            mm(B[7][:, 32:48], ones, chosen[:, 1, :], start=False, stop=True).then_inc(s["place_ready"], 1)
            for b in range(4):
                mm(B[b][:], zeros[:], bc(ident[:], 1, [P, 4, P]), start=True, stop=False)
            pe.wait_ge(s["selected"], 2 * (i + 1))
            pe.wait_ge(s["flag_ready"], i + 1)
            gather(0, 0, False)
            gather(0, 1)
            inputs(n0, 0, 0, 0, True)
            gather(1, 0, False)
            gather(1, 1)
            turn_step(unit_tile(n0, 1), 0, 1, 1, scatter_old=False)
            with pe.Fori(0, (U - 4) // 2) as t:
                for j in range(2):
                    turn_step(unit_tile(n0, 2 + j), t, 2 * t + (2 + j), j)
            turn_step(unit_tile(n0, U - 2), 0, U - 2, 0)
            turn_step(unit_tile(n0, U - 1), 0, U - 1, 1, gather_next=False)
            for h in range(2):
                down(unit_tile(n0, U - 1) + 3, 0, U - 1, 1, h)
            scatter(U - 2, 0)
            pe.wait_ge(s["swT_out"], base + U - 1)
            weights(U - 1, 1)
            scatter(U - 1, 1, last=True)

            over = overflows(pe, name)
            with pe.If(over > 0):
                pe.wait_ge(s[f"rest_start{i}"], 1)
                for j in range(8):
                    if j >= 4:
                        pe.wait_ge(s[f"combT_out{i}"], j - 3)
                    for a in range(2):
                        for tt in range(TT):
                            ins = mm(B[j % 4][:, a * T + tt * P:a * T + (tt + 1) * P],
                                     comb[:, tt, 2 * j + a:2 * j + a + 1].broadcast_to([P, P]), ident[:],
                                     start=True, stop=True)
                    ins.then_inc(s[f"combT_ready{i}"], 1)
                pe.wait_ge(s[f"combT_out{i}"], 8)
                for b in range(4):
                    ins = mm(B[b][:], zeros[:], bc(ident[:], 1, [P, 4, P]), start=True, stop=False)
                ins.then_inc(s[f"rest_used{i}"], 1)
                F = 512 if large else 256
                with pe.Fori(0, 16) as e:
                    pe.wait_ge(s[f"rest_landed{i}"], 48 * e + 48)
                    for slot in range(2):
                        wv = ring[slot][:, 0:C * F].rearrange("p (c f) -> p c f", f=F)
                        for k in range(F // P):
                            bank = B[4 + 2 * slot + k // 2]
                            for c in range(C):
                                ins = mm(bank[:, (k % 2) * T:(k % 2 + 1) * T], wv[:, c, k * P:(k + 1) * P],
                                         hT[:, c, :], start=c == 0, stop=c == C - 1)
                    ins.then_inc(s[f"rest_inputs{i}"], 1)
                    pe.wait_ge(s[f"rest_hid{i}"], e + 1)
                    wd = ring[2][:, 0:F // P * D].rearrange("p (k m) -> p k m", m=D)
                    for tt in range(TT):
                        for h in range(2):
                            for k in range(F // P):
                                ins = mm(B[2 * tt + h][:], hid_all[:, k, tt * P:(tt + 1) * P],
                                         wd[:, k, 512 * h:512 * (h + 1)], start=False, stop=False)
                    ins.then_inc(s[f"rest_used{i}"], 1)
                for b in range(4):
                    ins = mm(B[b][:], zeros[:], bc(ident[:], 1, [P, 4, P]), start=False, stop=True)
                ins.then_inc(s[f"rest_summed{i}"], 1)

        pe.wait_ge(s["constants"], 1)
        pe.wait_ge(s["rows_loaded"], 16 * len(colrows))
        for t in range(3):
            rows = (P, P, 57)[t]
            nc.tensor.transpose(B[4 + t][:, 0:rows], stage[0:rows, t, 0:P],
                                ident[0:rows, 0:rows]).then_inc(s["cols_transposed"], 1)

        pe.wait_ge(s["cact_ready"], 1)
        modulation("ada0", 0, 0)
        pe.wait_ge(s["mod_ready"], 1)
        pe.wait_ge(s["xn_ready"], 1)
        xn = pb[:, :, 0:D]
        transposes("h0", from_tokens(xn))
        stage_transposed(pe, "h0")
        project("evin", 6, hT)
        pe.wait_ge(s["roped"], 4)
        transposes("qk0", from_tokens(pb, lambda c: P * c if c < 8 else 1536 + P * (c - 8)))
        stage_transposed(pe, "qk0")
        proj_evacuated(pe, PROJ["evin"] + 5)
        attention("att0")
        pe.wait_ge(s["ob_ready"], 1)
        transposes("ob", from_tokens(pb))
        stage_transposed(pe, "ob")
        pe.wait_ge(s["ot_out"], 8)
        project("evout", 2, OT)
        pe.wait_ge(s["xn_ready"], 2)
        transposes("h1", from_tokens(xn))
        experts("moe0", "h1")
        pe.wait_ge(s["moe_added"], 1)
        modulation("ada1", 1, 0)
        pe.wait_ge(s["mod_ready"], 2)
        pe.wait_ge(s["xn_ready"], 3)
        transposes("h2", from_tokens(xn))
        stage_transposed(pe, "h2")
        project("odin", 5, hT)
        m = PROJ["odin"] + 5
        bank_pair_free(m)
        for tt in range(TT):
            for c in range(C):
                ins = mm(B[2 * (m % 2) + tt][:, 0:48], hT[:, c, tt * P:(tt + 1) * P], w48[:, c, :],
                         start=c == 0, stop=c == C - 1)
        ins.then_inc(s["tail_ready"], 1)
        pe.wait_ge(s["roped"], 9)
        proj_evacuated(pe, PROJ["odin"] + 5)
        transposes("qkv1", from_tokens(pb))
        for kv in range(2):
            n = TILE["cmp"] + kv
            pe.wait_ge(landed[n % NSLOT], LANDED[n])
            pe.wait_ge(s["blocks_ready"], kv + 1)
            w = ring[n % NSLOT][:].rearrange("p (c f) -> p c f", f=256)
            for l in range(16):
                ins = mm(B[kv][0:60, 0:256], cmpB[:, kv, l].rearrange("p g n -> p (g n)"), w[:, l, :],
                         start=l == 0, stop=l == 15)
            ins.then_inc(tile_used, 1)
        pe.wait_ge(s["hidden_done"], 2)
        transposes("cmph", lambda j, bank: [(bank[:, 60 * (2 * kv + k):60 * (2 * kv + k + 1)],
                                             cmph[:, kv, k * P:(k + 1) * P]) for kv in range(2) for k in range(2)])
        stage_transposed(pe, "cmph")
        hT4 = hidT_c.rearrange("p (v k g n) -> p v k g n", v=2, k=2, g=4)
        for k in range(2):
            ins = mm(B[6][:, 0:60], w2c[:, k, 0:2, :].rearrange("p e d -> p (e d)"),
                     hT4[:, 0, k].rearrange("p g n -> p (g n)"), start=k == 0, stop=k == 1)
        ins.then_inc(s["kcmp_ready"], 1)
        for g in range(4):
            for k in range(2):
                ins = mm(B[7][0:NCMP, g * HD:(g + 1) * HD], hT4[:, 1, k, g, :], w2c[:, k, 2, :],
                         start=k == 0, stop=k == 1)
        ins.then_inc(s["vcmp_ready"], 1)
        pe.wait_ge(s["kcmp_out"], 1)
        pe.wait_ge(s["vcmp_out"], 1)
        for tt in range(TT):
            for h in range(16):
                rows = slice((h % 2) * HD, (h % 2 + 1) * HD)
                slot = 8 * tt + h // 2
                ins = mm(B[6 + h % 2][:, slot * NCMP:(slot + 1) * NCMP],
                         A[rows, h // 2, tt * P:(tt + 1) * P], kcmpT[rows, (h // 4) * NCMP:(h // 4 + 1) * NCMP],
                         start=True, stop=True)
        ins.then_inc(s["cscore_ready"], 1)
        pe.wait_ge(s["cscore_out"], 1)
        attention("att1")
        pe.wait_ge(s["ot_out"], 16)
        project("odout", 2, OT)
        pe.wait_ge(s["xn_ready"], 4)
        transposes("h3", from_tokens(xn))
        experts("moe1", "h3")
        pe.wait_ge(s["moe_added"], 2)
        modulation("ada2", 2, C)
        pe.wait_ge(s["mod_ready"], 3)
        pe.wait_ge(s["xn_ready"], 5)
        transposes("h4", from_tokens(xn))
        stage_transposed(pe, "h4")
        for tt in range(TT):
            for c in range(C):
                ins = mm(B[6][:, 32 * tt:32 * tt + 24], hT[:, c, tt * P:(tt + 1) * P], wdf[:, c, :],
                         start=c == 0, stop=c == C - 1)
        ins.then_inc(s["dt_ready"], 1)
        for j in range(4):
            m = PROJ["xbc"] + j
            w = landed_tile(TILE["xbc"] + j)
            if j >= 2:
                bank_pair_free(m)
            for a in range(4):
                for c in range(C):
                    ins = mm(B[2 * (m % 2) + a // 2][:, (a % 2) * T:(a % 2 + 1) * T], w[:, c, a * P:(a + 1) * P],
                             hT[:, c, :], start=c == 0, stop=c == C - 1)
            ins.then_inc(tile_used, 1)
        pe.wait_ge(s["a_ready"], 1)
        for tt in range(TT):
            mm(B[7][:, 16 * tt:16 * tt + 16], tri, dts[:, 4, tt, 0:16], start=True, stop=True)
            ins = mm(B[7][:, 32 + 16 * tt:48 + 16 * tt], tri_gt[:], dts[:, 4, tt, 0:16], start=True, stop=True)
        ins.then_inc(s["cs_ready"], 1)
        pe.wait_ge(s["conv_act"], 16)
        transposes("xs", lambda j, bank: [(bank[:, P * a:P * (a + 1)],
                                           xT[:, 4 * (j % 2) + a, 3 + P * (j // 2):3 + P * (j // 2 + 1)])
                                          for a in range(4)])
        transposes("btok", lambda j, bank: [(bank[:, P * g:P * (g + 1)], xT[:, 8 + g, 3:3 + P]) for g in range(4)])
        stage_transposed(pe, "btok")
        pe.wait_ge(s["xdt_ready"], 1)
        pe.wait_ge(s["cs_out"], 1)
        for g in range(4):
            if g >= 2:
                pe.wait_ge(s["state_out"], g - 1)
            mm(B[2 + g % 2][:, 0:256], Btok[:, P * g:P * (g + 1)], xdte[:, 256 * g:256 * (g + 1)],
               start=True, stop=True).then_inc(s["state_ready"], 1)
        pe.wait_ge(s["state_out"], 4)
        for q in range(9):
            if q < 8:
                tt, g = q // 4, q % 4
                if q >= 2:
                    pe.wait_ge(s["seg_out"], q - 1)
                    pe.wait_ge(s["m_ready"], q - 1)
                for r in range(4):
                    mm(B[6 + q % 2][:, r * P:(r + 1) * P],
                       dts[:, 4, tt, 4 * g + r:4 * g + r + 1].broadcast_to([P, P]), tri, start=True, stop=True)
                tok = slice(3 + tt * P, 3 + (tt + 1) * P)
                mm(B[q % 2][:, 0:P], xT[:, 8 + g, tok], xT[:, 12 + g, tok], start=True,
                   stop=True).then_inc(s["seg_ready"], 1)
            if q >= 1:
                r0 = q - 1
                tt, g = r0 // 4, r0 % 4
                bank = B[2 + r0 % 2]
                if r0 >= 2:
                    pe.wait_ge(s["y_out"], r0 - 1)
                if tt == 1:
                    mm(bank[:, 256:512], xT[:, 12 + g, 3 + P:3 + 2 * P], stT[:, 256 * g:256 * (g + 1)],
                       start=True, stop=True)
                pe.wait_ge(s["m_ready"], r0 + 1)
                for r in range(4):
                    h = 4 * g + r
                    ins = mm(bank[:, r * HD:(r + 1) * HD], mt[r0 % 2][:, r * P:(r + 1) * P],
                             pb[:, tt, D + h * HD:D + (h + 1) * HD], start=True, stop=True)
                ins.then_inc(s["y_ready"], 1)
        pe.wait_ge(s["y_out"], 8)
        project("z", 2, hT)
        pe.wait_ge(s["gated_ready"], 1)
        transposes("gated", from_tokens(pb, lambda c: 2 * D + P * c))
        stage_transposed(pe, "gated")
        project("ssdo", 2, OT)
        bank_pair_free(PROJ["qkv"])
        bank_pair_free(PROJ["qkv"] + 1)
        project("qkv", 3, hT)
        proj_evacuated(pe, PROJ["qkv"] + 2)
        transposes("qk2", from_tokens(pb))
        stage_transposed(pe, "qk2")
        attention("att2")
        pe.wait_ge(s["ot_out"], 20)
        n = TILE["atto"]
        pe.wait_ge(landed[n % NSLOT], LANDED[n])
        w = ring[n % NSLOT][:].rearrange("p (c n) -> p c n", n=D)
        for j in range(2):
            m = PROJ["atto"] + j
            for tt in range(TT):
                for c in range(4):
                    ins = mm(B[2 * (m % 2) + tt][:], OT[:, c, tt * P:(tt + 1) * P],
                             w[:, c, 512 * j:512 * (j + 1)], start=c == 0, stop=c == 3)
        ins.then_inc(tile_used, 1)
        bank_pair_free(PROJ["gates"])
        bank_pair_free(PROJ["gates"] + 1)
        project("gates", 4, hT)
        pe.wait_ge(s["merged_ready"], 1)
        transposes("merged", from_tokens(pb, lambda c: D + P * c))
        stage_transposed(pe, "merged")
        project("wo", 2, OT)
        pe.wait_ge(s["xn_ready"], 6)
        transposes("h5", from_tokens(xn))
        experts("moe2", "h5")


_NAMES = ("x c norm1_g norm2_g final_g ada_w ada_b ev_w_in ev_w_out ev_lambda ev_subln_g od_w_in od_w_out "
          "od_cmp_pos od_cmp_w1 od_cmp_b1 od_cmp_w2 od_cmp_b2 moe_wg moe_bg moe_we moe_be moe_w_gate moe_w_up "
          "moe_w_down c_2 w_mod_2 b_mod_2 w_in_2 conv_w_2 conv_b_2 dt_bias_2 a_log_2 d_skip_2 ssd_norm_w_2 "
          "forget_b_2 w_ssd_o_2 w_att_o_2 w_o_2 ln1_g_2 ln1_b_2 w_router_group_2 b_router_group_2 "
          "w_router_expert_2 b_router_expert_2 w_gate_2 w_up_2 w_down_2 ln2_g_2 ln2_b_2").split()


def rope_table():
    inv = (np.float32(500000.0) ** (-np.arange(0, 16, 2, dtype=np.float32) / np.float32(16))).astype(np.float32)
    ang = np.arange(T, dtype=np.float32)[:, None] * inv[None, :]
    return np.stack([np.tile(np.cos(ang), (1, 2)), np.tile(np.sin(ang), (1, 2))]).astype(np.float32)


def kernel(**inputs):
    import numpy as _np
    import concourse.bacc as _bacc
    from concourse import mybir as _mybir
    from concourse.bass_utils import run_bass_kernel_spmd as _run

    nc = _bacc.Bacc("TRN2", target_bir_lowering=False, num_devices=1)
    arrays, params = {}, {}
    for name in _NAMES:
        a = _np.ascontiguousarray(inputs[name])
        arrays[f"in_{name}"] = a
        params[name] = nc.dram_tensor(f"in_{name}", a.shape, _mybir.dt.from_np(a.dtype), kind="ExternalInput").ap()
    table = rope_table()
    arrays["rope_table"] = table
    rope = nc.dram_tensor("rope_table", table.shape, _mybir.dt.float32, kind="ExternalInput").ap()
    out = nc.dram_tensor("out_0", (1, T, D), _mybir.dt.float32, kind="ExternalOutput").ap()
    two_blocks(nc, params, rope, out)
    r = _run(nc, [arrays], core_ids=[0])
    return r.results[0]["out_0"]
```

```python
import math
from contextlib import ExitStack

import numpy as np

import concourse.bass as bass
from concourse import mybir

F32 = mybir.dt.float32
ALU = mybir.AluOpType
ACT = mybir.ActivationFunctionType
AX = mybir.AxisListType

P = 128
T = 256
TT = T // P
D = 1024
C = D // P
HD = 64
HALF_ROPE = 8
SCALE = HD ** -0.5
NEG = -1e30
RMS_EPS = 1e-6
LN_EPS = 1e-5
ALPHA = 2 ** 0.25
LAMBDA_INIT = 0.8 - 0.6 * math.exp(0.0)
NSLOT = 6
SLOT = 4096
NSMALL = 28
NCMP = (T - 32) // 16 + 1
GELU = ACT.Gelu_apprx_tanh

PHASES = [("mod_a", 4), ("evin", 6), ("mod_b", 12), ("evout", 2), ("moe0", 24),
          ("odin", 5), ("cmp", 2), ("mod_c", 20), ("odout", 2), ("moe1", 24),
          ("xbc", 4), ("z", 2), ("qkv", 3), ("ssdo", 2), ("gates", 4), ("atto", 1),
          ("wo", 2), ("moe2", 48)]
TILE = {}
_n = 0
for _name, _k in PHASES:
    TILE[_name] = _n
    _n += _k
NTILES = _n
LOADS_PER_TILE = {}
for _n in range(NTILES):
    LOADS_PER_TILE[_n] = 1
for _moe in ("moe0", "moe1"):
    _u = 8
    for _n in range(TILE[_moe], TILE[_moe] + 3 * _u):
        _r = _n - TILE[_moe]
        _down = _r == 3 * _u - 1 or (_r >= 2 and (_r - 2) % 3 == 2)
        LOADS_PER_TILE[_n] = 1 if _down else 2
for _n in range(TILE["cmp"], TILE["cmp"] + 2):
    LOADS_PER_TILE[_n] = 1
LANDED = {}
_count = [0] * NSLOT
for _n in range(NTILES):
    _count[_n % NSLOT] += 16 * LOADS_PER_TILE[_n]
    LANDED[_n] = _count[_n % NSLOT]

MOD_TILE = ([TILE["mod_a"]] + [TILE["mod_b"] + 4 * _g for _g in range(3)]
            + [TILE["mod_c"] + 4 * _g for _g in range(5)])

TRANS = {}


def unit_tile(base, u):
    return base + (3 * u - 1 if u else 0)

TRANS_STAGES = [("h0", 4), ("qk0", 8), ("att0", 12), ("ob", 2), ("h1", 4),
                ("h2", 4), ("qkv1", 12), ("cmph", 1), ("att1", 48), ("h3", 4),
                ("h4", 4), ("xs", 4), ("btok", 1), ("gated", 4), ("qk2", 4), ("att2", 8),
                ("merged", 4), ("h5", 4)]
_n = 0
for _name, _k in TRANS_STAGES:
    TRANS[_name] = _n
    _n += _k
TRANS_END = {_name: TRANS[_name] + _k for _name, _k in TRANS_STAGES}

PROJ_STAGES = [("evin", 6, 1, 1), ("evout", 2, 0, 1), ("odin", 6, 1, 1), ("odout", 2, 0, 1),
               ("xbc", 4, 1, 1), ("z", 2, 1, 0), ("ssdo", 2, 1, 1),
               ("atto", 2, 1, 1), ("wo", 2, 0, 1)]
PROJ = {}
PROJ_ACT, PROJ_DVE = [], []
for _name, _k, _a, _d in PROJ_STAGES:
    PROJ[_name] = len(PROJ_ACT)
    for _ in range(_k):
        PROJ_ACT.append((PROJ_ACT[-1] if PROJ_ACT else 0) + _a)
        PROJ_DVE.append((PROJ_DVE[-1] if PROJ_DVE else 0) + _d)

SOFT = {"att0": 0, "att1": 16, "att2": 48}
OTB = {"att0": 0, "att1": 8, "att2": 16}
NORMS = ["h0", "h1", "h2", "h3", "h4", "h5"]
COL = {}


def col_rows(params):
    out = []

    def put(name, tile, row, view):
        COL[name] = tile * P + row
        out.append((tile, row, view.shape[0], view))

    put("ada_b", 0, 0, params["ada_b"].rearrange("l (r p) -> (l r) p", p=P))
    put("norm1_g", 0, 96, params["norm1_g"].rearrange("l (r p) -> (l r) p", p=P))
    put("norm2_g", 0, 112, params["norm2_g"].rearrange("l (r p) -> (l r) p", p=P))
    put("b_mod_2", 1, 0, params["b_mod_2"].rearrange("l (r p) -> (l r) p", p=P))
    put("conv_w_2", 1, 48, params["conv_w_2"].rearrange("l k (r p) -> (l k r) p", p=P))
    put("conv_b_2", 1, 112, params["conv_b_2"].rearrange("l (r p) -> (l r) p", p=P))
    put("c", 2, 0, params["c"].rearrange("l (r p) -> (l r) p", p=P))
    put("c_2", 2, 8, params["c_2"].rearrange("l (r p) -> (l r) p", p=P))
    put("ssd_norm_w_2", 2, 16, params["ssd_norm_w_2"].rearrange("l (r p) -> (l r) p", p=P))
    put("ev_subln_g", 2, 24, params["ev_subln_g"])
    put("pos", 2, 25, params["od_cmp_pos"].rearrange("o k (r l) d -> (o k r) (l d)", l=2))
    return out


class Semaphores(dict):

    def __init__(self, nc, ctx):
        super().__init__()
        self.nc, self.ctx = nc, ctx

    def __missing__(self, name):
        self[name] = self.ctx.enter_context(self.nc.semaphore(name))
        return self[name]


def two_blocks(nc, params, rope, out):
    with ExitStack() as ctx:
        emit(nc, ctx, params, rope, out)


def emit(nc, ctx, p, rope_dram, out):
    def sb(name, shape):
        return ctx.enter_context(nc.sbuf_tensor(name, shape, F32))

    ring = [sb(f"ring{i}", [P, SLOT]) for i in range(NSLOT)]
    x = sb("x", [P, TT, D])
    hT = sb("hT", [P, C, T])
    gate1 = sb("gate1", [P, D])
    gate2 = sb("gate2", [P, D])
    PBW = 3584
    pb = sb("pb", [P, TT, PBW])
    pb_flat = pb[:].rearrange("p a b -> p (a b)")
    A = sb("A", [P, 24, T])
    A_flat = A[:].rearrange("p a b -> p (a b)")
    OT = sb("OT", [P, C, T])
    OT_flat = OT[:].rearrange("p a b -> p (a b)")
    Pm = sb("Pm", [P, 2, 384])
    PT = sb("PT", [P, 2, 384])
    tmp = sb("tmp", [P, 2, 512])
    S_sb = tmp[:, :, 0:384]
    ident = sb("ident", [P, P])
    mask384 = sb("mask384", [P, 384])
    maskT = sb("maskT", [P, P])
    tri_one = sb("tri_one", [P, T])
    tri = tri_one[:, 0:P]
    tri_gt = sb("tri_gt", [P, P])
    zeros = sb("zeros", [P, P])
    mark = sb("mark", [P, 8])
    maskc = sb("maskc", [P, TT, NCMP])
    cmp_live = sb("cmp_live", [P, TT])
    cosd = sb("cosd", [P, TT, 16])
    sind = sb("sind", [P, TT, 16])
    ropeA, ropeB = (Pm[:, i, 0:256].rearrange("p (a h d) -> p a h d", a=TT, h=8) for i in range(2))
    cols = sb("cols", [P, 3 * P])
    stage = A
    modc = sb("modc", [P, 18, C])
    cact = sb("cact", [P, 2 * C])
    stats = sb("stats", [P, TT, 2, 6])
    mv = sb("mv", [P, TT, 2])
    rstd = sb("rstd", [P, TT])
    nhalf = sb("nhalf", [P, 8])
    nmx = sb("nmx", [P, 2, 2])
    rs = sb("rs", [P, 2, 2])
    rr = sb("rr", [P, 2, 2])
    lam = sb("lam", [P, 8])
    lamrow = OT_flat[:, 0:4 * HD].rearrange("p (r d) -> p r d", r=4)
    subc = sb("subc", [P, 1])
    obs = sb("obs", [P, 8])
    wr = [sb(f"wr{i}", [P, C, 20]) for i in range(3)]
    br = [sb(f"br{i}", [P, 20]) for i in range(3)]
    w48 = A_flat[:, 4096:4096 + C * 48].rearrange("p (c n) -> p c n", c=C)
    wdf = sb("wdf", [P, C, 24])
    gts = sb("gts", [P, TT, 48])
    rt = sb("rt", [P, TT, 16, 4])
    comb = sb("comb", [P, TT, 16])
    chosen = sb("chosen", [P, TT, 16])
    place = sb("place", [P, TT, 16])
    slot_no = sb("slot_no", [P, 96])
    count = sb("count", [P, 2])
    flag = ctx.enter_context(nc.sbuf_tensor("flag", [P, 3], mybir.dt.int32))
    first = sb("first", [P, 4])
    b1c = OT_flat[0:60, 512:1024].rearrange("p (k f) -> p k f", k=2)
    b2v = sb("b2v", [NCMP, HD])
    w2c = sb("w2c", [P, 2, 3, HD])
    b2k = sb("b2k", [P, 1])
    kcmpT = sb("kcmpT", [P, 60])
    vcmp = sb("vcmp", [NCMP, 4, HD])
    cs = sb("cs", [P, 4, 32])
    dts = sb("dts", [P, 6, TT, 24])
    bdf = sb("bdf", [P, 24])
    alog = sb("alog", [P, 16])
    dsk = sb("dsk", [P, 16])
    B = [ctx.enter_context(nc.psum_tensor(f"bank{i}", [P, 512], F32)) for i in range(8)]
    s = Semaphores(nc, ctx)
    for i in range(NSLOT):
        s[f"landed{i}"]
    landed = [s[f"landed{i}"] for i in range(NSLOT)]
    tile_used = s["tile_used"]

    colrows = col_rows(p)

    def col(name, i=0, n=1):
        return cols[:, COL[name] + i:COL[name] + i + n]

    def bc(ap, axis, shape):
        return ap.unsqueeze(axis).broadcast_to(shape)

    def trans_evacuated(eng, k):
        eng.wait_ge(s["tr_act"] if k % 2 == 0 else s["tr_dve"], k // 2 + 1)

    def stage_transposed(eng, name):
        for k in (TRANS_END[name] - 2, TRANS_END[name] - 1):
            if k >= 0:
                trans_evacuated(eng, k)

    def proj_evacuated(eng, m):
        if PROJ_ACT[m]:
            eng.wait_ge(s["proj_act"], PROJ_ACT[m])
        if PROJ_DVE[m]:
            eng.wait_ge(s["proj_dve"], PROJ_DVE[m])

    def tile_ready(eng, n):
        eng.wait_ge(tile_used, n + 1)

    mod_raw = [hT[:, 2 * b:2 * b + 2, :].rearrange("p a t -> p (a t)") for b in range(2)]
    MOD_WORK = {"att0": (1, 3, 1), "att1": (4, 5, 2), "att2": None}

    def mod_tile_step(name, t):
        if MOD_WORK[name] is None:
            return None
        g0, groups, every = MOD_WORK[name]
        k, part = t // every, t % every
        return (g0 + k // 4, k % 4, range(part * C // every, (part + 1) * C // every)) if k < 4 * groups else None

    def mod_group_step(name, t, lag):
        if MOD_WORK[name] is None or t % MOD_WORK[name][2]:
            return None
        g0, groups, every = MOD_WORK[name]
        k = t // every - 4 - lag
        return g0 + k // 4 if k >= 0 and k % 4 == 0 and k < 4 * groups else None

    QKV_COL = (0, 512, 3072)

    def head(buf, chunk, half):
        return buf[half * HD:(half + 1) * HD, chunk, :]

    def attention_items(stage_name):
        items = []
        u, k, o = SOFT[stage_name], TRANS[stage_name], OTB[stage_name]

        def plain_pv(vbuf, voff, half, bank, start, stop):
            def pv(pt):
                dst = B[bank][half * HD:(half + 1) * HD, 0:T]
                v = [vbuf[:, tt, voff:voff + HD] for tt in range(TT)]
                return [(dst, v[0], pt[:, 0:T], start, False),
                        (dst[:, P:T], v[1], pt[:, T:384], False, stop)]
            return pv

        if stage_name in ("att0", "att2"):
            for h in range(8):
                ot = o + h // 2
                items.append(dict(
                    soft=u, tr=k, kind="plain", q=head(A, h // 2, h % 2), k=head(A, 4 + h // 2, h % 2),
                    pv=plain_pv(pb, (1024 if stage_name == "att0" else QKV_COL[2]) + h * HD, h % 2, ot % 2, True, True),
                    forget=h if stage_name == "att2" else None,
                    ot=ot, ot_first=h % 2 == 0,
                    evac=(OT[:, h // 2, :], B[ot % 2][:, 0:T]) if h % 2 else None, gate=None))
                u, k = u + 1, k + 1
        if stage_name == "att0":
            for h in range(4):
                for m in range(2):
                    ot = o + 4 + h

                    def pv(pt, h=h, ot=ot):
                        bank = B[ot % 2][:, 0:T]
                        v = [pb[:, tt, 2560 + h * P:2560 + (h + 1) * P] for tt in range(TT)]
                        return [(bank[:, 0:P], pt[:, 0:P], v[0], True, True),
                                (bank[:, P:T], pt[:, P:T], v[0], True, False),
                                (bank[:, P:T], pt[:, T:384], v[1], False, True)]
                    items.append(dict(
                        soft=u, tr=k if m else None, kind=f"map{m}", q=head(A, 8 + h, m), k=head(A, 12 + h, m),
                        pv=pv, forget=None, ot=ot, ot_first=True, gate=None,
                        evac=(pb[:, :, h * P:(h + 1) * P], B[ot % 2][:, 0:T].rearrange("p (a b) -> p a b", a=TT))))
                    u += 1
                k += 1
        if stage_name == "att1":
            for h in range(16):
                g = h // 4
                ot = o + h // 2
                for b, (kc0, voff) in enumerate(((16, 3072), (20, 3328))):
                    items.append(dict(
                        soft=u, tr=k, kind="plain", q=head(A, h // 2, h % 2), k=head(A, kc0 + g, h % 2),
                        pv=plain_pv(pb, voff + g * HD, h % 2, ot % 2, b == 0, False), forget=None,
                        ot=ot, ot_first=h % 2 == 0 and b == 0, gate=(h, b + 1), evac=None))
                    u, k = u + 1, k + 1

                def pv(pt, g=g, h=h, ot=ot):
                    dst = B[ot % 2][(h % 2) * HD:(h % 2 + 1) * HD, 0:T]
                    return [(dst, vcmp[:, g, :], pt[0:NCMP, 0:T], False, True)]
                items.append(dict(
                    soft=None, tr=k, kind="cmp", h=h, pv=pv, ot=ot, ot_first=False, gate=None, forget=None,
                    evac=(OT[:, h // 2, :], B[ot % 2][:, 0:T]) if h % 2 else None))
                k += 1
        return items

    ITEMS = {name: attention_items(name) for name in SOFT}
    PV_BASE = {"att0": 0, "att1": 12, "att2": 60}
    for name in SOFT:
        n = PV_BASE[name]
        for it in ITEMS[name]:
            it["pvn"] = n
            if it["tr"] is not None:
                n += 1
    ALL = [it for name in ("att0", "att1", "att2") for it in ITEMS[name]]
    READER = {it["soft"]: it["tr"] for it in ALL if it["soft"] is not None}
    ALL_TR = [it for it in ALL if it["tr"] is not None]
    PREV_PV = {}
    last_on = {}
    for it in ALL_TR:
        PREV_PV[it["tr"]] = last_on.get(it["tr"] % 2)
        last_on[it["tr"] % 2] = it["pvn"]
    OT_DONE = {}
    for it in ALL_TR:
        OT_DONE[it["ot"]] = it["pvn"] + 1

    MOE = {"moe0": dict(U=8, unit=0, ga=0, idx=0, slots=64, width=128, passes=2, eu=2),
           "moe1": dict(U=8, unit=8, ga=16, idx=1, slots=64, width=128, passes=2, eu=2),
           "moe2": dict(U=16, unit=16, ga=32, idx=2, slots=96, width=96, passes=2, eu=1)}
    hg = [A_flat[:, 1024 * b:1024 * (b + 1)] for b in range(2)]
    hidb = [A_flat[:, 2048 + 384 * b:2432 + 384 * b] for b in range(2)]
    silub = [A_flat[:, 2816 + 384 * b:3200 + 384 * b] for b in range(2)]
    swT = [A_flat[:, 3584 + T * b:3584 + T * (b + 1)] for b in range(2)]
    ye = [OT_flat[:, D * b:D * (b + 1)] for b in range(2)]
    swb = [pb[:, :, 2560 + P * b:2560 + P * (b + 1)] for b in range(2)]
    hid_all = A[:, 0:4, :]
    silu_all = A[:, 4:8, :]
    combT = pb_flat[:, 0:16 * T].rearrange("p (e t) -> p e t", e=16)
    rowp = A[:, 16:24, :].rearrange("p (r a) t -> p r (a t)", r=2)

    cmph = OT_flat[0:60, 0:512].rearrange("p (k f) -> p k f", k=2)
    hidT_c = OT_flat[:, 1024:1264]
    cmpB = pb[:, :, 0:960].rearrange("p k (l g n) -> p k l g n", l=16, g=4)
    pc = pb[:, 0, 1024:1504]
    xT = A_flat[:, 0:16 * 259].rearrange("p (c t) -> p c t", t=259)
    mt = [A_flat[:, 4144 + 512 * b:4656 + 512 * b] for b in range(2)]
    xdte = OT_flat[:, 0:D]
    stT = OT_flat[:, D:2 * D]
    Btok = pb[:, 0, 3072:3584]
    satt = A[:, 8:16, :].rearrange("p (a c) t -> p a (c t)", a=TT)

    def odd_kv(copy, j, tt, bank):
        def twice(c0, src):
            return copy(pb[:, tt, c0:c0 + 512].rearrange("p (g e d) -> p g e d", g=4, e=2),
                        bc(src.rearrange("p (g d) -> p g d", g=4), 2, [P, 4, 2, HD]))
        twice({2: 1024, 3: 2048, 4: 2560}[j], bank[:, 0:256])
        if j == 2:
            return twice(1536, bank[:, 256:512])
        return copy(pb[:, tt, 3072 + 256 * (j - 3):3328 + 256 * (j - 3)], bank[:, 256:512])

    def evacuate_p(eng, it, copy, done):
        k = it["tr"]
        eng.wait_ge(s["tr_ready"], k + 1)
        if PREV_PV[k] is not None:
            eng.wait_ge(s["pv_done"], PREV_PV[k] + 1)
        rows, width = (NCMP, T) if it["kind"] == "cmp" else (P, 384)
        copy(PT[0:rows, k % 2, 0:width], B[4 + k % 2][0:rows, 0:width]).then_inc(s[done], 1)

    def routing_exp(act, name):
        i = MOE[name]["idx"]
        act.wait_ge(s["route_shifted"], i + 1)
        nc.scalar.activation(rt[:, :, 0:2, :], rt[:, :, 0:2, :], ACT.Exp).then_inc(s["route_exp"], 1)

    def overflows(eng, name):
        i = MOE[name]["idx"]
        eng.wait_ge(s["flag_ready"], i + 1)
        return eng.value_load(flag[0:1, i:i + 1], min_val=0, max_val=1)

    block = ctx.enter_context(nc.Block())

    @block.sync
    def _(sp):
        def slot_free(n):
            if isinstance(n, int):
                if n >= NSLOT:
                    sp.wait_ge(tile_used, n - NSLOT + 1)
            else:
                sp.wait_ge(tile_used, n - (NSLOT - 1))

        def load(n, slot, view, src, wait=True):
            if wait:
                slot_free(n)
            sp.dma_start(view, src).then_inc(landed[slot], 16)

        def kview(slot, width=512):
            return ring[slot][:].rearrange("p (c n) -> p c n", n=width)

        def columns(w, n0, col0, tiles):
            for j in range(tiles):
                n = n0 + j
                load(n, n % NSLOT, kview(n % NSLOT),
                     w.rearrange("(c p) n -> p c n", p=P)[:, :, col0 + 512 * j:col0 + 512 * (j + 1)])

        def ada(n0, w):
            wv = w.rearrange("(c p) n -> p c n", p=P)
            with sp.Fori(0, 2) as i:
                for j in range(6):
                    slot = (n0 + j) % NSLOT
                    sp.wait_ge(tile_used, 6 * i + (n0 + j - NSLOT + 1))
                    sp.dma_start(kview(slot), wv[:, :, bass.ds(3072 * i + 512 * j, 512)]).then_inc(landed[slot], 16)

        def moe_small(name, wg, wu, wd):
            n0, U = TILE[name], 8
            gv = wg.rearrange("e (c p) f -> e p c f", p=P)
            uv = wu.rearrange("e (c p) f -> e p c f", p=P)
            dv = wd.rearrange("(u e) (k p) d -> u p (e k) d", p=P, e=2)

            def pick(v, i):
                return v[i] if isinstance(i, int) else v[bass.ds(i, 1)].rearrange("o p c f -> (o p) c f")

            def inputs(u, n, slots):
                for j in range(2):
                    slot = slots[j]
                    slot_free(n + j)
                    kv = ring[slot][:].rearrange("p (g c f) -> p g c f", g=2, f=256)
                    sp.dma_start(kv[:, 0], pick(gv, 2 * u + j)).then_inc(landed[slot], 16)
                    sp.dma_start(kv[:, 1], pick(uv, 2 * u + j)).then_inc(landed[slot], 16)

            def down(u, n, slot):
                slot_free(n)
                sp.dma_start(kview(slot, D), pick(dv, u)).then_inc(landed[slot], 16)
            stream(n0, U, inputs, down)

        def moe_large(name, wg, wu, wd):
            n0, U = TILE[name], 16
            gv = wg.rearrange("e (c p) f -> e p c f", p=P)
            uv = wu.rearrange("e (c p) f -> e p c f", p=P)
            dv = wd.rearrange("e (k p) d -> e p k d", p=P)

            def pick(v, i):
                return v[i] if isinstance(i, int) else v[bass.ds(i, 1)].rearrange("o p c f -> (o p) c f")

            def inputs(u, n, slots):
                for j, v in enumerate((gv, uv)):
                    slot_free(n + j)
                    sp.dma_start(kview(slots[j]), pick(v, u)).then_inc(landed[slots[j]], 16)

            def down(u, n, slot):
                slot_free(n)
                sp.dma_start(kview(slot, D), pick(dv, u)).then_inc(landed[slot], 16)
            stream(n0, U, inputs, down)

        def stream(n0, U, inputs, down):
            inputs(0, n0, [n0 % NSLOT, (n0 + 1) % NSLOT])
            with sp.Fori(0, (U - 2) // 2) as i:
                for j in range(2):
                    u = 1 + j
                    n = unit_tile(n0, u)
                    slots = [(n + a) % NSLOT for a in range(3)]
                    inputs(2 * i + u, 6 * i + n, slots)
                    down(2 * i + (u - 1), 6 * i + (n + 2), slots[2])
            u = U - 1
            n = unit_tile(n0, u)
            inputs(u, n, [n % NSLOT, (n + 1) % NSLOT])
            down(u - 1, n + 2, (n + 2) % NSLOT)
            down(u, n + 3, (n + 3) % NSLOT)

        def moe_rest(name, wg, wu, wd):
            i, n_end = MOE[name]["idx"], TILE[name] + 3 * MOE[name]["U"]
            F = wg.shape[-1]
            nk = F // P
            gv = wg.rearrange("e (c p) f -> e p c f", p=P)
            uv = wu.rearrange("e (c p) f -> e p c f", p=P)
            dv = wd.rearrange("e (k p) d -> e p k d", p=P)
            over = overflows(sp, name)
            with sp.If(over > 0):
                sp.wait_ge(tile_used, n_end)
                with sp.Fori(0, 16) as e:
                    sp.wait_ge(s[f"rest_used{i}"], e + 1)
                    for slot, v, n in ((0, gv, C), (1, uv, C), (2, dv, nk)):
                        dst = ring[slot][:, 0:n * v.shape[-1]].rearrange("p (c f) -> p c f", c=n)
                        sp.dma_start(dst, v[bass.ds(e, 1)].rearrange("o p c f -> (o p) c f")).then_inc(
                            s[f"rest_landed{i}"], 16)
                sp.wait_ge(s[f"rest_used{i}"], 17)

        for tile, row, n, view in colrows:
            sp.dma_start(stage[row:row + n, tile, 0:P], view).then_inc(s["rows_loaded"], 16)
        columns(p["ada_w"][0], TILE["mod_a"], 0, 2)
        sp.dma_start(x[:], p["x"].rearrange("b (a q) d -> q (b a) d", q=P)).then_inc(s["x_loaded"], 16)
        columns(p["ada_w"][0], TILE["mod_a"] + 2, 1024, 2)
        columns(p["ev_w_in"][0], TILE["evin"], 0, 6)
        columns(p["ada_w"][0], TILE["mod_b"], 2048, 8)
        columns(p["ada_w"][1], TILE["mod_b"] + 8, 0, 4)
        columns(p["ev_w_out"][0], TILE["evout"], 0, 2)
        moe_small("moe0", p["moe_w_gate"][0], p["moe_w_up"][0], p["moe_w_down"][0])
        moe_rest("moe0", p["moe_w_gate"][0], p["moe_w_up"][0], p["moe_w_down"][0])
        columns(p["od_w_in"][0], TILE["odin"], 0, 5)
        for j in range(2):
            n = TILE["cmp"] + j
            load(n, n % NSLOT, kview(n % NSLOT, 256), p["od_cmp_w1"][0, j].rearrange("(r p) f -> p r f", p=P))
        columns(p["ada_w"][1], TILE["mod_c"], 2048, 8)
        ada(TILE["mod_c"] + 8, p["w_mod_2"][0])
        columns(p["od_w_out"][0], TILE["odout"], 0, 2)
        moe_small("moe1", p["moe_w_gate"][1], p["moe_w_up"][1], p["moe_w_down"][1])
        moe_rest("moe1", p["moe_w_gate"][1], p["moe_w_up"][1], p["moe_w_down"][1])
        columns(p["w_in_2"][0], TILE["xbc"], 1024, 4)
        columns(p["w_in_2"][0], TILE["z"], 0, 2)
        columns(p["w_in_2"][0], TILE["qkv"], 3088, 3)
        columns(p["w_ssd_o_2"][0], TILE["ssdo"], 0, 2)
        columns(p["w_in_2"][0], TILE["gates"], 4632, 4)
        n = TILE["atto"]
        load(n, n % NSLOT, kview(n % NSLOT, D), p["w_att_o_2"][0].rearrange("(c p) n -> p c n", p=P))
        columns(p["w_o_2"][0], TILE["wo"], 0, 2)
        moe_large("moe2", p["w_gate_2"][0], p["w_up_2"][0], p["w_down_2"][0])
        moe_rest("moe2", p["w_gate_2"][0], p["w_up_2"][0], p["w_down_2"][0])
        sp.wait_ge(s["result"], 1)
        sp.dma_start(out.rearrange("b (a p) d -> p (b a) d", p=P), x[:]).then_inc(s["stored"], 16)
        sp.wait_ge(s["stored"], 16)

    @block.gpsimd
    def _(pool):
        steps = [0]

        def step(ins):
            steps[0] += 1
            ins.then_inc(s["pool_step"], 1)
            pool.wait_ge(s["pool_step"], steps[0])

        g = nc.gpsimd
        step(g.memset(ident[:], 0.0))
        step(g.affine_select(out=ident[:], in_=ident[:], compare_op=ALU.not_equal, fill=1.0, base=0,
                             pattern=[[-1, P]], channel_multiplier=1))
        g.memset(zeros[:], 0.0)
        g.iota(slot_no[:], pattern=[[1, 96]], base=1, channel_multiplier=0, allow_small_or_imprecise_dtypes=True)
        g.memset(nhalf[:], -0.5)
        g.memset(tri_one[:], 1.0)
        g.memset(tri_gt[:], 1.0)
        g.memset(maskT[:], 0.0)
        g.memset(mask384[:], 0.0)
        g.memset(maskc[:], 0.0)
        g.memset(cmp_live[:], 1.0)
        for j in range(4):
            ins = g.memset(first[:, j:j + 1], 4.0 - j)
        step(ins)
        g.affine_select(out=tri, in_=tri, compare_op=ALU.is_ge, fill=0.0, base=0,
                        pattern=[[1, P]], channel_multiplier=-1)
        g.affine_select(out=tri_gt[:], in_=tri_gt[:], compare_op=ALU.is_gt, fill=0.0, base=0,
                        pattern=[[-1, P]], channel_multiplier=1)
        g.affine_select(out=maskT[:], in_=maskT[:], compare_op=ALU.is_ge, fill=NEG, base=0,
                        pattern=[[1, P]], channel_multiplier=-1)
        for a in (0, 2 * P):
            g.affine_select(out=mask384[:, a:a + P], in_=mask384[:, a:a + P], compare_op=ALU.is_ge, fill=NEG,
                            base=0, pattern=[[-1, P]], channel_multiplier=1)
        for a in range(TT):
            g.affine_select(out=maskc[:, a, :], in_=maskc[:, a, :], compare_op=ALU.is_ge, fill=NEG,
                            base=P * a - 31, pattern=[[-16, NCMP]], channel_multiplier=1)
        step(g.affine_select(out=cmp_live[:, 0:1], in_=cmp_live[:, 0:1], compare_op=ALU.is_ge, fill=0.0,
                             base=-31, pattern=[[0, 1]], channel_multiplier=1))
        g.memset(mark[:, 0:1], 0.0).then_inc(s["constants"], 1)
        ropes = [0]

        def rope(col0, m):
            proj_evacuated(pool, m)
            t = pb[:, :, col0:col0 + 512].rearrange("p a (h d) -> p a h d", d=HD)[:, :, :, 0:16]
            cb = bc(cosd[:], 2, [P, TT, 8, 16])
            sbb = bc(sind[:], 2, [P, TT, 8, 16])
            g.tensor_tensor(ropeA[:], t, cb, ALU.mult)
            step(g.tensor_tensor(ropeB[:], t, sbb, ALU.mult))
            g.tensor_tensor(t[:, :, :, 0:8], ropeA[:, :, :, 0:8], ropeB[:, :, :, 8:16], ALU.subtract)
            step(g.tensor_tensor(t[:, :, :, 8:16], ropeA[:, :, :, 8:16], ropeB[:, :, :, 0:8], ALU.add))
            ropes[0] += 1
            g.memset(mark[:, 0:1], 0.0).then_inc(s["roped"], 1)

        powers = [0]

        def power(dst, src):
            powers[0] += 1
            pool.wait_ge(s["var_ready"], powers[0])
            g.tensor_tensor(dst, src, nhalf[:, 0:src.shape[-1]], ALU.pow).then_inc(s["pow_done"], 1)

        power(rstd[:], rstd[:])
        pool.wait_ge(s["small_loads"], 16 * NSMALL)
        for c0, j in ((0, 0), (512, 1), (1536, 3), (2048, 4)):
            rope(c0, PROJ["evin"] + j)
        power(obs[:], obs[:])
        power(rstd[:], rstd[:])
        power(rstd[:], rstd[:])
        for c0, j in ((0, 0), (512, 1), (1024, 2), (2048, 3), (2560, 4)):
            rope(c0, PROJ["odin"] + j)
        power(rstd[:], rstd[:])
        power(rstd[:], rstd[:])
        power(rstd[:], rstd[:])
        power(rstd[:], rstd[:])
        power(rstd[:], rstd[:])
        power(rstd[:], rstd[:])
        power(rstd[:], rstd[:])

    @block.scalar
    def _(act):
        a = nc.scalar
        ndma = [0]

        def small(dst, src):
            ndma[0] += 1
            act.dma_start(dst, src).then_inc(s["small_loads"], 16)

        small(cosd[:], rope_dram[0].rearrange("(a q) d -> q a d", q=P))
        small(sind[:], rope_dram[1].rearrange("(a q) d -> q a d", q=P))
        small(lamrow[:], p["ev_lambda"][0].partition_broadcast(P))
        for i in range(2):
            small(wr[i][:, :, 0:4], p["moe_wg"][i].rearrange("(c q) n -> q c n", q=P))
            small(wr[i][:, :, 4:20], p["moe_we"][i].rearrange("(c q) n -> q c n", q=P))
            small(br[i][:, 0:4], p["moe_bg"][i].partition_broadcast(P))
            small(br[i][:, 4:20], p["moe_be"][i].partition_broadcast(P))
        small(wr[2][:, :, 0:4], p["w_router_group_2"][0].rearrange("(c q) n -> q c n", q=P))
        small(wr[2][:, :, 4:20], p["w_router_expert_2"][0].rearrange("(c q) n -> q c n", q=P))
        small(br[2][:, 0:4], p["b_router_group_2"][0].partition_broadcast(P))
        small(br[2][:, 4:20], p["b_router_expert_2"][0].partition_broadcast(P))
        small(w48[:], p["od_w_in"][0].rearrange("(c q) n -> q c n", q=P)[:, :, 2560:2608])
        wv = p["w_in_2"][0].rearrange("(c q) n -> q c n", q=P)
        small(wdf[:, :, 0:16], wv[:, :, 3072:3088])
        small(wdf[:, :, 16:24], wv[:, :, 4624:4632])
        small(bdf[:, 0:16], p["dt_bias_2"][0].partition_broadcast(P))
        small(bdf[:, 16:24], p["forget_b_2"][0].partition_broadcast(P))
        small(alog[:], p["a_log_2"][0].partition_broadcast(P))
        small(dsk[:], p["d_skip_2"][0].partition_broadcast(P))
        small(b2v[:], p["od_cmp_b2"][0, 1].partition_broadcast(NCMP))
        for i in range(2):
            small(b2k[i * HD:(i + 1) * HD, :], p["od_cmp_b2"][0, 0].rearrange("(d o) -> d o", o=1))
            small(w2c[:, :, i, :], p["od_cmp_w2"][0, 0].rearrange("(k q) d -> q k d", q=P))
        small(w2c[:, :, 2, :], p["od_cmp_w2"][0, 1].rearrange("(k q) d -> q k d", q=P))
        assert ndma[0] == NSMALL, ndma[0]

        act.wait_ge(s["cols_ready"], 3)
        a.activation(cact[:], cols[:, COL["c"]:COL["c"] + 16], ACT.Silu).then_inc(s["cact_ready"], 1)

        def trans_out(name, op):
            for k in range(TRANS[name], TRANS_END[name]):
                if k % 2 == 0:
                    act.wait_ge(s["tr_ready"], k + 1)
                    op(k - TRANS[name], B[4]).then_inc(s["tr_act"], 1)

        def mod_out(G):
            tile_ready(act, MOD_TILE[G] + 3)
            a.copy(mod_raw[G % 2], B[2][:]).then_inc(s["mod_raw_out"], 1)

        def gate_rows(g):
            act.wait_ge(s["gate_spread"], g + 1)
            gate = gate2 if g % 2 else gate1
            if g >= 2 and g % 2:
                act.wait_ge(s["moe_added"], g // 2)
            elif g >= 2:
                act.wait_ge(s["proj_dve"], PROJ_DVE[PROJ["evout" if g == 2 else "odout"] + 1])
            a.copy(gate[:, 0:512], B[6][:])
            a.copy(gate[:, 512:1024], B[7][:]).then_inc(s["gate_rows"], 1)

        def modulated(layer, kind):
            shift, scale = 6 * layer + kind, 6 * layer + kind + 1

            def op(j, bank):
                if j == 0:
                    act.wait_ge(s["mod_ready"], 3 * layer + (3 if kind else 1))
                for i in range(2):
                    c = 2 * j + i
                    ins = a.activation(hT[:, c, :], bank[:, i * T:(i + 1) * T], ACT.Identity,
                                       bias=modc[:, shift, c:c + 1], scale=modc[:, scale, c:c + 1])
                return ins
            return op

        def chunks_to(dst, c0=0):
            def op(j, bank):
                return a.copy(dst[:, c0 + 2 * j:c0 + 2 * j + 2, :], bank[:])
            return op

        def proj_out(name, j, op, n=None):
            tile_ready(act, TILE[name] + j if n is None else n)
            m = PROJ[name] + j
            op(j, B[2 * (m % 2)], B[2 * (m % 2) + 1]).then_inc(s["proj_act"], 1)

        def to_pb(j, b0, b1):
            return a.copy(pb[:, 0, 512 * j:512 * (j + 1)], b0[:])

        def attention(name):
            items = ITEMS[name]
            for t in range(len(items) + 3):
                if 0 <= t - 2 < len(items):
                    it = items[t - 2]
                    if it["tr"] is not None and it["tr"] % 2 == 0:
                        evacuate_p(act, it, a.copy, "tr_act")
                if t < len(items) and items[t]["soft"] is not None:
                    u = items[t]["soft"]
                    act.wait_ge(s["max_ready"], u + 1)
                    if u >= 2:
                        if READER[u - 2] is None:
                            act.wait_ge(s["p_ready"], u)
                        else:
                            act.wait_ge(s["tr_ready"], READER[u - 2] + 1)
                    b = u % 2
                    for q in range(2):
                        sl = slice(0, P) if q == 0 else slice(P, 384)
                        ins = a.activation(Pm[:, b, sl], S_sb[:, b, sl], ACT.Exp, bias=nmx[:, b, q:q + 1],
                                           accum_out=rs[:, b, q:q + 1])
                    ins.then_inc(s["exp_done"], 1)
                if 0 <= t - 3 < len(items):
                    it = items[t - 3]
                    if it["tr"] is not None and it["evac"] is not None:
                        act.wait_ge(s["pv_done"], it["pvn"] + 1)
                        a.copy(it["evac"][0], it["evac"][1]).then_inc(s["ot_out"], 1)
                G = mod_group_step(name, t, 0)
                if G is not None:
                    mod_out(G)
                if name == "att2" and t < 8:
                    j, tt = t // 2, t % 2
                    if tt:
                        tile_ready(act, TILE["gates"] + j)
                    else:
                        act.wait_ge(s["branch_ready"], j + 1)
                    dst = (pb[:, tt, 1024 + 512 * j:1536 + 512 * j] if j < 2
                           else satt[:, tt, 512 * (j - 2):512 * (j - 1)])
                    a.activation(dst, B[2 + tt][:], ACT.Sigmoid).then_inc(s["branch_out"], 1)

        def moe_act(name):
            d = MOE[name]
            n0, U, base, w = TILE[name], d["U"], d["unit"], d["width"]
            cw = 4 * d["slots"]

            def silu(u, par):
                n = n0 if isinstance(u, int) and u == 0 else 3 * u + (n0 - 1)
                act.wait_ge(tile_used, n + 2)
                sw = cw if name == "moe2" else 256
                a.activation(silub[par][:, 0:sw], B[4][:, 0:sw], ACT.Silu).then_inc(s["silu_done"], 1)

            def outputs(u, par):
                for h in range(2):
                    if h == 0:
                        act.wait_ge(s["ye_ready"], u + (base + 1))
                    else:
                        act.wait_ge(tile_used, 3 * u + (n0 + (3 if isinstance(u, int) and u == U - 1 else 5)))
                    a.copy(ye[par][0:w, 512 * h:512 * (h + 1)], B[7][0:w, :]).then_inc(s["ye_out"], 1)

            def weights(u, par):
                act.wait_ge(s["swT_ready"], u + (base + 1))
                a.copy(swT[par][0:w, :], B[6][0:w, 0:T]).then_inc(s["swT_out"], 1)
            silu(0, 0)
            silu(1, 1)
            outputs(0, 0)
            weights(0, 0)
            with act.Fori(0, (U - 4) // 2) as t:
                for j in range(2):
                    silu(2 * t + (2 + j), j)
                    outputs(2 * t + (1 + j), 1 - j)
                    weights(2 * t + (1 + j), 1 - j)
            for u in (U - 2, U - 1):
                silu(u, u % 2)
                outputs(u - 1, (u - 1) % 2)
                weights(u - 1, (u - 1) % 2)
            outputs(U - 1, 1)
            weights(U - 1, 1)
            i = d["idx"]
            nb = 2 if name == "moe2" else 1
            over = overflows(act, name)
            with act.If(over > 0):
                for j in range(8):
                    act.wait_ge(s[f"combT_ready{i}"], j + 1)
                    a.copy(combT[:, 2 * j:2 * j + 2, :], B[j % 4][:]).then_inc(s[f"combT_out{i}"], 1)
                with act.Fori(0, 16) as e:
                    for k in range(nb):
                        act.wait_ge(s[f"rest_inputs{i}"], e + 1)
                        a.activation(silu_all[:, 2 * k:2 * k + 2, :], B[4 + k][:], ACT.Silu).then_inc(
                            s[f"rest_silu{i}"], 1)

        mod_out(0)
        trans_out("h0", modulated(0, 0))
        for j in range(6):
            proj_out("evin", j, to_pb)
        trans_out("qk0", lambda j, bank: a.copy(A[:, 2 * j:2 * j + 2, :], bank[:]))
        act.wait_ge(s["lam_sums"], 1)
        a.activation(lam[:, 2:4], lam[:, 0:2], ACT.Exp).then_inc(s["lam_exp"], 1)
        attention("att0")
        gate_rows(0)
        trans_out("ob", lambda j, bank: a.activation(OT[:, 4 + 2 * j:6 + 2 * j, :], bank[:], ACT.Copy, scale=subc[:, 0:1]))
        gate_rows(1)
        trans_out("h1", modulated(0, 3))
        routing_exp(act, "moe0")
        moe_act("moe0")
        act.wait_ge(s["moe_added"], 1)
        act.dma_start(b1c, p["od_cmp_b1"][0].partition_broadcast(60)).then_inc(s["b1_loaded"], 16)
        trans_out("h2", modulated(1, 0))

        def odd_out(j, b0, b1):
            if j < 2:
                return a.copy(pb[:, 0, 512 * j:512 * (j + 1)], b0[:])
            return odd_kv(a.copy, j, 0, b0)
        for j in range(5):
            proj_out("odin", j, odd_out)
        act.wait_ge(s["tail_ready"], 1)
        m = PROJ["odin"] + 5
        a.activation(gts[:, 0, :], B[2 * (m % 2)][:, 0:48], ACT.Sigmoid)
        a.activation(gts[:, 1, :], B[2 * (m % 2) + 1][:, 0:48], ACT.Sigmoid).then_inc(s["proj_act"], 1)
        trans_out("qkv1", lambda j, bank: a.copy(A[:, 2 * j:2 * j + 2, :], bank[:]))
        for j in range(2):
            act.wait_ge(s["hidden_biased"], j + 1)
            a.activation(cmph[:, j, :], cmph[:, j, :], GELU).then_inc(s["hidden_done"], 1)
        trans_out("cmph", lambda j, bank: a.copy(hidT_c, bank[:, 0:240]))
        act.wait_ge(s["kcmp_ready"], 1)
        a.activation(kcmpT[:], B[6][:, 0:60], ACT.Identity, bias=b2k[:, 0:1]).then_inc(s["kcmp_out"], 1)
        act.wait_ge(s["cscore_shifted"], 1)
        a.activation(pc, pc, ACT.Exp).then_inc(s["cscore_exp"], 1)
        attention("att1")
        gate_rows(2)
        gate_rows(3)
        act.wait_ge(s["proj_dve"], PROJ_DVE[PROJ["odout"] + 1])
        act.dma_start(rowp[:, 0, :], p["final_g"].partition_broadcast(P)).then_inc(s["rows_param"], 16)
        trans_out("h3", modulated(1, 3))
        routing_exp(act, "moe1")
        moe_act("moe1")
        trans_out("h4", modulated(2, 0))
        act.wait_ge(s["dt_abs"], 1)
        a.activation(dts[:, 1], dts[:, 1], ACT.Exp).then_inc(s["dt_exp"], 1)
        act.wait_ge(s["dt_exp"], 1)
        a.activation(dts[:, 2], dts[:, 1], ACT.Ln, bias=1.0).then_inc(s["dt_ln"], 1)
        a.activation(cs[:, 3, 0:16], alog[:], ACT.Exp).then_inc(s["alog_exp"], 1)
        act.wait_ge(s["xT_padded"], 1)
        for j in range(4):
            proj_out("xbc", j, lambda j, b0, b1: a.copy(
                xT[:, 4 * j:4 * j + 2, 3:259], b0[:].rearrange("p (c t) -> p c t", t=T)))
        act.wait_ge(s["cs_ready"], 1)
        a.activation(cs[:, 1, :], B[7][:, 32:64], ACT.Exp)
        a.activation(cs[:, 2, :], B[7][:, 0:32], ACT.Exp)
        a.copy(cs[:, 0, :], B[7][:, 0:32]).then_inc(s["cs_out"], 1)
        act.wait_ge(s["moe_added"], 2)

        def silu_z(j, b0, b1):
            a.activation(gate1[:, 512 * j:512 * j + 512], b0[:], ACT.Silu)
            return a.activation(gate2[:, 512 * j:512 * j + 512], b1[:], ACT.Silu)
        for cc in range(16):
            act.wait_ge(s["conv_done"], cc + 1)
            a.activation(xT[:, cc, 3:259], tmp[:, cc % 2, 0:T], ACT.Silu).then_inc(s["conv_act"], 1)
            if cc % 8 == 7:
                proj_out("z", cc // 8, silu_z)
        trans_out("xs", lambda j, bank: a.copy(pb[:, j // 2, 512 * (j % 2):512 * (j % 2) + 512], bank[:]))
        trans_out("btok", lambda j, bank: a.copy(Btok, bank[:]))
        for g in range(4):
            act.wait_ge(s["state_ready"], g + 1)
            a.copy(stT[:, 256 * g:256 * (g + 1)], B[2 + g % 2][:, 0:256]).then_inc(s["state_out"], 1)
        act.wait_ge(s["xh_used"], 1)
        for q in range(8):
            act.wait_ge(s["seg_shifted"], q + 1)
            a.activation(mt[q % 2], mt[q % 2], ACT.Exp).then_inc(s["decay_done"], 1)
            if q < 6 and q % 2 == 0:
                act.wait_ge(s["qkv_ready"], q // 2 + 1)
                c0 = QKV_COL[q // 2]
                a.copy(pb[:, 0, c0:c0 + 512], B[4][:]).then_inc(s["qkv_act"], 1)

        def gated_out(j, bank):
            for i in range(2):
                c = 2 * j + i
                ins = a.activation(OT[:, c, :], bank[:, i * T:(i + 1) * T], ACT.Copy,
                                   scale=col("ssd_norm_w_2", c))
            return ins
        trans_out("gated", gated_out)
        act.wait_ge(s["final_scaled"], 1)
        act.dma_start(rowp[:, 0, :], p["ln1_g_2"][0].partition_broadcast(P)).then_inc(s["rows_param"], 16)
        act.dma_start(rowp[:, 1, :], p["ln1_b_2"][0].partition_broadcast(P)).then_inc(s["rows_param"], 16)
        for j in range(2):
            proj_out("ssdo", j, lambda j, b0, b1: a.copy(pb[:, 0, 2048 + 512 * j:2560 + 512 * j], b0[:]))
        trans_out("qk2", lambda j, bank: a.copy(A[:, 2 * j:2 * j + 2, :], bank[:]))
        attention("att2")
        gate_rows(4)
        for j in range(2):
            proj_out("atto", j, to_pb, n=TILE["atto"])
        trans_out("merged", lambda j, bank: a.copy(OT[:, 2 * j:2 * j + 2, :], bank[:]))
        gate_rows(5)
        trans_out("h5", modulated(2, 3))
        act.wait_ge(s["ln_scaled"], 1)
        act.dma_start(rowp[:, 0, :], p["ln2_g_2"][0].partition_broadcast(P)).then_inc(s["rows_param"], 16)
        act.dma_start(rowp[:, 1, :], p["ln2_b_2"][0].partition_broadcast(P)).then_inc(s["rows_param"], 16)
        routing_exp(act, "moe2")
        moe_act("moe2")

    @block.vector
    def _(dve):
        v = nc.vector
        steps = [0]

        def step(ins):
            steps[0] += 1
            ins.then_inc(s["dve_step"], 1)
            dve.wait_ge(s["dve_step"], steps[0])

        def trans_out(name, op):
            for k in range(TRANS[name], TRANS_END[name]):
                if k % 2 == 1:
                    dve.wait_ge(s["tr_ready"], k + 1)
                    op(k - TRANS[name], B[5]).then_inc(s["tr_dve"], 1)

        def modulated(layer, kind):
            shift, scale = 6 * layer + kind, 6 * layer + kind + 1

            def op(j, bank):
                for i in range(2):
                    c = 2 * j + i
                    ins = v.tensor_scalar(hT[:, c, :], bank[:, i * T:(i + 1) * T], modc[:, scale, c:c + 1],
                                          modc[:, shift, c:c + 1], ALU.mult, ALU.add)
                return ins
            return op

        def proj_out(name, j, op, n=None):
            tile_ready(dve, TILE[name] + j if n is None else n)
            m = PROJ[name] + j
            op(j, B[2 * (m % 2)], B[2 * (m % 2) + 1]).then_inc(s["proj_dve"], 1)

        def to_pb(j, b0, b1):
            return v.tensor_copy(pb[:, 1, 512 * j:512 * (j + 1)], b1[:])

        evals = [0]

        def scale_factor(src, eps, center):
            for tt in range(TT):
                for h in range(2):
                    ins = v.bn_stats(stats[:, tt, h, :], src[:, tt, 512 * h:512 * (h + 1)])
            step(ins)
            for tt in range(TT):
                ins = v.bn_aggr(mv[:, tt, :], stats[:, tt].rearrange("p a b -> p (a b)"))
            step(ins)
            if center:
                var = mv[:, :, 1]
            else:
                step(v.tensor_tensor(rstd[:], mv[:, :, 0], mv[:, :, 0], ALU.mult))
                step(v.tensor_tensor(rstd[:], rstd[:], mv[:, :, 1], ALU.add))
                var = rstd[:]
            v.tensor_scalar(rstd[:], var, eps, None, ALU.add).then_inc(s["var_ready"], 1)
            evals[0] += 1
            dve.wait_ge(s["pow_done"], evals[0])

        def normalise(dst, src, eps, center):
            scale_factor(src, eps, center)
            for tt in range(TT):
                if center:
                    ins = v.tensor_scalar(dst[:, tt, :], src[:, tt, :], mv[:, tt, 0:1], rstd[:, tt:tt + 1],
                                          ALU.subtract, ALU.mult)
                else:
                    ins = v.tensor_scalar(dst[:, tt, :], src[:, tt, :], rstd[:, tt:tt + 1], None, ALU.mult)
            return ins

        def mod_columns(G):
            layer, third = G // 3, G % 3
            dst = modc[:, 2 * G:2 * G + 2, :].rearrange("p a b -> p (a b)")
            dve.wait_ge(s["mod_turned"], G + 1)
            bias = col("ada_b", 48 * layer + 16 * third, 16) if layer < 2 else col("b_mod_2", 16 * third, 16)
            step(v.tensor_tensor(dst, B[3][:].rearrange("p (b r) -> p b r", r=32)[:, :, 0], bias, ALU.add))
            if layer < 2:
                if third != 1:
                    kind = 2 * G + (1 if third == 0 else 0)
                    gain = col("norm1_g" if third == 0 else "norm2_g", 8 * layer, C)
                    step(v.scalar_tensor_tensor(modc[:, kind, :], modc[:, kind, :], 1.0, gain, ALU.add, ALU.mult))
            else:
                part = {0: slice(2 * G + 1, 2 * G + 2), 1: slice(2 * G, 2 * G + 1), 2: slice(2 * G, 2 * G + 2)}[third]
                step(v.tensor_scalar(modc[:, part, :], modc[:, part, :], 1.0, None, ALU.add))
            v.memset(mark[:, 1:2], 0.0).then_inc(s["mod_ready"], 1)

        def attention(name):
            items = ITEMS[name]
            for t in range(len(items) + 3):
                if 0 <= t - 2 < len(items):
                    it = items[t - 2]
                    if it["tr"] is not None and it["tr"] % 2 == 1:
                        evacuate_p(dve, it, v.tensor_copy, "tr_dve")
                if t < len(items) and items[t]["soft"] is not None:
                    u = items[t]["soft"]
                    b = u % 2
                    dve.wait_ge(s["s_ready"], u + 1)
                    if u >= 2:
                        dve.wait_ge(s["exp_done"], u - 1)
                    v.scalar_tensor_tensor(S_sb[:, b, :], B[6 + b][:, 0:384], SCALE, mask384[:], ALU.mult,
                                           ALU.add).then_inc(s["s_masked"], 1)
                    dve.wait_ge(s["s_masked"], u + 1)
                    v.tensor_reduce(nmx[:, b, 0:1], S_sb[:, b, 0:P], AX.X, ALU.max, negate=True)
                    v.tensor_reduce(nmx[:, b, 1:2], S_sb[:, b, P:384], AX.X, ALU.max,
                                    negate=True).then_inc(s["max_ready"], 1)
                if 0 <= t - 1 < len(items) and items[t - 1]["soft"] is not None:
                    it = items[t - 1]
                    u = it["soft"]
                    b = u % 2
                    dve.wait_ge(s["exp_done"], u + 1)
                    step(v.reciprocal(rr[:, b, :], rs[:, b, :]))
                    if it["gate"] is not None:
                        h, branch = it["gate"]
                        step(v.tensor_tensor(rr[:, b, :], rr[:, b, :], gts[:, :, 3 * h + branch], ALU.mult))
                    if it["kind"] == "map1":
                        step(v.tensor_scalar(rr[:, b, :], rr[:, b, :], lam[:, 4:5], None, ALU.mult))
                    for q in range(2):
                        sl = slice(0, P) if q == 0 else slice(P, 384)
                        if it["kind"] == "map1":
                            ins = v.scalar_tensor_tensor(Pm[:, b, sl], Pm[:, b, sl], rr[:, b, q:q + 1],
                                                         Pm[:, 1 - b, sl], ALU.mult, ALU.add)
                        else:
                            ins = v.tensor_scalar(Pm[:, b, sl], Pm[:, b, sl], rr[:, b, q:q + 1], None, ALU.mult)
                    ins.then_inc(s["p_ready"], 1)
                    if it["kind"] == "map0":
                        dve.wait_ge(s["p_ready"], u + 1)
                G = mod_group_step(name, t, 2)
                if G is not None:
                    mod_columns(G)

        def residual(name, gate, alpha=None):
            layer = ("evout", "odout", "wo").index(name)
            dve.wait_ge(s["gate_rows"], 2 * layer + 1)
            for j in range(2):
                def op(j, b0, b1):
                    gs = gate[:, 512 * j:512 * (j + 1)]
                    for tt, bank in enumerate((b0, b1)):
                        step(v.tensor_tensor(tmp[:, tt, :], bank[:], gs, ALU.mult))
                        xs = x[:, tt, 512 * j:512 * (j + 1)]
                        if alpha is None:
                            ins = v.tensor_tensor(xs, xs, tmp[:, tt, :], ALU.add)
                        else:
                            ins = v.scalar_tensor_tensor(xs, xs, alpha, tmp[:, tt, :], ALU.mult, ALU.add)
                    return ins
                proj_out(name, j, op)
            dve.wait_ge(s["proj_dve"], PROJ_DVE[PROJ[name] + 1])

        def first_of_max(dst, vals, m, n):
            step(v.tensor_reduce(m, vals, AX.X, ALU.max))
            step(v.tensor_tensor(dst, vals, bc(m, 3, [P, TT, n, 4]), ALU.is_equal))
            step(v.tensor_tensor(dst, dst, first[:].unsqueeze(1).unsqueeze(1).broadcast_to([P, TT, n, 4]), ALU.mult))
            step(v.tensor_reduce(rt[:, :, 15, 0:n], dst, AX.X, ALU.max))
            step(v.tensor_tensor(dst, dst, bc(rt[:, :, 15, 0:n], 3, [P, TT, n, 4]), ALU.is_equal))

        def selection(name):
            return pb[:, :, D:D + 16 * MOE[name]["slots"]]

        def routing(name):
            i = MOE[name]["idx"]
            dve.wait_ge(s["router_ready"], i + 1)
            lg = rt[:, :, 8:13, :]
            for tt in range(TT):
                ins = v.tensor_tensor(lg[:, tt].rearrange("p a b -> p (a b)"), B[7][:, 32 * tt:32 * tt + 20],
                                      br[i][:], ALU.add)
            ins.then_inc(s["router_out"], 1)
            dve.wait_ge(s["router_out"], i + 1)
            m1, m2 = rt[:, :, 7, 0:1], rt[:, :, 7, 1:2]
            gl = rt[:, :, 8:9, :]
            goh = rt[:, :, 2:3, :]
            first_of_max(goh, gl, m1, 1)
            step(v.tensor_tensor(rt[:, :, 0:1, :], gl, bc(m1, 3, [P, TT, 1, 4]), ALU.subtract))
            prod = rt[:, :, 9:13, :]
            step(v.tensor_tensor(prod, prod, bc(rt[:, :, 2, :], 3, [P, TT, 4, 4]), ALU.mult))
            el = rt[:, :, 3:4, :]
            step(v.tensor_reduce(rt[:, :, 3, :], prod.rearrange("p t g e -> p t e g"), AX.X, ALU.add))
            first_of_max(rt[:, :, 4:5, :], el, m1, 1)
            for tt in range(TT):
                ins = v.scalar_tensor_tensor(rt[:, tt, 6, :], rt[:, tt, 4, :], NEG, rt[:, tt, 3, :], ALU.mult, ALU.add)
            step(ins)
            first_of_max(rt[:, :, 5:6, :], rt[:, :, 6:7, :], m2, 1)
            step(v.memset(rt[:, :, 1, :], 0.0))
            step(v.tensor_tensor(rt[:, :, 1, 0:1], m2, m1, ALU.subtract))
            v.memset(mark[:, 1:2], 0.0).then_inc(s["route_shifted"], 1)
            dve.wait_ge(s["route_exp"], i + 1)
            step(v.tensor_reduce(rt[:, :, 7, 0:1], rt[:, :, 0:1, :], AX.X, ALU.add))
            step(v.tensor_scalar(rt[:, :, 7, 1:2], rt[:, :, 1, 0:1], 1.0, None, ALU.add))
            step(v.reciprocal(rt[:, :, 7, 0:2], rt[:, :, 7, 0:2]))
            step(v.tensor_tensor(rt[:, :, 7, 2:3], rt[:, :, 7, 0:1], rt[:, :, 7, 1:2], ALU.mult))
            step(v.tensor_tensor(rt[:, :, 7, 3:4], rt[:, :, 7, 2:3], rt[:, :, 1, 0:1], ALU.mult))
            step(v.tensor_tensor(rt[:, :, 4, :], rt[:, :, 4, :], rt[:, :, 7, 2:3].broadcast_to([P, TT, 4]), ALU.mult))
            step(v.tensor_tensor(rt[:, :, 5, :], rt[:, :, 5, :], rt[:, :, 7, 3:4].broadcast_to([P, TT, 4]), ALU.mult))
            step(v.tensor_tensor(rt[:, :, 4, :], rt[:, :, 4, :], rt[:, :, 5, :], ALU.add))
            v.tensor_tensor(comb[:].rearrange("p t (g e) -> p t g e", g=4), bc(rt[:, :, 2, :], 3, [P, TT, 4, 4]),
                            bc(rt[:, :, 4, :], 2, [P, TT, 4, 4]), ALU.mult).then_inc(s["comb_ready"], 1)
            dve.wait_ge(s["comb_ready"], i + 1)
            v.tensor_scalar(chosen[:], comb[:], 0.0, None, ALU.is_gt).then_inc(s["chosen_ready"], 1)
            dve.wait_ge(s["chosen_ready"], i + 1)
            dve.wait_ge(s["place_ready"], i + 1)
            n = MOE[name]["slots"]
            step(v.tensor_tensor(place[:].rearrange("p a e -> p (a e)"), B[7][:, 0:32],
                                 chosen[:].rearrange("p a e -> p (a e)"), ALU.mult))
            for tt in range(TT):
                v.tensor_tensor(selection(name)[:, tt].rearrange("p (e k) -> p e k", k=n),
                                bc(place[:, tt, :], 2, [P, 16, n]), bc(slot_no[:, 0:n], 1, [P, 16, n]),
                                ALU.is_equal).then_inc(s["selected"], 1)
            step(v.tensor_reduce(count[:, 0:1], B[7][:, 32:48], AX.X, ALU.max))
            v.tensor_scalar(flag[:, i:i + 1], count[:, 0:1], float(n), None, ALU.is_gt).then_inc(s["flag_ready"], 1)

        def experts(name, gate, alpha=None):
            d = MOE[name]
            i, n0, U, base, w, n = d["idx"], TILE[name], d["U"], d["unit"], d["width"], d["slots"]
            cw = 4 * n
            shift, scale = 6 * i + 3, 6 * i + 4

            def gathered(u, par, turned=None):
                if name == "moe2":
                    turned = None
                for g in range(2):
                    dve.wait_ge(s["gather_ready"], 2 * u + (d["ga"] + g + 1))
                    for c in range(4):
                        cc = 4 * g + c
                        ins = v.tensor_scalar(hg[par][:, cc * w:(cc + 1) * w], B[6][:, c * w:(c + 1) * w],
                                              modc[:, scale, cc:cc + 1], modc[:, shift, cc:cc + 1], ALU.mult, ALU.add)
                    ins.then_inc(s["gathered"], 1)
                    if g == 0 and turned is not None:
                        hidden_turned(turned, 1 - par)

            def hidden(u, par):
                dve.wait_ge(s["silu_done"], u + (base + 1))
                if name == "moe2":
                    v.tensor_tensor(hidb[par][:, 0:cw], silub[par][:, 0:cw], B[5][:, 0:cw],
                                    ALU.mult).then_inc(s["hid_done"], 1)
                else:
                    v.tensor_tensor(silub[par][:, 0:256], silub[par][:, 0:256], B[4][:, 256:512],
                                    ALU.mult).then_inc(s["hid_rows"], 1)

            def hidden_turned(u, par):
                dve.wait_ge(s["hidT_ready"], u + (base + 1))
                v.tensor_copy(hidb[par][:, 0:256], B[5][:, 0:256]).then_inc(s["hid_done"], 1)

            def weighted(u, par):
                sel = selection(name)
                if isinstance(u, int):
                    su, cu = sel[:, :, w * u:w * (u + 1)], comb[:, :, d["eu"] * u:d["eu"] * (u + 1)]
                else:
                    su, cu = sel[:, :, bass.ds(w * u, w)], comb[:, :, bass.ds(d["eu"] * u, d["eu"])]
                for tt in range(TT):
                    ins = v.tensor_tensor(swb[par][:, tt, 0:w].rearrange("p (e k) -> p e k", k=n),
                                          su[:, tt].rearrange("p (e k) -> p e k", k=n),
                                          bc(cu[:, tt], 2, [P, d["eu"], n]), ALU.mult)
                ins.then_inc(s["sw_ready"], 1)

            gathered(0, 0)
            hidden(0, 0)
            gathered(1, 1, turned=0)
            weighted(0, 0)
            hidden(1, 1)
            gathered(2, 0, turned=1)
            with dve.Fori(0, (U - 4) // 2) as t:
                for j in range(2):
                    weighted(2 * t + (1 + j), 1 - j)
                    hidden(2 * t + (2 + j), j)
                    gathered(2 * t + (3 + j), 1 - j, turned=2 * t + (2 + j))
            weighted(U - 3, 1)
            hidden(U - 2, 0)
            gathered(U - 1, 1, turned=U - 2)
            weighted(U - 2, 0)
            hidden(U - 1, 1)
            if name != "moe2":
                hidden_turned(U - 1, 1)
            weighted(U - 1, 1)
            dve.wait_ge(s["moe_summed"], i + 1)
            dve.wait_ge(s["gate_rows"], 2 * i + 2)
            for tt in range(TT):
                for h in range(2):
                    step(v.tensor_tensor(tmp[:, h, :], B[2 * tt + h][:], gate[:, 512 * h:512 * (h + 1)], ALU.mult))
                    xs = x[:, tt, 512 * h:512 * (h + 1)]
                    if alpha is None:
                        ins = v.tensor_tensor(xs, xs, tmp[:, h, :], ALU.add)
                    else:
                        ins = v.scalar_tensor_tensor(xs, xs, alpha, tmp[:, h, :], ALU.mult, ALU.add)
            ins.then_inc(s["moe_main"], 1)
            dve.wait_ge(s["moe_main"], i + 1)
            large = name == "moe2"
            over = overflows(dve, name)
            with dve.If(over > 0):
                v.tensor_scalar(chosen[:].rearrange("p a e -> p (a e)"), place[:].rearrange("p a e -> p (a e)"),
                                float(n), None, ALU.is_gt).then_inc(s[f"rest_step{i}"], 1)
                dve.wait_ge(s[f"rest_step{i}"], 1)
                v.tensor_tensor(comb[:], comb[:], chosen[:], ALU.mult).then_inc(s[f"rest_start{i}"], 1)
                dve.wait_ge(s[f"combT_out{i}"], 8)
                nb = 2 if large else 1
                with dve.Fori(0, 16) as e:
                    for k in range(nb):
                        dve.wait_ge(s[f"rest_silu{i}"], nb * e + (k + 1))
                        sil = silu_all[:, 2 * k:2 * k + 2, :]
                        v.tensor_tensor(sil, sil, B[6 + k][:].rearrange("p (c t) -> p c t", t=T),
                                        ALU.mult).then_inc(s[f"rest_up{i}"], 1)
                        dve.wait_ge(s[f"rest_up{i}"], nb * e + (k + 1))
                        ins = v.tensor_tensor(hid_all[:, 2 * k:2 * k + 2, :], sil,
                                              combT[:, bass.ds(e, 1), :].broadcast_to([P, 2, T]), ALU.mult)
                    ins.then_inc(s[f"rest_hid{i}"], 1)
                dve.wait_ge(s[f"rest_summed{i}"], 1)
                for tt in range(TT):
                    for h in range(2):
                        v.tensor_tensor(tmp[:, h, :], B[2 * tt + h][:], gate[:, 512 * h:512 * (h + 1)],
                                        ALU.mult).then_inc(s[f"rest_step{i}"], 1)
                        dve.wait_ge(s[f"rest_step{i}"], 2 + 2 * tt + h)
                        xs = x[:, tt, 512 * h:512 * (h + 1)]
                        v.tensor_tensor(xs, xs, tmp[:, h, :], ALU.add).then_inc(s[f"rest_added{i}"], 1)
                dve.wait_ge(s[f"rest_added{i}"], 4)
            v.memset(mark[:, 3:4], 0.0).then_inc(s["moe_added"], 1)

        def normalise_gain(rows, eps, center):
            scale_factor(x, eps, center)
            dve.wait_ge(s["rows_param"], 16 * rows)
            for tt in range(TT):
                if center:
                    ins = v.scalar_tensor_tensor(x[:, tt, :], x[:, tt, :], mv[:, tt, 0:1], rowp[:, 0, :],
                                                 ALU.subtract, ALU.mult)
                else:
                    ins = v.scalar_tensor_tensor(x[:, tt, :], x[:, tt, :], rstd[:, tt:tt + 1], rowp[:, 0, :],
                                                 ALU.mult, ALU.mult)
            step(ins)
            if center:
                for tt in range(TT):
                    ins = v.scalar_tensor_tensor(x[:, tt, :], x[:, tt, :], rstd[:, tt:tt + 1], rowp[:, 1, :],
                                                 ALU.mult, ALU.add)
                step(ins)

        dve.wait_ge(s["constants"], 1)
        for t in range(3):
            dve.wait_ge(s["cols_transposed"], t + 1)
            n = (P, P, 57)[t]
            v.tensor_copy(cols[:, P * t:P * t + n], B[4 + t][:, 0:n]).then_inc(s["cols_ready"], 1)

        dve.wait_ge(s["x_loaded"], 16)
        normalise(pb[:, :, 0:D], x[:], RMS_EPS, False).then_inc(s["xn_ready"], 1)
        dve.wait_ge(s["cols_ready"], 3)
        v.tensor_scalar(subc[:], col("ev_subln_g"), 1.0 - LAMBDA_INIT, None, ALU.mult)
        mod_columns(0)
        trans_out("h0", modulated(0, 0))
        dve.wait_ge(s["small_loads"], 16 * NSMALL)
        step(v.tensor_tensor(lamrow[:, 0:2, :], lamrow[:, 0::2, :], lamrow[:, 1::2, :], ALU.mult))
        v.tensor_reduce(lam[:, 0:2], lamrow[:, 0:2, :], AX.X, ALU.add).then_inc(s["lam_sums"], 1)
        for j in range(6):
            proj_out("evin", j, to_pb)
        trans_out("qk0", lambda j, bank: v.tensor_copy(A[:, 2 * j:2 * j + 2, :], bank[:]))
        dve.wait_ge(s["lam_exp"], 1)
        step(v.tensor_tensor(lam[:, 4:5], lam[:, 3:4], lam[:, 2:3], ALU.subtract))
        step(v.tensor_scalar(lam[:, 4:5], lam[:, 4:5], LAMBDA_INIT, None, ALU.subtract))
        attention("att0")
        dve.wait_ge(s["ot_out"], 8)
        ob = pb[:, :, 0:512]
        step(v.tensor_tensor(tmp[:], ob, ob, ALU.mult))
        step(v.tensor_reduce(obs[:].rearrange("p (a h) -> p a h", a=TT),
                             tmp[:].rearrange("p a (h e) -> p a h e", e=P), AX.X, ALU.add))
        v.tensor_scalar(obs[:], obs[:], 1.0 / P, RMS_EPS, ALU.mult, ALU.add).then_inc(s["var_ready"], 1)
        evals[0] += 1
        dve.wait_ge(s["pow_done"], evals[0])
        obh = ob.rearrange("p a (h e) -> p a h e", e=P)
        v.tensor_tensor(obh, obh, bc(obs[:].rearrange("p (a h) -> p a h", a=TT), 3, [P, TT, 4, P]),
                        ALU.mult).then_inc(s["ob_ready"], 1)
        trans_out("ob", lambda j, bank: v.tensor_scalar(OT[:, 4 + 2 * j:6 + 2 * j, :],
                                                        bank[:].rearrange("p (c t) -> p c t", t=T),
                                                        subc[:, 0:1], None, ALU.mult))
        residual("evout", gate1)
        normalise(pb[:, :, 0:D], x[:], RMS_EPS, False).then_inc(s["xn_ready"], 1)
        trans_out("h1", modulated(0, 3))
        routing("moe0")
        experts("moe0", gate2)
        normalise(pb[:, :, 0:D], x[:], RMS_EPS, False).then_inc(s["xn_ready"], 1)
        trans_out("h2", modulated(1, 0))

        def odd_out(j, b0, b1):
            if j < 2:
                return v.tensor_copy(pb[:, 1, 512 * j:512 * (j + 1)], b1[:])
            return odd_kv(v.tensor_copy, j, 1, b1)
        for j in range(5):
            proj_out("odin", j, odd_out)
        v.memset(mark[:, 1:2], 0.0).then_inc(s["proj_dve"], 1)
        trans_out("qkv1", lambda j, bank: v.tensor_copy(A[:, 2 * j:2 * j + 2, :], bank[:]))
        stage_transposed(dve, "qkv1")
        for kv in range(2):
            for par in range(2):
                rows = slice(par * HD, (par + 1) * HD)
                for g in range(4):
                    src = A[rows, 8 + 4 * kv + g, :]
                    for half in range(2):
                        sv = src[:, 16 * half:16 * half + 16 * NCMP].rearrange(
                            "p (n l e) -> p e l n", e=2, l=8)[:, par]
                        pos = bc(cols[rows, COL["pos"] + 16 * kv + 8 * half:COL["pos"] + 16 * kv + 8 * half + 8],
                                 2, [HD, 8, NCMP])
                        ins = v.tensor_tensor(cmpB[rows, kv, 8 * half:8 * half + 8, g, :], sv, pos, ALU.add)
            ins.then_inc(s["blocks_ready"], 1)
        dve.wait_ge(s["b1_loaded"], 16)
        for kv in range(2):
            tile_ready(dve, TILE["cmp"] + kv)
            v.tensor_tensor(cmph[:, kv, :], B[kv][0:60, 0:256], b1c[:, kv, :], ALU.add).then_inc(s["hidden_biased"], 1)
        dve.wait_ge(s["vcmp_ready"], 1)
        v.tensor_tensor(vcmp[:], B[7][0:NCMP, 0:256].rearrange("p (g d) -> p g d", g=4),
                        bc(b2v[:], 1, [NCMP, 4, HD]), ALU.add).then_inc(s["vcmp_out"], 1)
        dve.wait_ge(s["cscore_ready"], 1)
        pc3 = pc.rearrange("p (b n) -> p b n", n=NCMP)
        for tt in range(TT):
            for par in range(2):
                ins = v.scalar_tensor_tensor(
                    pc3[:, 16 * tt + par:16 * tt + 16:2],
                    B[6 + par][:, 120 * tt:120 * tt + 120].rearrange("p (h n) -> p h n", n=NCMP), SCALE,
                    bc(maskc[:, tt, :], 1, [P, 8, NCMP]), ALU.mult, ALU.add)
        ins.then_inc(s["cscore_out"], 1)
        dve.wait_ge(s["cscore_out"], 1)
        step(v.tensor_reduce(cs[:, 0, :], pc3, AX.X, ALU.max))
        v.tensor_tensor(pc3, pc3, bc(cs[:, 0, :], 2, [P, 32, NCMP]), ALU.subtract).then_inc(s["cscore_shifted"], 1)
        dve.wait_ge(s["cscore_exp"], 1)
        step(v.tensor_reduce(cs[:, 1, :], pc3, AX.X, ALU.add))
        step(v.reciprocal(cs[:, 1, :], cs[:, 1, :]))
        for tt in range(TT):
            ins = v.scalar_tensor_tensor(cs[:, 2, 16 * tt:16 * tt + 16], gts[:, tt, 0::3], cmp_live[:, tt:tt + 1],
                                         cs[:, 1, 16 * tt:16 * tt + 16], ALU.mult, ALU.mult)
        step(ins)
        v.tensor_tensor(pc3, pc3, bc(cs[:, 2, :], 2, [P, 32, NCMP]), ALU.mult).then_inc(s["pc_ready"], 1)
        attention("att1")
        residual("odout", gate1)
        normalise(pb[:, :, 0:D], x[:], RMS_EPS, False).then_inc(s["xn_ready"], 1)
        trans_out("h3", modulated(1, 3))
        routing("moe1")
        experts("moe1", gate2)
        normalise_gain(1, RMS_EPS, False)
        v.memset(mark[:, 1:2], 0.0).then_inc(s["final_scaled"], 1)
        normalise(pb[:, :, 0:D], x[:], LN_EPS, True).then_inc(s["xn_ready"], 1)
        trans_out("h4", modulated(2, 0))
        dve.wait_ge(s["dt_ready"], 1)
        for tt in range(TT):
            ins = v.tensor_tensor(dts[:, 0, tt, :], B[6][:, 32 * tt:32 * tt + 24], bdf[:], ALU.add)
        step(ins)
        step(v.tensor_scalar(dts[:, 0, :, 16:24], dts[:, 0, :, 16:24], -1.0, None, ALU.mult))
        step(v.scalar_tensor_tensor(dts[:, 1], dts[:, 0], -1.0, dts[:, 0], ALU.mult, ALU.max))
        v.tensor_scalar(dts[:, 1], dts[:, 1], -1.0, None, ALU.mult).then_inc(s["dt_abs"], 1)
        v.memset(xT[:, :, 0:3], 0.0).then_inc(s["xT_padded"], 1)
        dve.wait_ge(s["dt_ln"], 1)
        step(v.scalar_tensor_tensor(dts[:, 3], dts[:, 0], 0.0, dts[:, 2], ALU.max, ALU.add))
        dve.wait_ge(s["alog_exp"], 1)
        for tt in range(TT):
            v.scalar_tensor_tensor(dts[:, 4, tt, 0:16], dts[:, 3, tt, 0:16], -1.0, cs[:, 3, 0:16],
                                   ALU.mult, ALU.mult)
        v.tensor_scalar(dts[:, 5, :, 16:24], dts[:, 3, :, 16:24], 1.0 / SCALE, None,
                        ALU.mult).then_inc(s["a_ready"], 1)
        for j in range(4):
            proj_out("xbc", j, lambda j, b0, b1: v.tensor_copy(
                xT[:, 4 * j + 2:4 * j + 4, 3:259], b1[:].rearrange("p (c t) -> p c t", t=T)))
        proj_evacuated(dve, PROJ["xbc"] + 3)
        for cc in range(16):
            acc = tmp[:, cc % 2, 0:T]
            if cc >= 2:
                dve.wait_ge(s["conv_act"], cc - 1)
            step(v.tensor_scalar(acc, xT[:, cc, 3:259], col("conv_w_2", 48 + cc), col("conv_b_2", cc),
                                 ALU.mult, ALU.add))
            for k in (2, 1):
                step(v.scalar_tensor_tensor(acc, xT[:, cc, k:k + T], col("conv_w_2", 16 * k + cc), acc,
                                            ALU.mult, ALU.add))
            v.scalar_tensor_tensor(acc, xT[:, cc, 0:T], col("conv_w_2", cc), acc, ALU.mult,
                                   ALU.add).then_inc(s["conv_done"], 1)
        trans_out("xs", lambda j, bank: v.tensor_copy(pb[:, j // 2, 512 * (j % 2):512 * (j % 2) + 512], bank[:]))
        trans_out("btok", lambda j, bank: v.tensor_copy(Btok, bank[:]))
        stage_transposed(dve, "xs")
        dve.wait_ge(s["cs_out"], 1)
        for tt in range(TT):
            xh = pb[:, tt, 0:D].rearrange("p (h e) -> p h e", e=HD)
            v.tensor_tensor(pb[:, tt, 2 * D:3 * D].rearrange("p (h e) -> p h e", e=HD), xh,
                            bc(dsk[:], 2, [P, 16, HD]), ALU.mult)
            ins = v.tensor_tensor(pb[:, tt, D:2 * D].rearrange("p (h e) -> p h e", e=HD), xh,
                                  bc(dts[:, 3, tt, 0:16], 2, [P, 16, HD]), ALU.mult)
        ins.then_inc(s["xh_used"], 1)
        dve.wait_ge(s["xh_used"], 1)
        v.tensor_tensor(xdte.rearrange("p (h e) -> p h e", e=HD),
                        pb[:, 0, D:2 * D].rearrange("p (h e) -> p h e", e=HD),
                        bc(cs[:, 1, 0:16], 2, [P, 16, HD]), ALU.mult).then_inc(s["xdt_ready"], 1)
        for q in range(9):
            if q < 8:
                tt, g = q // 4, q % 4
                dve.wait_ge(s["seg_ready"], q + 1)
                m3 = mt[q % 2].rearrange("p (r l) -> p r l", r=4)
                if q >= 2:
                    dve.wait_ge(s["y_ready"], q - 1)
                v.tensor_tensor(m3, B[6 + q % 2][:].rearrange("p (r l) -> p r l", r=4),
                                bc(maskT[:], 1, [P, 4, P]), ALU.add).then_inc(s["seg_out"], 1)
                dve.wait_ge(s["seg_out"], q + 1)
                v.tensor_tensor(m3, m3, bc(cs[:, 0, 16 * tt + 4 * g:16 * tt + 4 * g + 4], 2, [P, 4, P]),
                                ALU.subtract).then_inc(s["seg_shifted"], 1)
            if q >= 1:
                r = q - 1
                tt, g = r // 4, r % 4
                ys = pb[:, tt, 2 * D + 256 * g:2 * D + 256 * (g + 1)]
                m3 = mt[r % 2].rearrange("p (r l) -> p r l", r=4)
                dve.wait_ge(s["decay_done"], r + 1)
                v.tensor_tensor(m3, m3, bc(B[r % 2][:, 0:P], 1, [P, 4, P]), ALU.mult).then_inc(s["m_ready"], 1)
                dve.wait_ge(s["y_ready"], r + 1)
                bank = B[2 + r % 2]
                step(v.tensor_tensor(ys, ys, bank[:, 0:256], ALU.add))
                if tt == 1:
                    step(v.tensor_tensor(tmp[:, 0, 0:256].rearrange("p (r e) -> p r e", e=HD),
                                         bank[:, 256:512].rearrange("p (r e) -> p r e", e=HD),
                                         bc(cs[:, 2, 16 + 4 * g:20 + 4 * g], 2, [P, 4, HD]), ALU.mult))
                    step(v.tensor_tensor(ys, ys, tmp[:, 0, 0:256], ALU.add))
                v.memset(mark[:, 1:2], 0.0).then_inc(s["y_out"], 1)
            if q < 6 and q % 2 == 1:
                tile_ready(dve, TILE["qkv"] + q // 2)
                c0 = QKV_COL[q // 2]
                v.tensor_copy(pb[:, 1, c0:c0 + 512], B[5][:]).then_inc(s["qkv_dve"], 1)
        yv = pb[:, :, 2 * D:3 * D]
        dve.wait_ge(s["proj_act"], PROJ_ACT[PROJ["z"] + 1])
        for tt, silu_z in enumerate((gate1, gate2)):
            ins = v.tensor_tensor(yv[:, tt], yv[:, tt], silu_z[:], ALU.mult)
        step(ins)
        normalise(yv, yv, LN_EPS, False).then_inc(s["gated_ready"], 1)

        def gated_out(j, bank):
            for i in range(2):
                c = 2 * j + i
                ins = v.tensor_scalar(OT[:, c, :], bank[:, i * T:(i + 1) * T], col("ssd_norm_w_2", c), None,
                                      ALU.mult)
            return ins
        trans_out("gated", gated_out)
        for j in range(2):
            proj_out("ssdo", j, lambda j, b0, b1: v.tensor_copy(pb[:, 1, 2048 + 512 * j:2560 + 512 * j], b1[:]))
        trans_out("qk2", lambda j, bank: v.tensor_copy(A[:, 2 * j:2 * j + 2, :], bank[:]))
        attention("att2")
        for j in range(2):
            proj_out("atto", j, to_pb, n=TILE["atto"])
        proj_evacuated(dve, PROJ["atto"] + 1)
        dve.wait_ge(s["branch_out"], 8)
        mg = pb[:, :, D:2 * D]
        v.tensor_tensor(mg, mg, pb[:, :, 2 * D:3 * D], ALU.mult)
        step(v.tensor_tensor(satt, satt, pb[:, :, 0:D], ALU.mult))
        v.tensor_tensor(mg, mg, satt, ALU.add).then_inc(s["merged_ready"], 1)
        trans_out("merged", lambda j, bank: v.tensor_copy(OT[:, 2 * j:2 * j + 2, :], bank[:]))
        residual("wo", gate1, ALPHA)
        normalise_gain(3, LN_EPS, True)
        v.memset(mark[:, 1:2], 0.0).then_inc(s["ln_scaled"], 1)
        normalise(pb[:, :, 0:D], x[:], LN_EPS, True).then_inc(s["xn_ready"], 1)
        trans_out("h5", modulated(2, 3))
        routing("moe2")
        experts("moe2", gate2, ALPHA)
        normalise_gain(5, LN_EPS, True)
        v.memset(mark[:, 2:3], 0.0).then_inc(s["result"], 1)

    @block.tensor
    def _(pe):
        mm = nc.tensor.matmul

        def transposes(name, sources):
            for k in range(TRANS[name], TRANS_END[name]):
                if k >= 2:
                    trans_evacuated(pe, k - 2)
                for dst, src in sources(k - TRANS[name], B[4 + k % 2]):
                    n = src.shape[0]
                    ins = nc.tensor.transpose(dst, src, ident[0:n, 0:n])
                ins.then_inc(s["tr_ready"], 1)

        def from_tokens(src, column=lambda c: P * c):
            def sources(j, bank):
                return [(bank[:, i * T + tt * P:i * T + (tt + 1) * P],
                         src[:, tt, column(2 * j + i):column(2 * j + i) + P]) for i in range(2) for tt in range(TT)]
            return sources

        def landed_tile(n):
            pe.wait_ge(landed[n % NSLOT], LANDED[n])
            return ring[n % NSLOT][:].rearrange("p (c n) -> p c n", n=512)

        def bank_pair_free(m):
            if m >= 2:
                proj_evacuated(pe, m - 2)

        def project(name, tiles, lhs):
            for j in range(tiles):
                m = PROJ[name] + j
                w = landed_tile(TILE[name] + j)
                if j >= 2:
                    bank_pair_free(m)
                for tt in range(TT):
                    for c in range(C):
                        ins = mm(B[2 * (m % 2) + tt][:], lhs[:, c, tt * P:(tt + 1) * P], w[:, c, :],
                                 start=c == 0, stop=c == C - 1)
                ins.then_inc(tile_used, 1)

        def mod_tile(G, k, chunks=range(C)):
            if k == 0 and chunks[0] == 0 and G:
                pe.wait_ge(s["mod_raw_out"], G)
            w = landed_tile(MOD_TILE[G] + k)
            c0 = C if G >= 6 else 0
            for c in chunks:
                for q in range(4):
                    ins = mm(B[2][32 * q:32 * (q + 1), k * P:(k + 1) * P],
                             cact[:, c0 + c:c0 + c + 1].broadcast_to([P, 32]), w[:, c, q * P:(q + 1) * P],
                             start=c == 0, stop=c == C - 1)
            if chunks[-1] == C - 1:
                ins.then_inc(tile_used, 1)

        def mod_turn(G):
            pe.wait_ge(s["mod_raw_out"], G + 1)
            if G:
                pe.wait_ge(s["mod_ready"], G)
            for k in range(4):
                ins = nc.tensor.transpose(B[3][:, k * P:(k + 1) * P], mod_raw[G % 2][:, k * P:(k + 1) * P], ident[:])
            ins.then_inc(s["mod_turned"], 1)

        def gate_spread(g):
            pe.wait_ge(s["mod_ready"], 3 * (g // 2) + (3 if g % 2 else 2))
            if g % 2:
                pe.wait_ge(s["gate_rows"], g)
            for b in range(C):
                ins = mm(B[6 + b // 4][:, (b % 4) * P:(b % 4 + 1) * P],
                         modc[:, 6 * (g // 2) + (5 if g % 2 else 2), b:b + 1].broadcast_to([P, P]), ident[:],
                         start=True, stop=True)
            ins.then_inc(s["gate_spread"], 1)

        def attention(name):
            items = ITEMS[name]
            for t in range(len(items) + 2):
                if t < len(items) and items[t]["soft"] is not None:
                    it = items[t]
                    u = it["soft"]
                    bank = B[6 + u % 2]
                    if u >= 2:
                        pe.wait_ge(s["s_masked"], u - 1)
                    q, k, f = it["q"], it["k"], it["forget"]
                    ins = mm(bank[:, 0:P], q[:, 0:P], k[:, 0:P], start=True, stop=f is None)
                    if f is not None:
                        fb = [dts[:, 5, tt, 16 + f:17 + f].broadcast_to([P, P]) for tt in range(TT)]
                        mm(bank[:, 0:P], fb[0], tri, start=False, stop=True)
                    ins = mm(bank[:, P:384], q[:, P:T], k[:, 0:T], start=True, stop=f is None)
                    if f is not None:
                        mm(bank[:, P:384], fb[0], tri_one[:], start=False, stop=False)
                        ins = mm(bank[:, T:384], fb[1], tri, start=False, stop=True)
                    ins.then_inc(s["s_ready"], 1)
                if 0 <= t - 2 < len(items) and items[t - 2]["tr"] is not None:
                    it = items[t - 2]
                    k = it["tr"]
                    trans_evacuated(pe, k)
                    if it["ot_first"] and it["ot"] >= 2:
                        pe.wait_ge(s["ot_out"], it["ot"] - 1)
                    for dst, lhs, rhs, start, stop in it["pv"](PT[:, k % 2, :]):
                        ins = mm(dst, lhs, rhs, start=start, stop=stop)
                    ins.then_inc(s["pv_done"], 1)
                G = mod_group_step(name, t, 1)
                if G is not None:
                    mod_turn(G)
                if mod_tile_step(name, t) is not None:
                    mod_tile(*mod_tile_step(name, t))
                if name == "att2" and t < 8:
                    j, tt = t // 2, t % 2
                    if t >= 2:
                        pe.wait_ge(s["branch_out"], t - 1)
                    w = landed_tile(TILE["gates"] + j)
                    for c in range(C):
                        ins = mm(B[2 + tt][:], hT[:, c, tt * P:(tt + 1) * P], w[:, c, :],
                                 start=c == 0, stop=c == C - 1)
                    ins.then_inc(tile_used if tt else s["branch_ready"], 1)
                if 0 <= t - 1 < len(items) and items[t - 1]["tr"] is not None:
                    it = items[t - 1]
                    k = it["tr"]
                    bank = B[4 + k % 2]
                    trans_evacuated(pe, k - 2)
                    if it["kind"] == "cmp":
                        pe.wait_ge(s["pc_ready"], 1)
                        for tt in range(TT):
                            src = pc[:, (16 * tt + it["h"]) * NCMP:(16 * tt + it["h"] + 1) * NCMP]
                            ins = nc.tensor.transpose(bank[0:NCMP, tt * P:(tt + 1) * P], src, ident[:])
                    else:
                        pe.wait_ge(s["p_ready"], it["soft"] + 1)
                        for j in range(3):
                            ins = nc.tensor.transpose(bank[:, j * P:(j + 1) * P],
                                                      Pm[:, it["soft"] % 2, j * P:(j + 1) * P], ident[:])
                    ins.then_inc(s["tr_ready"], 1)
            pe.wait_ge(s["s_masked"], max(it["soft"] + 1 for it in items if it["soft"] is not None))

        def experts(name, hname):
            d = MOE[name]
            i, n0, U = d["idx"], TILE[name], d["U"]
            large = name == "moe2"
            stage_transposed(pe, hname)
            if i == 0:
                pe.wait_ge(s["small_loads"], 16 * NSMALL)
            for tt in range(TT):
                for c in range(C):
                    ins = mm(B[7][:, 32 * tt:32 * tt + 20], hT[:, c, tt * P:(tt + 1) * P], wr[i][:, c, :],
                             start=c == 0, stop=c == C - 1)
            ins.then_inc(s["router_ready"], 1)

            sel = pb[:, :, D:D + 16 * d["slots"]]
            base, w, n, eu = d["unit"], d["width"], d["slots"], d["eu"]

            def landed_at(n_static, turn):
                slot = n_static % NSLOT
                if isinstance(turn, int):
                    pe.wait_ge(landed[slot], LANDED[n_static + 6 * turn])
                else:
                    per = LANDED[n_static + 6] - LANDED[n_static]
                    pe.wait_ge(landed[slot], turn * per + LANDED[n_static])
                return ring[slot][:]

            def inputs(n_tile, turn, u, par, first_unit=False):
                pe.wait_ge(s["gathered"], 2 * u + (d["ga"] + 2))
                h3 = hg[par][:, 0:C * w].rearrange("p (c k) -> p c k", c=C)
                if large:
                    if not first_unit:
                        pe.wait_ge(s["hid_done"], u + base)
                    for b in range(2):
                        wv = landed_at(n_tile + b, turn).rearrange("p (c f) -> p c f", f=512)
                        for k in range(4):
                            for c in range(C):
                                ins = mm(B[4 + b][:, k * n:(k + 1) * n], wv[:, c, k * P:(k + 1) * P], h3[:, c, :],
                                         start=c == 0, stop=c == C - 1)
                        ins.then_inc(tile_used, 1)
                    return
                if not first_unit:
                    pe.wait_ge(s["hid_rows"], u + base)
                wv = [landed_at(n_tile + b, turn).rearrange("p (g c f) -> p g c f", g=2, f=256) for b in range(2)]
                for c in range(C):
                    for b in range(2):
                        ins = mm(B[4][n * b:n * (b + 1), :], h3[:, c, n * b:n * (b + 1)], wv[b][:, :, c, :],
                                 start=c == 0, stop=c == C - 1)
                        if c == C - 1:
                            ins.then_inc(tile_used, 1)

            def hidden_turn(u, par):
                pe.wait_ge(s["hid_rows"], u + (base + 1))
                if not (isinstance(u, int) and u + base == 0):
                    pe.wait_ge(s["hid_done"], u + base)
                for k in range(2):
                    ins = nc.tensor.transpose(B[5][:, k * P:(k + 1) * P], silub[par][:, k * P:(k + 1) * P], ident[:])
                ins.then_inc(s["hidT_ready"], 1)

            def gather(u, g, any_before=True):
                if g == 0 and any_before:
                    if not (isinstance(u, int) and u + base == 2):
                        pe.wait_ge(s["swT_out"], u + (base - 2))
                elif not (isinstance(u, int) and 2 * u + d["ga"] + g == 0):
                    pe.wait_ge(s["gathered"], 2 * u + (d["ga"] + g))
                su = sel[:, :, w * u:w * (u + 1)] if isinstance(u, int) else sel[:, :, bass.ds(w * u, w)]
                for c in range(4):
                    cc = 4 * g + c
                    for tt in range(TT):
                        ins = mm(B[6][:, c * w:(c + 1) * w], xn[:, tt, cc * P:(cc + 1) * P], su[:, tt, :],
                                 start=tt == 0, stop=tt == TT - 1)
                ins.then_inc(s["gather_ready"], 1)

            def down(n_tile, turn, u, par, h):
                ws = landed_at(n_tile, turn).rearrange("p (k m) -> p k m", m=D)
                if h == 0:
                    pe.wait_ge(s["hid_done"], u + (base + 1))
                if not (isinstance(u, int) and u == 0 and h == 0 and base == 0):
                    pe.wait_ge(s["ye_out"], 2 * u + (2 * base + h))
                for k in range(4 // eu):
                    for b in range(eu):
                        kk = k if large else 2 * b + k
                        h0 = k * n if large else k * P + b * n
                        ins = mm(B[7][n * b:n * (b + 1), :], hidb[par][:, h0:h0 + n],
                                 ws[:, kk, 512 * h:512 * (h + 1)], start=k == 0, stop=k == 4 // eu - 1)
                ins.then_inc(tile_used if h else s["ye_ready"], 1)

            def weights(u, par):
                pe.wait_ge(s["sw_ready"], u + (base + 1))
                for tt in range(TT):
                    ins = nc.tensor.transpose(B[6][0:w, tt * P:(tt + 1) * P], swb[par][:, tt, 0:w], ident[:])
                ins.then_inc(s["swT_ready"], 1)

            def scatter(u, par, last=False):
                pe.wait_ge(s["ye_out"], 2 * u + (2 * base + 2))
                pe.wait_ge(s["swT_out"], u + (base + 1))
                for tt in range(TT):
                    for h in range(2):
                        ins = mm(B[2 * tt + h][:], swT[par][0:w, tt * P:(tt + 1) * P],
                                 ye[par][0:w, 512 * h:512 * (h + 1)], start=False, stop=last)
                if last:
                    ins.then_inc(s["moe_summed"], 1)

            def turn_step(n_tile, turn, u, par, gather_next=True, before=True, scatter_old=True):
                inputs(n_tile, turn, u, par)
                if gather_next:
                    gather(u + 1, 0)
                down(n_tile + 2, turn, u - 1, 1 - par, 0)
                if not large:
                    hidden_turn(u, par)
                if gather_next:
                    gather(u + 1, 1)
                down(n_tile + 2, turn, u - 1, 1 - par, 1)
                if scatter_old:
                    scatter(u - 2, par)
                if gather_next:
                    pe.wait_ge(s["gathered"], 2 * u + (d["ga"] + 4))
                else:
                    pe.wait_ge(s["swT_out"], u + (base - 1))
                weights(u - 1, 1 - par)

            for b in range(4):
                mm(B[b][:], zeros[:], bc(ident[:], 1, [P, 4, P]), start=True, stop=False)
            pe.wait_ge(s["chosen_ready"], i + 1)
            mm(B[7][:, 0:16], tri, chosen[:, 0, :], start=True, stop=True)
            ones = tri_one[:, P:T]
            mm(B[7][:, 16:32], ones, chosen[:, 0, :], start=True, stop=False)
            mm(B[7][:, 16:32], tri, chosen[:, 1, :], start=False, stop=True)
            mm(B[7][:, 32:48], ones, chosen[:, 0, :], start=True, stop=False)
            mm(B[7][:, 32:48], ones, chosen[:, 1, :], start=False, stop=True).then_inc(s["place_ready"], 1)
            pe.wait_ge(s["selected"], 2 * (i + 1))
            pe.wait_ge(s["flag_ready"], i + 1)
            gather(0, 0, False)
            gather(0, 1)
            inputs(n0, 0, 0, 0, True)
            gather(1, 0, False)
            if not large:
                hidden_turn(0, 0)
            gather(1, 1)
            turn_step(unit_tile(n0, 1), 0, 1, 1, scatter_old=False)
            with pe.Fori(0, (U - 4) // 2) as t:
                for j in range(2):
                    turn_step(unit_tile(n0, 2 + j), t, 2 * t + (2 + j), j)
            turn_step(unit_tile(n0, U - 2), 0, U - 2, 0)
            turn_step(unit_tile(n0, U - 1), 0, U - 1, 1, gather_next=False)
            for h in range(2):
                down(unit_tile(n0, U - 1) + 3, 0, U - 1, 1, h)
            scatter(U - 2, 0)
            pe.wait_ge(s["swT_out"], base + U - 1)
            weights(U - 1, 1)
            scatter(U - 1, 1, last=True)

            over = overflows(pe, name)
            with pe.If(over > 0):
                pe.wait_ge(s[f"rest_start{i}"], 1)
                for j in range(8):
                    if j >= 4:
                        pe.wait_ge(s[f"combT_out{i}"], j - 3)
                    for a in range(2):
                        for tt in range(TT):
                            ins = mm(B[j % 4][:, a * T + tt * P:a * T + (tt + 1) * P],
                                     comb[:, tt, 2 * j + a:2 * j + a + 1].broadcast_to([P, P]), ident[:],
                                     start=True, stop=True)
                    ins.then_inc(s[f"combT_ready{i}"], 1)
                pe.wait_ge(s[f"combT_out{i}"], 8)
                for b in range(4):
                    ins = mm(B[b][:], zeros[:], bc(ident[:], 1, [P, 4, P]), start=True, stop=False)
                ins.then_inc(s[f"rest_used{i}"], 1)
                F = 512 if large else 256
                with pe.Fori(0, 16) as e:
                    pe.wait_ge(s[f"rest_landed{i}"], 48 * e + 48)
                    for slot in range(2):
                        wv = ring[slot][:, 0:C * F].rearrange("p (c f) -> p c f", f=F)
                        for k in range(F // P):
                            bank = B[4 + 2 * slot + k // 2]
                            for c in range(C):
                                ins = mm(bank[:, (k % 2) * T:(k % 2 + 1) * T], wv[:, c, k * P:(k + 1) * P],
                                         hT[:, c, :], start=c == 0, stop=c == C - 1)
                    ins.then_inc(s[f"rest_inputs{i}"], 1)
                    pe.wait_ge(s[f"rest_hid{i}"], e + 1)
                    wd = ring[2][:, 0:F // P * D].rearrange("p (k m) -> p k m", m=D)
                    for tt in range(TT):
                        for h in range(2):
                            for k in range(F // P):
                                ins = mm(B[2 * tt + h][:], hid_all[:, k, tt * P:(tt + 1) * P],
                                         wd[:, k, 512 * h:512 * (h + 1)], start=False, stop=False)
                    ins.then_inc(s[f"rest_used{i}"], 1)
                for b in range(4):
                    ins = mm(B[b][:], zeros[:], bc(ident[:], 1, [P, 4, P]), start=False, stop=True)
                ins.then_inc(s[f"rest_summed{i}"], 1)

        pe.wait_ge(s["constants"], 1)
        pe.wait_ge(s["rows_loaded"], 16 * len(colrows))
        for t in range(3):
            rows = (P, P, 57)[t]
            nc.tensor.transpose(B[4 + t][:, 0:rows], stage[0:rows, t, 0:P],
                                ident[0:rows, 0:rows]).then_inc(s["cols_transposed"], 1)

        pe.wait_ge(s["cact_ready"], 1)
        for k in range(4):
            mod_tile(0, k)
        mod_turn(0)
        pe.wait_ge(s["xn_ready"], 1)
        xn = pb[:, :, 0:D]
        transposes("h0", from_tokens(xn))
        stage_transposed(pe, "h0")
        project("evin", 6, hT)
        pe.wait_ge(s["roped"], 4)
        transposes("qk0", from_tokens(pb, lambda c: P * c if c < 8 else 1536 + P * (c - 8)))
        stage_transposed(pe, "qk0")
        proj_evacuated(pe, PROJ["evin"] + 5)
        attention("att0")
        gate_spread(0)
        pe.wait_ge(s["ob_ready"], 1)
        transposes("ob", from_tokens(pb))
        stage_transposed(pe, "ob")
        pe.wait_ge(s["ot_out"], 8)
        pe.wait_ge(s["mod_ready"], 4)
        project("evout", 2, OT)
        gate_spread(1)
        pe.wait_ge(s["gate_rows"], 2)
        pe.wait_ge(s["xn_ready"], 2)
        transposes("h1", from_tokens(xn))
        experts("moe0", "h1")
        pe.wait_ge(s["moe_added"], 1)
        pe.wait_ge(s["xn_ready"], 3)
        transposes("h2", from_tokens(xn))
        stage_transposed(pe, "h2")
        project("odin", 5, hT)
        m = PROJ["odin"] + 5
        bank_pair_free(m)
        for tt in range(TT):
            for c in range(C):
                ins = mm(B[2 * (m % 2) + tt][:, 0:48], hT[:, c, tt * P:(tt + 1) * P], w48[:, c, :],
                         start=c == 0, stop=c == C - 1)
        ins.then_inc(s["tail_ready"], 1)
        pe.wait_ge(s["roped"], 9)
        proj_evacuated(pe, PROJ["odin"] + 5)
        transposes("qkv1", from_tokens(pb))
        for kv in range(2):
            n = TILE["cmp"] + kv
            pe.wait_ge(landed[n % NSLOT], LANDED[n])
            pe.wait_ge(s["blocks_ready"], kv + 1)
            w = ring[n % NSLOT][:].rearrange("p (c f) -> p c f", f=256)
            for l in range(16):
                ins = mm(B[kv][0:60, 0:256], cmpB[:, kv, l].rearrange("p g n -> p (g n)"), w[:, l, :],
                         start=l == 0, stop=l == 15)
            ins.then_inc(tile_used, 1)
        pe.wait_ge(s["hidden_done"], 2)
        transposes("cmph", lambda j, bank: [(bank[:, 60 * (2 * kv + k):60 * (2 * kv + k + 1)],
                                             cmph[:, kv, k * P:(k + 1) * P]) for kv in range(2) for k in range(2)])
        stage_transposed(pe, "cmph")
        hT4 = hidT_c.rearrange("p (v k g n) -> p v k g n", v=2, k=2, g=4)
        for k in range(2):
            ins = mm(B[6][:, 0:60], w2c[:, k, 0:2, :].rearrange("p e d -> p (e d)"),
                     hT4[:, 0, k].rearrange("p g n -> p (g n)"), start=k == 0, stop=k == 1)
        ins.then_inc(s["kcmp_ready"], 1)
        for g in range(4):
            for k in range(2):
                ins = mm(B[7][0:NCMP, g * HD:(g + 1) * HD], hT4[:, 1, k, g, :], w2c[:, k, 2, :],
                         start=k == 0, stop=k == 1)
        ins.then_inc(s["vcmp_ready"], 1)
        pe.wait_ge(s["kcmp_out"], 1)
        pe.wait_ge(s["vcmp_out"], 1)
        for tt in range(TT):
            for h in range(16):
                rows = slice((h % 2) * HD, (h % 2 + 1) * HD)
                slot = 8 * tt + h // 2
                ins = mm(B[6 + h % 2][:, slot * NCMP:(slot + 1) * NCMP],
                         A[rows, h // 2, tt * P:(tt + 1) * P], kcmpT[rows, (h // 4) * NCMP:(h // 4 + 1) * NCMP],
                         start=True, stop=True)
        ins.then_inc(s["cscore_ready"], 1)
        pe.wait_ge(s["cscore_out"], 1)
        attention("att1")
        gate_spread(2)
        pe.wait_ge(s["ot_out"], 16)
        pe.wait_ge(s["mod_ready"], 9)
        project("odout", 2, OT)
        gate_spread(3)
        pe.wait_ge(s["gate_rows"], 4)
        pe.wait_ge(s["xn_ready"], 4)
        transposes("h3", from_tokens(xn))
        experts("moe1", "h3")
        pe.wait_ge(s["moe_added"], 2)
        pe.wait_ge(s["xn_ready"], 5)
        transposes("h4", from_tokens(xn))
        stage_transposed(pe, "h4")
        for tt in range(TT):
            for c in range(C):
                ins = mm(B[6][:, 32 * tt:32 * tt + 24], hT[:, c, tt * P:(tt + 1) * P], wdf[:, c, :],
                         start=c == 0, stop=c == C - 1)
        ins.then_inc(s["dt_ready"], 1)
        for j in range(4):
            m = PROJ["xbc"] + j
            w = landed_tile(TILE["xbc"] + j)
            if j >= 2:
                bank_pair_free(m)
            for a in range(4):
                for c in range(C):
                    ins = mm(B[2 * (m % 2) + a // 2][:, (a % 2) * T:(a % 2 + 1) * T], w[:, c, a * P:(a + 1) * P],
                             hT[:, c, :], start=c == 0, stop=c == C - 1)
            ins.then_inc(tile_used, 1)
        pe.wait_ge(s["a_ready"], 1)
        for tt in range(TT):
            mm(B[7][:, 16 * tt:16 * tt + 16], tri, dts[:, 4, tt, 0:16], start=True, stop=True)
            ins = mm(B[7][:, 32 + 16 * tt:48 + 16 * tt], tri_gt[:], dts[:, 4, tt, 0:16], start=True, stop=True)
        ins.then_inc(s["cs_ready"], 1)
        bank_pair_free(PROJ["z"])
        bank_pair_free(PROJ["z"] + 1)
        project("z", 2, hT)
        pe.wait_ge(s["conv_act"], 16)
        transposes("xs", lambda j, bank: [(bank[:, P * a:P * (a + 1)],
                                           xT[:, 4 * (j % 2) + a, 3 + P * (j // 2):3 + P * (j // 2 + 1)])
                                          for a in range(4)])
        transposes("btok", lambda j, bank: [(bank[:, P * g:P * (g + 1)], xT[:, 8 + g, 3:3 + P]) for g in range(4)])
        stage_transposed(pe, "btok")
        pe.wait_ge(s["xdt_ready"], 1)
        pe.wait_ge(s["cs_out"], 1)
        proj_evacuated(pe, PROJ["z"] + 1)
        for g in range(4):
            if g >= 2:
                pe.wait_ge(s["state_out"], g - 1)
            mm(B[2 + g % 2][:, 0:256], Btok[:, P * g:P * (g + 1)], xdte[:, 256 * g:256 * (g + 1)],
               start=True, stop=True).then_inc(s["state_ready"], 1)
        pe.wait_ge(s["state_out"], 4)
        for q in range(9):
            if q < 8:
                tt, g = q // 4, q % 4
                if q >= 2:
                    pe.wait_ge(s["seg_out"], q - 1)
                    pe.wait_ge(s["m_ready"], q - 1)
                for r in range(4):
                    mm(B[6 + q % 2][:, r * P:(r + 1) * P],
                       dts[:, 4, tt, 4 * g + r:4 * g + r + 1].broadcast_to([P, P]), tri, start=True, stop=True)
                tok = slice(3 + tt * P, 3 + (tt + 1) * P)
                mm(B[q % 2][:, 0:P], xT[:, 8 + g, tok], xT[:, 12 + g, tok], start=True,
                   stop=True).then_inc(s["seg_ready"], 1)
            if q < 6:
                if q >= 2:
                    pe.wait_ge(s["qkv_act"] if q % 2 == 0 else s["qkv_dve"], q // 2)
                w = landed_tile(TILE["qkv"] + q // 2)
                for c in range(C):
                    ins = mm(B[4 + q % 2][:], hT[:, c, (q % 2) * P:(q % 2 + 1) * P], w[:, c, :],
                             start=c == 0, stop=c == C - 1)
                ins.then_inc(tile_used if q % 2 else s["qkv_ready"], 1)
            if q >= 1:
                r0 = q - 1
                tt, g = r0 // 4, r0 % 4
                bank = B[2 + r0 % 2]
                if r0 >= 2:
                    pe.wait_ge(s["y_out"], r0 - 1)
                if tt == 1:
                    mm(bank[:, 256:512], xT[:, 12 + g, 3 + P:3 + 2 * P], stT[:, 256 * g:256 * (g + 1)],
                       start=True, stop=True)
                pe.wait_ge(s["m_ready"], r0 + 1)
                for r in range(4):
                    h = 4 * g + r
                    ins = mm(bank[:, r * HD:(r + 1) * HD], mt[r0 % 2][:, r * P:(r + 1) * P],
                             pb[:, tt, D + h * HD:D + (h + 1) * HD], start=True, stop=True)
                ins.then_inc(s["y_ready"], 1)
        pe.wait_ge(s["y_out"], 8)
        pe.wait_ge(s["gated_ready"], 1)
        transposes("gated", from_tokens(pb, lambda c: 2 * D + P * c))
        stage_transposed(pe, "gated")
        project("ssdo", 2, OT)
        pe.wait_ge(s["qkv_act"], 3)
        pe.wait_ge(s["qkv_dve"], 3)
        transposes("qk2", from_tokens(pb))
        stage_transposed(pe, "qk2")
        for j in range(2):
            proj_evacuated(pe, PROJ["ssdo"] + j)
        attention("att2")
        gate_spread(4)
        pe.wait_ge(s["ot_out"], 20)
        pe.wait_ge(s["branch_out"], 8)
        n = TILE["atto"]
        pe.wait_ge(landed[n % NSLOT], LANDED[n])
        w = ring[n % NSLOT][:].rearrange("p (c n) -> p c n", n=D)
        for j in range(2):
            m = PROJ["atto"] + j
            for tt in range(TT):
                for c in range(4):
                    ins = mm(B[2 * (m % 2) + tt][:], OT[:, c, tt * P:(tt + 1) * P],
                             w[:, c, 512 * j:512 * (j + 1)], start=c == 0, stop=c == 3)
        ins.then_inc(tile_used, 1)
        pe.wait_ge(s["merged_ready"], 1)
        transposes("merged", from_tokens(pb, lambda c: D + P * c))
        stage_transposed(pe, "merged")
        project("wo", 2, OT)
        gate_spread(5)
        pe.wait_ge(s["gate_rows"], 6)
        pe.wait_ge(s["xn_ready"], 6)
        transposes("h5", from_tokens(xn))
        experts("moe2", "h5")


_NAMES = ("x c norm1_g norm2_g final_g ada_w ada_b ev_w_in ev_w_out ev_lambda ev_subln_g od_w_in od_w_out "
          "od_cmp_pos od_cmp_w1 od_cmp_b1 od_cmp_w2 od_cmp_b2 moe_wg moe_bg moe_we moe_be moe_w_gate moe_w_up "
          "moe_w_down c_2 w_mod_2 b_mod_2 w_in_2 conv_w_2 conv_b_2 dt_bias_2 a_log_2 d_skip_2 ssd_norm_w_2 "
          "forget_b_2 w_ssd_o_2 w_att_o_2 w_o_2 ln1_g_2 ln1_b_2 w_router_group_2 b_router_group_2 "
          "w_router_expert_2 b_router_expert_2 w_gate_2 w_up_2 w_down_2 ln2_g_2 ln2_b_2").split()


def rope_table():
    inv = (np.float32(500000.0) ** (-np.arange(0, 16, 2, dtype=np.float32) / np.float32(16))).astype(np.float32)
    ang = np.arange(T, dtype=np.float32)[:, None] * inv[None, :]
    return np.stack([np.tile(np.cos(ang), (1, 2)), np.tile(np.sin(ang), (1, 2))]).astype(np.float32)


def kernel(**inputs):
    import numpy as _np
    import concourse.bacc as _bacc
    from concourse import mybir as _mybir
    from concourse.bass_utils import run_bass_kernel_spmd as _run

    nc = _bacc.Bacc("TRN2", target_bir_lowering=False, num_devices=1)
    arrays, params = {}, {}
    for name in _NAMES:
        a = _np.ascontiguousarray(inputs[name])
        arrays[f"in_{name}"] = a
        params[name] = nc.dram_tensor(f"in_{name}", a.shape, _mybir.dt.from_np(a.dtype), kind="ExternalInput").ap()
    table = rope_table()
    arrays["rope_table"] = table
    rope = nc.dram_tensor("rope_table", table.shape, _mybir.dt.float32, kind="ExternalInput").ap()
    out = nc.dram_tensor("out_0", (1, T, D), _mybir.dt.float32, kind="ExternalOutput").ap()
    two_blocks(nc, params, rope, out)
    r = _run(nc, [arrays], core_ids=[0])
    return r.results[0]["out_0"]
```
